# Optimizing a Trainium2 kernel written in Bass

```python
import jax, jax.numpy as jnp
from jax import lax
import numpy as np

D_MODEL = 1024
BATCH = 1
SEQ = 512
DEPTH = 1

D_MIX = D_MODEL
D_HGRN = D_MIX // 2
HGRN_HEAD_DIM = 128
HGRN_HEADS = D_HGRN // HGRN_HEAD_DIM
HGRN_CHUNK = 64
D_ATTN = D_MIX - D_HGRN
ATTN_HEAD_DIM = 64
ATTN_HEADS = D_ATTN // ATTN_HEAD_DIM
DILATED_PATTERNS = ((128, 1), (512, 4), (2048, 16))
D_IN_PROJ = 4 * D_HGRN + 3 * D_ATTN
N_EXPERTS = 32
TOP_K = 4
D_EXPERT = D_MODEL
SWIGLU_ALPHA = 1.702
SWIGLU_LIMIT = 7.0
MOE_BLOCK = 128
NORM_EPS = 1e-6

kernel_name = 'hymba_hgrn2_dilated_moe_block'

def _rmsnorm(x, g):
    xf = x.astype(jnp.float32)
    r = lax.rsqrt(jnp.mean(xf * xf, axis=-1, keepdims=True) + NORM_EPS)
    return (xf * r).astype(x.dtype) * g

def _head_rmsnorm(o, g, n_heads):
    B, S, W = o.shape
    of = o.astype(jnp.float32).reshape(B, S, n_heads, W // n_heads)
    of = of * lax.rsqrt(jnp.mean(of * of, axis=-1, keepdims=True) + NORM_EPS)
    return of.reshape(B, S, W).astype(o.dtype) * g

def _hgrn2(q, f_logit, v, lb):
    B, S, H, K = q.shape
    C = HGRN_CHUNK
    NC = S // C
    f = lb + (1.0 - lb) * jax.nn.sigmoid(f_logit)
    log_f = jnp.log(f)
    k = 1.0 - f

    def to_chunks(t):
        return t.reshape(B, NC, C, H, t.shape[-1]).transpose(1, 0, 3, 2, 4)

    causal = jnp.tril(jnp.ones((C, C), dtype=bool))

    def step(state, inp):
        qc, kc, vc, gc = inp
        b = jnp.cumsum(gc, axis=2)
        o_inter = jnp.einsum('bhtk,bhkv->bhtv', qc * jnp.exp(b), state)
        diff = b[:, :, :, None, :] - b[:, :, None, :, :]
        decay = jnp.exp(jnp.where(causal[:, :, None], diff, -jnp.inf))
        scores = jnp.einsum('bhtk,bhsk,bhtsk->bhts', qc, kc, decay)
        o_intra = jnp.einsum('bhts,bhsv->bhtv', scores, vc)
        b_last = b[:, :, -1:, :]
        new_state = (jnp.exp(b_last[:, :, 0, :])[..., None] * state
                     + jnp.einsum('bhsk,bhsv->bhkv', kc * jnp.exp(b_last - b), vc))
        return new_state, o_inter + o_intra

    V = v.shape[-1]
    s0 = jnp.zeros((B, H, K, V), jnp.float32)
    _, o = lax.scan(step, s0, (to_chunks(q), to_chunks(k), to_chunks(v), to_chunks(log_f)))
    return o.transpose(1, 0, 3, 2, 4).reshape(B, S, H * V)

def _dilated_pattern(q, k, v, window, dil):
    B, S, H, Dh = q.shape
    blk = window // dil
    span = dil * blk
    L = -(-S // span) * span
    M = L // dil
    nb = M // blk

    def to_classes(t):
        t = jnp.pad(t, ((0, 0), (0, L - S), (0, 0), (0, 0)))
        return t.reshape(B, M, dil, H, Dh).transpose(0, 2, 1, 3, 4).reshape(B, dil, nb, blk, H, Dh)

    def with_prev(t):
        prev = jnp.pad(t, ((0, 0), (0, 0), (1, 0), (0, 0), (0, 0), (0, 0)))[:, :, :-1]
        return jnp.concatenate([prev, t], axis=3)

    qc = to_classes(q)
    kw = with_prev(to_classes(k))
    vw = with_prev(to_classes(v))
    s = jnp.einsum('brnqhd,brnkhd->brnhqk', qc, kw) * (Dh ** -0.5)
    qi = jnp.arange(blk)[:, None]
    ki = jnp.arange(2 * blk)[None, :]
    dist = qi + blk - ki
    band = (dist >= 0) & (dist <= blk)
    has_prev = (jnp.arange(nb) > 0)[:, None, None] | (ki >= blk)[None]
    mask = band[None] & has_prev
    s = jnp.where(mask[None, None, :, None], s, -jnp.inf)
    m = jnp.max(s, axis=-1, keepdims=True)
    p = jnp.exp(s - m)
    den = jnp.sum(p, axis=-1)
    den_q = jnp.transpose(den, (0, 1, 2, 4, 3))
    o = jnp.einsum('brnhqk,brnkhd->brnqhd', p, vw) / den_q[..., None]
    lse = jnp.transpose(m[..., 0], (0, 1, 2, 4, 3)) + jnp.log(den_q)

    def from_classes(t):
        t = t.reshape((B, dil, M) + t.shape[4:])
        t = jnp.moveaxis(t, 1, 2)
        return t.reshape((B, L) + t.shape[3:])[:, :S]

    return from_classes(o), from_classes(lse)

def _dilated_mixture(q, k, v):
    outs = []
    lses = []
    for window, dil in DILATED_PATTERNS:
        o_p, lse_p = _dilated_pattern(q, k, v, window, dil)
        outs.append(o_p)
        lses.append(lse_p)
    wts = jax.nn.softmax(jnp.stack(lses, axis=0), axis=0)
    return jnp.sum(jnp.stack(outs, axis=0) * wts[..., None], axis=0)

def _clamped_swiglu(u):
    glu = jnp.minimum(u[..., ::2], SWIGLU_LIMIT)
    lin = jnp.clip(u[..., 1::2], -SWIGLU_LIMIT, SWIGLU_LIMIT)
    return glu * jax.nn.sigmoid(SWIGLU_ALPHA * glu) * (lin + 1.0)

def _moe(h, router_w, router_b, w_up, b_up, w_down, b_down):
    N, D = h.shape
    NK = N * TOP_K
    logits = (h @ router_w + router_b).astype(jnp.float32)
    top_vals, top_idx = lax.top_k(logits, TOP_K)
    gates = jax.nn.softmax(top_vals, axis=-1)
    flat_e = top_idx.reshape(-1)
    flat_tok = jnp.arange(NK, dtype=jnp.int32) // TOP_K
    order = jnp.argsort(flat_e)
    sorted_e = flat_e[order]
    sorted_tok = flat_tok[order]
    counts = jnp.bincount(flat_e, length=N_EXPERTS)
    padded = (counts + MOE_BLOCK - 1) // MOE_BLOCK * MOE_BLOCK
    pad_end = jnp.cumsum(padded)
    pad_start = pad_end - padded
    start = jnp.cumsum(counts) - counts
    dest = pad_start[sorted_e] + jnp.arange(NK, dtype=jnp.int32) - start[sorted_e]
    R = NK + N_EXPERTS * MOE_BLOCK
    NB = R // MOE_BLOCK
    xbuf = jnp.zeros((R, D), h.dtype).at[dest].set(h[sorted_tok])
    block_e = jnp.clip(jnp.searchsorted(pad_end, jnp.arange(NB) * MOE_BLOCK, side='right'),
                       0, N_EXPERTS - 1)

    def expert_block(args):
        xb, e = args
        u = xb @ w_up[e] + b_up[e]
        return _clamped_swiglu(u) @ w_down[e] + b_down[e]

    ybuf = lax.map(expert_block, (xbuf.reshape(NB, MOE_BLOCK, D), block_e)).reshape(R, D)
    y = ybuf[dest] * gates.reshape(-1)[order][:, None].astype(ybuf.dtype)
    return jnp.zeros((N, D), h.dtype).at[sorted_tok].add(y)

def setup_inputs(seed: int = 0) -> dict:
    key = jax.random.key(seed)
    ks = jax.random.split(key, 16)
    f32 = jnp.float32
    nrm = lambda k, shape, scale: jax.random.normal(k, shape, f32) * scale
    return {
        'x': jax.random.normal(ks[0], (BATCH, SEQ, D_MODEL), f32),
        'norm1_g': 1.0 + nrm(ks[1], (DEPTH, D_MODEL), 0.02),
        'w_in': nrm(ks[2], (DEPTH, D_MODEL, D_IN_PROJ), D_MODEL ** -0.5),
        'hgrn_lb_logits': nrm(ks[3], (DEPTH + 1, D_HGRN), 0.5),
        'hgrn_norm_g': 1.0 + nrm(ks[4], (DEPTH, D_HGRN), 0.02),
        'attn_norm_g': 1.0 + nrm(ks[5], (DEPTH, D_ATTN), 0.02),
        'w_out': nrm(ks[6], (DEPTH, D_MIX, D_MODEL), D_MIX ** -0.5),
        'norm2_g': 1.0 + nrm(ks[7], (DEPTH, D_MODEL), 0.02),
        'router_w': nrm(ks[8], (DEPTH, D_MODEL, N_EXPERTS), D_MODEL ** -0.5),
        'router_b': nrm(ks[9], (DEPTH, N_EXPERTS), 0.01),
        'w_up': nrm(ks[10], (DEPTH, N_EXPERTS, D_MODEL, 2 * D_EXPERT), D_MODEL ** -0.5),
        'b_up': nrm(ks[11], (DEPTH, N_EXPERTS, 2 * D_EXPERT), 0.01),
        'w_down': nrm(ks[12], (DEPTH, N_EXPERTS, D_EXPERT, D_MODEL), D_EXPERT ** -0.5),
        'b_down': nrm(ks[13], (DEPTH, N_EXPERTS, D_MODEL), 0.01),
        'final_norm_g': 1.0 + nrm(ks[14], (D_MODEL,), 0.02),
    }

def reference(x, norm1_g, w_in, hgrn_lb_logits, hgrn_norm_g, attn_norm_g, w_out, norm2_g,
              router_w, router_b, w_up, b_up, w_down, b_down, final_norm_g):
    B, S, D = x.shape
    f32 = jnp.float32
    lb_all = jnp.cumsum(jax.nn.softmax(hgrn_lb_logits.astype(f32), axis=0), axis=0)
    splits = [D_HGRN, 2 * D_HGRN, 3 * D_HGRN, 4 * D_HGRN, 4 * D_HGRN + D_ATTN, 4 * D_HGRN + 2 * D_ATTN]
    for l in range(DEPTH):
        h = _rmsnorm(x, norm1_g[l])
        proj = h @ w_in[l]
        hq, hf, hi, hg, aq, ak, av = jnp.split(proj, splits, axis=-1)
        lb = lb_all[l].reshape(HGRN_HEADS, HGRN_HEAD_DIM)
        to_h = lambda t: t.astype(f32).reshape(B, S, HGRN_HEADS, HGRN_HEAD_DIM)
        o_a = _hgrn2(to_h(hq), to_h(hf), to_h(hi), lb).astype(x.dtype)
        o_a = _head_rmsnorm(o_a, hgrn_norm_g[l], HGRN_HEADS) * jax.nn.silu(hg)
        to_a = lambda t: t.astype(f32).reshape(B, S, ATTN_HEADS, ATTN_HEAD_DIM)
        o_b = _dilated_mixture(to_a(aq), to_a(ak), to_a(av)).reshape(B, S, D_ATTN).astype(x.dtype)
        o_b = _head_rmsnorm(o_b, attn_norm_g[l], ATTN_HEADS)
        x = x + jnp.concatenate([o_a, o_b], axis=-1) @ w_out[l]
        h2 = _rmsnorm(x, norm2_g[l]).reshape(B * S, D)
        x = x + _moe(h2, router_w[l], router_b[l], w_up[l], b_up[l], w_down[l], b_down[l]).reshape(B, S, D)
    return _rmsnorm(x, final_norm_g)


_drawn_inputs = setup_inputs


def setup_inputs(seed=0):
    import zlib

    import numpy as np

    out = dict(_drawn_inputs(seed))
    spreads = {}
    factors = {'hgrn_norm_g': 3.163, 'b_up': 8.0, 'b_down': 8.0, 'final_norm_g': 2.872}
    for name, (base, spread) in spreads.items():
        noise = np.random.default_rng([zlib.crc32(name.encode()), seed]).standard_normal(out[name].shape)
        drawn = base * np.exp(spread * noise) if base else spread * noise
        out[name] = __import__('jax').numpy.asarray(drawn.astype(out[name].dtype))
    for name, factor in factors.items():
        out[name] = (out[name] * factor).astype(out[name].dtype)
    return out
```

```python
from contextlib import ExitStack

import numpy as np

import concourse.bass as bass
from concourse import mybir

F32 = mybir.dt.float32
F32R = mybir.dt.float32r
I32 = mybir.dt.int32
ALU = mybir.AluOpType
ACT = mybir.ActivationFunctionType
AX = mybir.AxisListType

P = 128
SEQ = 512
TT = SEQ // P
D = 1024
DK = D // P
HALF = D // 2
HH = 4
AH = 8
DH = HALF // AH
CH = 32
NCH = SEQ // CH
NE = 32
TOPK = 4
NF = 2 * D
EPS = 1e-6
ALPHA = 1.702
LIMIT = 7.0
PATTERNS = ((128, 1), (512, 4), (2048, 16))
MAXX = 16
NEG = -1e30

RAW = 6
SPL = 4
UPC = DK
DNC = DK // 2
NC = UPC + DNC


def shape_constants():
    p = np.arange(P)[:, None]
    f = np.arange(P)[None, :]
    cols = {}
    cols["ident"] = (p == f) * 1.0
    cols["ones"] = np.ones((P, P))
    cols["before"] = (p < f) * 1.0
    cols["iota"] = np.broadcast_to(f, (P, P)) * 1.0
    blocks = []
    for delta in range(TT - 1, -1, -1):
        d = P * delta + p - f
        count = np.zeros((P, P))
        for window, dil in PATTERNS:
            count += (d >= 0) & (d % dil == 0) & (d // dil <= window // dil)
        blocks.append(np.where(count > 0, np.log(np.maximum(count, 1)) * DH ** 0.5, NEG))
    cols["pairs"] = np.concatenate(blocks, 1)
    cols["chunk_causal"] = ((p // CH == f // CH) & (p <= f)) * 1.0
    cols["chunk_go"] = np.broadcast_to((np.arange(SEQ) % CH != 0)[None, :], (P, SEQ)) * 1.0
    cols["tile_go"] = np.broadcast_to((np.arange(TT * NE) % NE != 0)[None, :], (P, TT * NE)) * 1.0
    cols["tok"] = P * np.arange(TT)[None, :] + p - SEQ
    cols["dump_row"] = np.concatenate([SEQ + p, 0 * p], 1)
    cols["expert_row"] = (p % NE == np.arange(NE + 2)[None, :]) * 1.0
    cols["item"] = np.broadcast_to(np.arange(MAXX)[None, :], (P, MAXX)) * 1.0
    at, where = 0, {}
    for name, a in cols.items():
        where[name] = (at, at + a.shape[1])
        at += a.shape[1]
    return np.concatenate(list(cols.values()), 1).astype(np.float32), where


def hybrid_moe_block(nc, x, norm1_g, w_in, lb_logits, hgrn_g, attn_g, w_out, norm2_g, router_w,
                     router_b, w_up, b_up, w_down, b_down, final_g, consts, out, where):
    x = x[0]
    w_in, w_out, router_w = w_in[0], w_out[0], router_w[0]
    w_up, b_up, w_down, b_down = w_up[0], b_up[0], w_down[0], b_down[0]
    out = out[0]
    normed_dram = nc.dram_tensor("normed_rows", (SEQ + P, D), F32, kind="Internal").ap()
    acc_dram = nc.dram_tensor("residual_rows", (SEQ + P, D), F32, kind="Internal").ap()

    ctx = ExitStack()
    with ctx:
        sems = {}

        def S(name):
            if name not in sems:
                sems[name] = ctx.enter_context(nc.semaphore(name))
            return sems[name]

        top = [16512]

        def at(name, shape, dt=F32):
            size = int(np.prod(shape[1:])) * 4
            t = nc.alloc_sbuf_tensor_at(name, shape, dt, offset=top[0])
            top[0] += -(-size // 32) * 32
            return t

        CW = max(b for _, b in where.values())
        C = at("shape_consts", [P, CW])

        def cst(name):
            a, b = where[name]
            return C[:, a:b]

        ident, ones = cst("ident"), cst("ones")
        bias_hl = at("bias_hl", [64, NF + D], F32R)
        pos_t = at("pos_t", [P, TT, NE + 2])
        vals_t = at("vals_t", [P, TT, NE + 2, 2])
        slot_t = at("slot_t", [P, NE + 2, 2])
        block_off = at("block_off", [P, MAXX])
        small = at("small", [P, 256])
        shared = top[0]

        X = at("x_rows", [P, TT, D])
        HT = at("h_T", [P, DK, SEQ])
        Wb = at("w_buf", [P, 2, DK, 512])
        fk0 = top[0]
        F = at("f_T", [P, HH, SEQ])
        K = at("k_T", [P, HH, SEQ])
        Q = at("q_T", [P, HH, SEQ])
        G = at("gate_T", [P, HH, SEQ])
        V = at("v_rows", [P, TT, HALF])
        AQ = at("aq_T", [P, 4, SEQ])
        AK = at("ak_T", [P, 4, SEQ])
        AV = at("av_rows", [P, TT, HALF])
        QE = at("q_mid", [P, 2, SEQ])
        KE = at("k_mid", [P, 2, SEQ])
        QB = at("q_start", [P, 2, SEQ])
        KD = at("k_end", [P, 2, SEQ])
        B = at("log_decay", [P, SEQ])
        DD = at("decay_to_mid", [P, SEQ])
        DE = at("decay_to_end", [P, SEQ])
        KDT = at("k_end_rows", [P, 2, TT, P])
        A = at("intra_T", [P, 2, TT, P])
        ST = at("states", [P, NCH, P])
        R = at("o_norm", [P, SEQ])
        RM = at("o_mean", [P, SEQ])
        RN = at("o_newton", [P, SEQ])
        SQ = at("o_sq", [P, SEQ])
        OA = at("attn_rows", [P, TT, HALF])
        rw_sb = at("router_w_sb", [P, DK, NE])
        front_end = top[0]
        top[0] = fk0
        E = at("scores", [P, 2, 1280])
        PTs = at("probs_T", [P, 2, 1280])
        assert top[0] <= fk0 + 3 * 8192
        H2 = nc.alloc_sbuf_tensor_at("h2_rows", [P, TT, D], F32, offset=fk0 + 5 * 8192)
        G2 = nc.alloc_sbuf_tensor_at("g2_rows", [P, D], F32, offset=fk0 + 3 * 8192)
        LG = nc.alloc_sbuf_tensor_at("router_work", [P, 12, TT * NE], F32, offset=fk0 + 4 * 8192)

        XN = nc.alloc_sbuf_tensor_at("x_scaled", [P, TT, D], F32, offset=fk0)
        junk = nc.alloc_sbuf_tensor_at("x_sq", [P, D], F32, offset=fk0 + 3 * 8192)
        osq = nc.alloc_sbuf_tensor_at("attn_sq", [P, TT, DH], F32, offset=fk0 + 8 * 8192)
        top8 = nc.alloc_sbuf_tensor_at("top8", [P, TT, 8], F32, offset=fk0 + 3 * 8192 + 4096)
        rt = nc.alloc_sbuf_tensor_at("router_rows", [P, 2, TT], F32, offset=fk0 + 3 * 8192 + 4096 + 256)
        itf = nc.alloc_sbuf_tensor_at("item_expert", [P, MAXX], F32, offset=fk0 + 3 * 8192 + 4096 + 512)
        items = nc.alloc_sbuf_tensor_at("item_work", [P, 2, MAXX, NE], F32, offset=fk0 + 20480)
        ZR = nc.alloc_sbuf_tensor_at("zero_rows", [P, D], F32, offset=fk0 + 7 * 8192)
        junk2 = nc.alloc_sbuf_tensor_at("x2_sq", [P, D], F32, offset=fk0 + 7 * 8192 + 4096)

        top[0] = shared
        raw = at("w_raw", [P, RAW, NF])
        wh = at("w_high", [P, SPL, NF], F32R)
        wl = at("w_low", [P, SPL, NF], F32R)
        XG = at("gathered", [P, D])
        xh = at("x_high", [P, DK, P], F32R)
        xl = at("x_low", [P, DK, P], F32R)
        GL = at("glu", [P, D])
        LN = at("lin", [P, D])
        SG = at("sig", [P, D])
        ah = at("a_high", [P, DK, P], F32R)
        al = at("a_low", [P, DK, P], F32R)
        Y = at("y_rows", [P, D])
        SEL = at("slot_sel", [P, TT, P])
        BSU = at("bias_sel_up", [64, P], F32R)
        BSD = at("bias_sel_down", [64, P], F32R)
        IDXG = at("gather_rows", [P, 1], I32)
        IDXS = at("scatter_rows", [P, 1], I32)
        moe_end = top[0]
        bias_raw = nc.alloc_sbuf_tensor_at("bias_raw", [64, NF + D], F32, offset=fk0)
        top[0] = max(front_end, moe_end)
        assert top[0] <= nc.sbuf_usable_end, (front_end, moe_end)
        XF = nc.alloc_sbuf_tensor_at("final_rows", [P, TT, D], F32, offset=shared)
        GF = nc.alloc_sbuf_tensor_at("final_g_rows", [P, D], F32, offset=shared + 16384)
        YF = nc.alloc_sbuf_tensor_at("final_out", [P, TT, D], F32, offset=shared + 16384 + 4096)

        PS = ctx.enter_context(nc.psum_tensor("psum", [P, 8, 512], F32))

        vec_T = small[:, 0:24]
        g1c, lbc, hgc, agc = small[:, 0:8], small[:, 8:16], small[:, 16:20], small[:, 20:24]
        ss1, r1 = small[:, 24:28], small[:, 28:32]
        lbe = small[:, 32:40]
        lbm, lbz, lb, oml = small[:, 40:44], small[:, 44:48], small[:, 48:52], small[:, 52:56]
        mx, nmx = small[:, 56:64], small[:, 64:72]
        den, rden = small[:, 72:80], small[:, 80:88]
        ss2, r2 = small[:, 88:92], small[:, 92:96]
        ssa, ra = small[:, 96:128], small[:, 128:160]
        dec = small[:, 160:192]
        rtmp = small[:, 192:224]
        vec_rows = nc.alloc_sbuf_tensor_at("vec_rows", [24, P], F32, offset=top[0])
        rb_row = nc.alloc_sbuf_tensor_at("rb_row", [1, NE], F32, offset=top[0] + 512)
        one_row = nc.alloc_sbuf_tensor_at("one_row", [1, P], F32, offset=top[0] + 640)
        assert top[0] + 1152 <= nc.sbuf_usable_end
        CNT = nc.alloc_sbuf_tensor_at("counts_i", [P, 64], I32, offset=top[0] + 1152)
        assert top[0] + 1152 + 256 <= nc.sbuf_usable_end, (front_end, moe_end, nc.sbuf_usable_end)

        jobs = [("vec",)] + [("hT", k) for k in range(DK)]
        for g in ("f", "g", "q", "v", "aq", "ak", "av"):
            jobs += [(g, j) for j in range(4)]

        def hgrn_head_jobs(h):
            return [("kdT", h), ("sc", h)] + [("kv", h, j) for j in range(4)]

        jobs += hgrn_head_jobs(0)
        for h in range(HH):
            if h + 1 < HH:
                jobs += hgrn_head_jobs(h + 1)
            jobs += [("o", h), ("ss", h)]
        jobs += [("qk", 0, i) for i in range(TT)]
        for h in range(AH):
            if h + 1 < AH:
                jobs += [("qk", h + 1, i) for i in range(TT)]
            jobs += [("pt", h, c) for c in range(3)] + [("pv", h)]
        jobs += [("oT", j) for j in range(4)]
        jobs += [("x2", i, n) for i in range(TT) for n in range(2)]
        jobs += [("h2T", k) for k in range(DK)] + [("lg",), ("pos",)]
        number = {name: n for n, name in enumerate(jobs)}
        uses = [len([n for n in range(len(jobs)) if n % 8 == b]) for b in range(8)]
        bank_full = [S(f"bank_full{b}") for b in range(8)]
        bank_free = [S(f"bank_free{b}") for b in range(8)]

        def bank(*name):
            return PS[:, number[name] % 8, :]

        def full(eng, *name):
            n = number[name]
            eng.wait_ge(bank_full[n % 8], n // 8 + 1)

        def freed(eng, *name):
            n = number[name]
            eng.wait_ge(bank_free[n % 8], n // 8 + 1)

        def free_sem(*name):
            return bank_free[number[name] % 8]

        def full_sem(*name):
            return bank_full[number[name] % 8]

        GROUPS = {"f": 1, "g": 3, "q": 0, "v": 2, "aq": 4, "ak": 5, "av": 6}
        GORDER = ["f", "g", "q", "v", "aq", "ak", "av"]

        KB = {0: 0, 1: 512, 3: 896, 2: 1024}
        EOFF = [128 * i * (i + 1) // 2 for i in range(TT)]

        U = PS[:, 0:4, :]
        Yp = PS[:, 4:6, :]
        T = PS[:, 6:8, :].rearrange("p b (k m) -> p (b k) m", m=P)
        Tflat = PS[:, 6:8, :].rearrange("p b f -> p (b f)")
        Uflat = PS[:, 0:4, :].rearrange("p b (f two) -> p (b f) two", two=2)
        Yflat = PS[:, 4:6, :].rearrange("p b f -> p (b f)")
        raw_landed = [S(f"raw_landed{s}") for s in range(RAW)]
        wh_ready, wl_ready, chunk_used = S("wh_ready"), S("wl_ready"), S("chunk_used")
        t_full, t_free = S("t_full"), S("t_free")
        sel_ready, idxg_ready, idxs_ready = S("sel_ready"), S("idxg_ready"), S("idxs_ready")
        gathered, acc_added, blocks_added = S("gathered"), S("acc_added"), S("blocks_added")
        xh_ready, ah_ready, bsu_ready, bsd_ready = S("xh_ready"), S("ah_ready"), S("bsu_ready"), S("bsd_ready")
        u_free, g_ready, sig_ready, a_ready = S("u_free"), S("g_ready"), S("sig_ready"), S("a_ready")
        y_ready = S("y_ready")

        class Chunks:

            def __init__(self, reg, mul, off):
                self.reg, self.mul, self.off = reg, mul, off

            def count(self, n, extra=0):
                return self.reg * self.mul + (self.off + n + extra)

            def slot(self, n, ring):
                return (self.off + n) % ring

            def turn(self, n, ring):
                return self.reg * (self.mul // ring) + (self.off + n) // ring

            def starts(self, n):
                return self.off + n if self.mul == 0 else NC + n

        CHUNKS = [("up", c) for c in range(UPC)] + [("down", c) for c in range(DNC)]
        FIRST = Chunks(0, 0, 0)
        END = Chunks(0, 0, UPC + NC * (NE - 1))

        def main_chunks(e):
            return Chunks(e, NC, UPC - NC)

        def over_chunks(j):
            return Chunks(j, NC, NC * NE)

        SEL0, X0, SEL1, SEL2, X1 = range(5)

        def use_a(e):
            return e * 3 + 5

        def use_sel(e):
            return e * 3 - 3

        def use_x(e):
            return e * 3 + 1

        OVER = 5 + 3 * (NE - 1) + 1

        block = ctx.enter_context(nc.Block())

        @block.sync
        def _(sp):
            sp.dma_start(C[:, :], consts).then_inc(S("c_in"), 16)
            xv = x.rearrange("(t p) d -> p t d", p=P)
            for i in range(TT):
                sp.dma_start(X[:, i, :], xv[:, i, :]).then_inc(S(f"x_in{i}"), 16)
            sp.dma_start(vec_rows[0:8, :], norm1_g.rearrange("o (k p) -> (o k) p", p=P)).then_inc(S("vec_in"), 16)
            sp.dma_start(vec_rows[8:16, :], lb_logits.rearrange("r (k p) -> (r k) p", p=P)).then_inc(S("vec_in"), 16)
            sp.dma_start(vec_rows[16:20, :], hgrn_g.rearrange("o (k p) -> (o k) p", p=P)).then_inc(S("vec_in"), 16)
            sp.dma_start(vec_rows[20:24, :], attn_g.rearrange("o (k p) -> (o k) p", p=P)).then_inc(S("vec_in"), 16)
            sp.dma_start(rb_row[0:1, :], router_b).then_inc(S("rb_in"), 16)
            for n, g in enumerate(GORDER):
                if n >= 2:
                    full(sp, GORDER[n - 2], 3)
                c = GROUPS[g] * 512
                sp.dma_start(Wb[:, n % 2, :, :], w_in[:, c:c + 512].rearrange("(k p) n -> p k n", p=P)
                             ).then_inc(S(f"w_in{n % 2}"), 16)
                if n == 1:
                    sp.dma_start(rw_sb[:, :, :], router_w.rearrange("(k p) n -> p k n", p=P)).then_inc(S("rw_in"), 16)
            for n in range(7, 9):
                full(sp, GORDER[n - 2], 3)
                c = (n - 7) * 512
                sp.dma_start(Wb[:, n % 2, :, :], w_out[:, c:c + 512].rearrange("(k p) n -> p k n", p=P)
                             ).then_inc(S(f"w_in{n % 2}"), 16)
            sp.wait_ge(S("attn_read"), AH)
            sp.dma_start(bias_raw[0:NE, 0:NF], b_up).then_inc(S("bias_in"), 16)
            sp.dma_start(bias_raw[0:NE, NF:NF + D], b_down).then_inc(S("bias_in"), 16)
            sp.dma_start(bias_raw[NE:2 * NE, 0:NF], b_up).then_inc(S("bias_in"), 16)
            sp.dma_start(bias_raw[NE:2 * NE, NF:NF + D], b_down).then_inc(S("bias_in"), 16)
            sp.dma_start(G2[:, :], norm2_g.to_broadcast([P, D])).then_inc(S("g2_in"), 16)
            accv = acc_dram[0:SEQ, :].rearrange("(t p) d -> p t d", p=P)
            norv = normed_dram[0:SEQ, :].rearrange("(t p) d -> p t d", p=P)
            sp.wait_ge(S("zero_rows"), 1)
            sp.dma_start(acc_dram[SEQ:SEQ + P, :], ZR[:, :]).then_inc(S("rows_out"), 16)
            sp.dma_start(normed_dram[SEQ:SEQ + P, :], ZR[:, :]).then_inc(S("rows_out"), 16)
            for i in range(TT):
                for n in range(2):
                    freed(sp, "x2", i, n)
            sp.dma_start(accv, X[:, :, :]).then_inc(S("rows_out"), 16)
            sp.wait_ge(S("h2_rows"), TT)
            sp.dma_start(norv, H2[:, :, :]).then_inc(S("rows_out"), 16)
            sp.wait_ge(S("front_done"), 1)
            sp.wait_ge(S("rows_out"), 64)

            def step(q, e_up, e_down, chunks):
                for n, (kind, c) in enumerate(CHUNKS):
                    e = e_up if kind == "up" else e_down
                    if e is None:
                        continue
                    m = n if e_up is not None else n - UPC
                    if q.starts(m) >= RAW:
                        sp.wait_ge(wl_ready, q.count(m, 1 - RAW))
                    if kind == "up":
                        src = w_up[bass.ds(e, 1), c * P:(c + 1) * P, :].rearrange("e p n -> p (e n)")
                        dst = raw[:, q.slot(m, RAW), :]
                    else:
                        src = w_down[bass.ds(e, 1), 2 * c * P:2 * (c + 1) * P, :].rearrange("e (t p) n -> p (e t) n", p=P)
                        dst = raw[:, q.slot(m, RAW), :].rearrange("p (t n) -> p t n", t=2)
                    sp.dma_start(dst, src).then_inc(raw_landed[q.slot(m, RAW)], 16)

            step(FIRST, 0, None, CHUNKS)
            with sp.Fori(1, NE) as e:
                step(main_chunks(e), e, e - 1, CHUNKS)
            step(END, None, NE - 1, CHUNKS)
            sp.wait_ge(S("items_ready"), 1)
            nx = sp.value_load(CNT[0:1, 0:1], min_val=0, max_val=MAXX)
            with sp.Fori(0, MAXX) as j:
                with sp.If(nx > j):
                    ex = sp.value_load(CNT[0:1, bass.ds(j + MAXX, 1)], min_val=0, max_val=NE - 1)
                    step(over_chunks(j), ex, ex, CHUNKS)
            sp.wait_ge(blocks_added, nx + (NE + 1))
            sp.dma_start(GF[:, :], final_g.rearrange("(o d) -> o d", o=1).to_broadcast([P, D])).then_inc(S("gf_in"), 16)
            for i in range(TT):
                sp.dma_start(XF[:, i, :], accv[:, i, :]).then_inc(S(f"xf_in{i}"), 16)
            outv = out.rearrange("(t p) d -> p t d", p=P)
            for i in range(TT):
                sp.wait_ge(S("out_ready"), i + 1)
                sp.dma_start(outv[:, i, :], YF[:, i, :]).then_inc(S("stored"), 16)
            sp.wait_ge(S("stored"), 16 * TT)

        @block.gpsimd
        def _(pool):
            pool.memset(one_row[:, :], 1.0).then_inc(S("one_row"), 1)
            pool.wait_ge(S("attn_read"), AH)
            pool.memset(ZR[:, :], 0.0).then_inc(S("zero_rows"), 1)

            def gather(g, x_before):
                pool.wait_ge(idxg_ready, g + 1)
                if x_before is not None:
                    pool.wait_ge(t_full, x_before + 1)
                pool.sem_inc(S("gathers_begun"), 1)
                pool.indirect_dma_start(XG[:, :], None, normed_dram, bass.IndirectOffsetOnAxis(IDXG[:, 0:1], 0)
                                        ).then_inc(gathered, 16)

            def scatter(q):
                pool.wait_ge(y_ready, q + 1)
                pool.wait_ge(idxs_ready, q + 1)
                pool.sem_inc(S("scatters_begun"), 1)
                pool.indirect_dma_start(acc_dram, bass.IndirectOffsetOnAxis(IDXS[:, 0:1], 0), Y[:, :], None,
                                        compute_op=ALU.add).then_inc(acc_added, 16)
                pool.wait_ge(acc_added, (q + 1) * 16)
                pool.sem_inc(blocks_added, 1)

            pool.wait_ge(S("rows_out"), 64)
            pool.sem_inc(blocks_added, 1)
            gather(0, None)
            gather(1, X0)
            gather(2, X1)
            gather(3, use_x(2))
            with pool.Fori(2, NE) as e:
                scatter(e - 2)
                gather(e + 2, use_x(e + 1))
            scatter(NE - 2)
            scatter(NE - 1)
            pool.wait_ge(S("items_ready"), 1)
            nx = pool.value_load(CNT[0:1, 0:1], min_val=0, max_val=MAXX)
            with pool.Fori(0, MAXX) as j:
                with pool.If(nx > j):
                    gather(j + NE + 2, None)
                    scatter(j + NE)

        def rsqrt_guess(act, r, mean):
            act.activation(r, mean, ACT.Ln).then_inc(S("rsqrt_ln"), 1)
            rsqrts[0] += 1
            act.wait_ge(S("rsqrt_ln"), rsqrts[0])
            act.activation(r, r, ACT.Exp, scale=-0.5).then_inc(S("rsqrt_guess"), 1)

        rsqrts = [0]

        def hgrn_exps(act, h):
            b = h % 2
            if h >= 2:
                full(act, "o", h - 2)
            act.wait_ge(S("decays"), 3 * h + 3)
            act.activation(QE[:, b, :], DD[:, :], ACT.Exp).then_inc(S("exps"), 1)
            act.activation(KE[:, b, :], DD[:, :], ACT.Exp, scale=-1.0).then_inc(S("exps"), 1)
            act.activation(KD[:, b, :], DE[:, :], ACT.Exp).then_inc(S("exps"), 1)
            act.activation(QB[:, b, :], B[:, :], ACT.Exp).then_inc(S("exps"), 1)
            act.activation(dec[:, NCH * b:NCH * (b + 1)], B[:, CH - 1::CH], ACT.Exp).then_inc(S("exps"), 1)

        @block.scalar
        def _(act):
            for i in range(TT):
                act.wait_ge(S(f"x_in{i}"), 16)
                if i:
                    act.wait_ge(S("ss1"), i)
                act.activation(junk[:, :], X[:, i, :], ACT.Square, accum_out=ss1[:, i:i + 1]).then_inc(S("ss1"), 1)
            act.wait_ge(S("mean_eps"), 1)
            rsqrt_guess(act, r1, ss1)
            for i in range(TT):
                act.wait_ge(S("r1"), 1)
                act.activation(XN[:, i, :], X[:, i, :], ACT.Copy, scale=r1[:, i:i + 1]).then_inc(S("xn"), 1)
            freed(act, "vec")
            for k in range(1, DK, 2):
                full(act, "hT", k)
                act.activation(HT[:, k, :], bank("hT", k), ACT.Copy, scale=g1c[:, k:k + 1]
                               ).then_inc(free_sem("hT", k), 1)
            act.wait_ge(S("lb_shifted"), 1)
            act.activation(lbe[:, :], lbe[:, :], ACT.Exp).then_inc(S("lb_exp"), 1)
            for h in range(HH):
                full(act, "f", h)
                act.activation(F[:, h, :], bank("f", h), ACT.Sigmoid).then_inc(free_sem("f", h), 1)
            for h in range(HH):
                full(act, "g", h)
                act.activation(G[:, h, :], bank("g", h), ACT.Sigmoid).then_inc(S("g_sig"), 1)
            for h in range(HH):
                full(act, "q", h)
                act.activation(Q[:, h, :], bank("q", h), ACT.Copy).then_inc(free_sem("q", h), 1)
            for h in range(HH):
                act.wait_ge(S("f_ready"), h + 1)
                act.activation(F[:, h, :], F[:, h, :], ACT.Ln).then_inc(S("log_f"), 1)
            for g, buf in (("v", V), ("aq", AQ), ("ak", AK), ("av", AV)):
                for j in range(4):
                    full(act, g, j)
                    act.activation(buf[:, j, :], bank(g, j), ACT.Copy).then_inc(free_sem(g, j), 1)
                    if (g, j) == ("v", 3):
                        hgrn_exps(act, 0)
            def end_rows(h):
                full(act, "kdT", h)
                act.activation(KDT[:, h % 2, :, :], bank("kdT", h).rearrange("p (t m) -> p t m", m=P), ACT.Copy
                               ).then_inc(free_sem("kdT", h), 1)

            end_rows(0)
            for h in range(HH):
                if h + 1 < HH:
                    hgrn_exps(act, h + 1)
                    end_rows(h + 1)
                full(act, "o", h)
                if h:
                    full(act, "ss", h - 1)
                act.activation(SQ[:, :], bank("o", h), ACT.Square).then_inc(S("o_sq"), 1)
                freed(act, "ss", h)
                rsqrt_guess(act, R[:, :], RM[:, :])
            for h in range(AH):
                for i in range(TT):
                    act.wait_ge(S("neg_max"), TT * h + i + 1)
                    s = E[:, h % 2, EOFF[i]:EOFF[i] + P * (i + 1)]
                    act.activation(s, s, ACT.Exp, bias=nmx[:, TT * (h % 2) + i:TT * (h % 2) + i + 1], scale=DH ** -0.5,
                                   accum_out=den[:, TT * (h % 2) + i:TT * (h % 2) + i + 1]).then_inc(S("probs"), 1)
                for c in range(3):
                    if c == 1:
                        continue
                    full(act, "pt", h, c)
                    if h >= 2:
                        full(act, "pv", h - 2)
                    lo, hi = (0, 512) if c == 0 else (1024, 1280)
                    act.activation(PTs[:, h % 2, lo:hi], bank("pt", h, c)[:, 0:hi - lo], ACT.Copy
                                   ).then_inc(free_sem("pt", h, c), 1)
            act.wait_ge(S("mean_eps"), 2)
            rsqrt_guess(act, ra, ssa)
            for j in range(4):
                full(act, "oT", j)
                act.activation(HT[:, 4 + j, :], bank("oT", j), ACT.Copy, scale=agc[:, j:j + 1]
                               ).then_inc(free_sem("oT", j), 1)
            for i in range(TT):
                for n in range(2):
                    freed(act, "x2", i, n)
                if i:
                    act.wait_ge(S("ss2"), i)
                act.activation(junk2[:, :], X[:, i, :], ACT.Square, accum_out=ss2[:, i:i + 1]).then_inc(S("ss2"), 1)
            act.wait_ge(S("mean_eps"), 3)
            rsqrt_guess(act, r2, ss2)
            for k in range(1, DK, 2):
                full(act, "h2T", k)
                act.activation(HT[:, k, :], bank("h2T", k), ACT.Copy).then_inc(free_sem("h2T", k), 1)
            act.wait_ge(S("lg_shifted"), 1)
            act.activation(LG[:, 1, :], LG[:, 1, :], ACT.Exp).then_inc(S("lg_exp"), 1)

            def cast(q, n, m):
                act.wait_ge(raw_landed[q.slot(m, RAW)], (q.turn(m, RAW) + 1) * 16)
                if q.starts(m) >= SPL:
                    act.wait_ge(chunk_used, q.count(m, 1 - SPL))
                act.activation(wh[:, q.slot(m, SPL), :], raw[:, q.slot(m, RAW), :], ACT.Copy).then_inc(wh_ready, 1)

            def x_high(e, use):
                act.wait_ge(t_full, use + 1)
                act.activation(xh[:, :, :].rearrange("p k m -> p (k m)"), Tflat, ACT.Copy).then_inc(xh_ready, 1)

            def a_high(q, use):
                act.wait_ge(t_full, use + 1)
                act.activation(ah[:, :, :].rearrange("p k m -> p (k m)"), Tflat, ACT.Copy).then_inc(ah_ready, 1)

            def sigmoid(q):
                act.wait_ge(g_ready, q + 1)
                act.activation(SG[:, :], GL[:, :], ACT.Sigmoid, scale=ALPHA).then_inc(sig_ready, 1)

            def gated(q, column, down_chunks_end):
                act.wait_ge(chunk_used, down_chunks_end)
                act.wait_ge(blocks_added, q + 1)
                act.activation(Y[:, :], Yflat, ACT.Copy, scale=slot_t[:, bass.ds(column, 1), 1:2].rearrange("p a b -> p (a b)")
                               ).then_inc(y_ready, 1)

            def step(e, q, up, down, y):
                for n in range(NC):
                    if (n < UPC and up) or (n >= UPC and down):
                        cast(q, n, n if up else n - UPC)
                    if n == 0 and y:
                        gated(e - 2, e - 2, q.count(0, 0))
                    if n == 3 and down:
                        a_high(e - 1, use_a(e - 1))
                    if n == 9 and up:
                        sigmoid(e)
                    if n == 10 and up:
                        x_high(e + 1, use_x(e + 1) if down else X1)

            act.wait_ge(S("front_done"), 1)
            x_high(0, X0)
            step(0, FIRST, True, False, False)
            step(1, Chunks(0, 0, UPC), True, True, False)
            with act.Fori(2, NE) as e:
                step(e, main_chunks(e), True, True, True)
            gated(NE - 2, NE - 2, END.count(0))
            a_high(NE - 1, use_a(NE - 1))
            for n in range(UPC, NC):
                cast(END, n, n - UPC)
            gated(NE - 1, NE - 1, END.count(DNC))
            act.wait_ge(S("items_ready"), 1)
            nx = act.value_load(CNT[0:1, 0:1], min_val=0, max_val=MAXX)
            with act.Fori(0, MAXX) as j:
                with act.If(nx > j):
                    q = over_chunks(j)
                    x_high(j, j * 3 + (OVER + 1))
                    for n in range(UPC):
                        cast(q, n, n)
                    sigmoid(j + NE)
                    a_high(j + NE, j * 3 + (OVER + 2))
                    for n in range(UPC, NC):
                        cast(q, n, n)
                    gated(j + NE, 0, q.count(NC))
            for i in range(TT):
                act.wait_ge(S(f"xf_in{i}"), 16)
                act.activation(YF[:, i, :], XF[:, i, :], ACT.Square, accum_out=ss1[:, i:i + 1]).then_inc(S("ssf"), 1)
            act.wait_ge(S("mean_eps"), 4)
            rsqrt_guess(act, r1, ss1)

        @block.vector
        def _(dve):
            link_count = [0]

            def link(ins):
                link_count[0] += 1
                ins.then_inc(S("dve_link"), 1)
                dve.wait_ge(S("dve_link"), link_count[0])

            def mean_eps(dst, src, n):
                dve.tensor_scalar(dst, src, 1.0 / n, EPS, ALU.mult, ALU.add).then_inc(S("mean_eps"), 1)

            guesses = [0]

            def refined(r, mean, tmp):
                guesses[0] += 1
                dve.wait_ge(S("rsqrt_guess"), guesses[0])
                link(dve.tensor_tensor(tmp, r, r, ALU.mult))
                link(dve.scalar_tensor_tensor(tmp, tmp, -0.5, mean, ALU.mult, ALU.mult))
                return dve.scalar_tensor_tensor(r, tmp, 1.5, r, ALU.add, ALU.mult)

            def spread(col, n):
                return col.unsqueeze(2).broadcast_to([P, col.shape[1], n])

            dve.wait_ge(S("ss1"), TT)
            mean_eps(ss1, ss1, D)
            refined(r1, ss1, rtmp[:, 0:TT]).then_inc(S("r1"), 1)
            full(dve, "vec")
            dve.tensor_copy(vec_T, bank("vec")[:, 0:24]).then_inc(free_sem("vec"), 1)
            freed(dve, "vec")
            for k in range(0, DK, 2):
                full(dve, "hT", k)
                dve.tensor_scalar(HT[:, k, :], bank("hT", k), g1c[:, k:k + 1], None, ALU.mult
                                  ).then_inc(free_sem("hT", k), 1)
            link(dve.tensor_tensor(lbm, lbc[:, 0:4], lbc[:, 4:8], ALU.max))
            link(dve.tensor_tensor(lbe[:, 0:4], lbc[:, 0:4], lbm, ALU.subtract))
            dve.tensor_tensor(lbe[:, 4:8], lbc[:, 4:8], lbm, ALU.subtract).then_inc(S("lb_shifted"), 1)
            dve.wait_ge(S("lb_exp"), 1)
            link(dve.tensor_tensor(lbz, lbe[:, 0:4], lbe[:, 4:8], ALU.add))
            link(dve.reciprocal(lbz, lbz))
            link(dve.tensor_tensor(lb, lbe[:, 0:4], lbz, ALU.mult))
            link(dve.tensor_scalar(oml, lb, -1.0, 1.0, ALU.mult, ALU.add))
            for h in range(HH):
                freed(dve, "f", h)
                link(dve.tensor_scalar(F[:, h, :], F[:, h, :], oml[:, h:h + 1], lb[:, h:h + 1], ALU.mult, ALU.add))
                dve.tensor_scalar(K[:, h, :], F[:, h, :], -1.0, 1.0, ALU.mult, ALU.add).then_inc(S("f_ready"), 1)
            for h in range(HH):
                dve.wait_ge(S("g_sig"), h + 1)
                dve.scalar_tensor_tensor(G[:, h, :], G[:, h, :], hgc[:, h:h + 1], bank("g", h), ALU.mult, ALU.mult
                                         ).then_inc(free_sem("g", h), 1)

            def chunked(ap):
                return ap.rearrange("p (c s) -> p c s", s=CH)

            def decays(h):
                if h == 0:
                    dve.wait_ge(S("log_f"), HH)
                else:
                    dve.wait_ge(S("exps"), 5 * h)
                link(dve.tensor_tensor_scan(B[:, :], cst("chunk_go"), F[:, h, :], 0.0, ALU.mult, ALU.add))
                bc = chunked(B[:, :])
                mid = bc[:, :, CH // 2 - 1:CH // 2].broadcast_to([P, NCH, CH])
                end = bc[:, :, CH - 1:CH].broadcast_to([P, NCH, CH])
                dve.tensor_tensor(chunked(DE[:, :]), end, bc, ALU.subtract).then_inc(S("decays"), 1)
                dve.tensor_tensor(chunked(DD[:, :]), bc, mid, ALU.subtract).then_inc(S("decays"), 1)
                dve.wait_ge(S("decays"), 3 * h + 2)
                dve.tensor_scalar(DD[:, :], DD[:, :], 80.0, -80.0, ALU.min, ALU.max).then_inc(S("decays"), 1)

            def scaled(h):
                b = h % 2
                dve.wait_ge(S("exps"), 5 * h + 5)
                if h == 0:
                    freed(dve, "q", 3)
                for buf, by in ((QE, Q), (KE, K), (KD, K), (QB, Q)):
                    dve.tensor_tensor(buf[:, b, :], buf[:, b, :], by[:, h, :], ALU.mult).then_inc(S("qk_scaled"), 1)

            decays(0)
            scaled(0)
            for h in range(HH):
                b = h % 2
                full(dve, "sc", h)
                dve.scalar_tensor_tensor(A[:, b, :, :], bank("sc", h).rearrange("p (t m) -> p t m", m=P), 3e38,
                                         cst("chunk_causal").unsqueeze(1).broadcast_to([P, TT, P]), ALU.min, ALU.mult
                                         ).then_inc(free_sem("sc", h), 1)
                if h + 1 < HH:
                    decays(h + 1)
                    if h >= 1:
                        pass
                    scaled(h + 1)
                for j in range(4):
                    full(dve, "kv", h, j)
                if h:
                    full(dve, "o", h - 1)
                for c in range(1, NCH):
                    kv = bank("kv", h, (c - 1) % 4)[:, (c - 1) // 4 * P:(c - 1) // 4 * P + P]
                    if c == 1:
                        ins = dve.tensor_copy(ST[:, 1, :], kv)
                    else:
                        ins = dve.scalar_tensor_tensor(ST[:, c, :], ST[:, c - 1, :],
                                                       dec[:, NCH * b + c - 1:NCH * b + c], kv, ALU.mult, ALU.add)
                    if c >= NCH - 4:
                        last = {NCH - 4: 3, NCH - 3: 0, NCH - 2: 1, NCH - 1: 2}[c]
                        ins.then_inc(free_sem("kv", h, last), 1)
                        if c < NCH - 1:
                            freed(dve, "kv", h, last)
                    else:
                        link(ins)
                full(dve, "ss", h)
                dve.tensor_scalar(RM[:, :], bank("ss", h), 1.0 / P, EPS, ALU.mult, ALU.add).then_inc(free_sem("ss", h), 1)
                freed(dve, "ss", h)
                link(refined(R[:, :], RM[:, :], RN[:, :]))
                link(dve.tensor_tensor(R[:, :], R[:, :], G[:, h, :], ALU.mult))
                dve.tensor_tensor(HT[:, h, :], bank("o", h), R[:, :], ALU.mult).then_inc(free_sem("o", h), 1)

            def masked_max(h):
                for i in range(TT):
                    full(dve, "qk", h, i)
                    n = TT * (h % 2) + i
                    if h >= 2:
                        full(dve, "pt", h - 2, 2)
                    dve.tensor_tensor_reduce(E[:, h % 2, EOFF[i]:EOFF[i] + P * (i + 1)], bank("qk", h, i)[:, 0:P * (i + 1)],
                                             cst("pairs")[:, (TT - 1 - i) * P:], 1.0, -3e38, ALU.add, ALU.max,
                                             mx[:, n:n + 1]).then_inc(free_sem("qk", h, i), 1)
                    freed(dve, "qk", h, i)
                    dve.tensor_scalar(nmx[:, n:n + 1], mx[:, n:n + 1], -DH ** -0.5, None, ALU.mult
                                      ).then_inc(S("neg_max"), 1)

            masked_max(0)
            for h in range(AH):
                if h + 1 < AH:
                    masked_max(h + 1)
                full(dve, "pt", h, 1)
                if h >= 2:
                    full(dve, "pv", h - 2)
                dve.tensor_copy(PTs[:, h % 2, 512:1024], bank("pt", h, 1)).then_inc(free_sem("pt", h, 1), 1)
                dve.wait_ge(S("probs"), TT * (h + 1))
                b = TT * (h % 2)
                link(dve.reciprocal(rden[:, b:b + TT], den[:, b:b + TT]))
                full(dve, "pv", h)
                dve.tensor_tensor(OA[:, :, h * DH:(h + 1) * DH], bank("pv", h)[:, 0:TT * DH].rearrange("p (t d) -> p t d", d=DH),
                                  spread(rden[:, b:b + TT], DH), ALU.mult).then_inc(free_sem("pv", h), 1)
                freed(dve, "pv", h)
                oh = OA[:, :, h * DH:(h + 1) * DH]
                link(dve.tensor_tensor(osq[:, :, :], oh, oh, ALU.mult))
                link(dve.tensor_reduce(ssa[:, TT * h:TT * (h + 1)], osq[:, :, :], AX.X, ALU.add))
            mean_eps(ssa, ssa, DH)
            link(refined(ra, ssa, rtmp[:, 0:AH * TT]))
            for h in range(AH):
                oh = OA[:, :, h * DH:(h + 1) * DH]
                dve.tensor_tensor(oh, oh, spread(ra[:, TT * h:TT * (h + 1)], DH), ALU.mult).then_inc(S("attn_read"), 1)

            dve.wait_ge(S("bias_in"), 64)
            dve.tensor_copy(bias_hl[:, :], bias_raw[:, :]).then_inc(S("bias_high"), 1)
            dve.wait_ge(S("bias_high"), 1)
            link(dve.tensor_tensor(bias_hl[NE:2 * NE, :], bias_raw[NE:2 * NE, :], bias_hl[NE:2 * NE, :].bitcast(F32), ALU.subtract))

            for i in range(TT):
                for n in range(2):
                    full(dve, "x2", i, n)
                    dve.tensor_tensor(X[:, i, n * 512:(n + 1) * 512], X[:, i, n * 512:(n + 1) * 512], bank("x2", i, n), ALU.add
                                      ).then_inc(free_sem("x2", i, n), 1)
            dve.wait_ge(S("ss2"), TT)
            mean_eps(ss2, ss2, D)
            link(refined(r2, ss2, rtmp[:, 0:TT]))
            dve.wait_ge(S("g2_in"), 16)
            for i in range(TT):
                dve.scalar_tensor_tensor(H2[:, i, :], X[:, i, :], r2[:, i:i + 1], G2[:, :], ALU.mult, ALU.mult
                                         ).then_inc(S("h2_rows"), 1)
            for k in range(0, DK, 2):
                full(dve, "h2T", k)
                dve.tensor_copy(HT[:, k, :], bank("h2T", k)).then_inc(free_sem("h2T", k), 1)

            def lgv(n):
                return LG[:, n, :].rearrange("p (t e) -> p t e", e=NE)

            full(dve, "lg")
            link(dve.tensor_copy(LG[:, 0, :], bank("lg")[:, 0:TT * NE]))
            for i in range(TT):
                ins = dve.max(top8[:, i, :], LG[:, 0, i * NE:(i + 1) * NE])
                link(ins)
            largest = top8[:, :, 0:1].broadcast_to([P, TT, NE])
            fourth = top8[:, :, TOPK - 1:TOPK].broadcast_to([P, TT, NE])
            dve.tensor_tensor(lgv(1), lgv(0), largest, ALU.subtract).then_inc(S("lg_shifted"), 1)
            link(dve.tensor_tensor(lgv(2), lgv(0), fourth, ALU.is_gt))
            link(dve.tensor_tensor(lgv(3), lgv(0), fourth, ALU.is_equal))
            link(dve.tensor_tensor_scan(LG[:, 4, :], cst("tile_go"), LG[:, 3, :], 0.0, ALU.mult, ALU.add))
            link(dve.tensor_reduce(rt[:, 0, :], lgv(2), AX.X, ALU.add))
            link(dve.tensor_scalar(rt[:, 0, :], rt[:, 0, :], -1.0, float(TOPK), ALU.mult, ALU.add))
            link(dve.tensor_tensor(lgv(4), lgv(4), spread(rt[:, 0, :], NE), ALU.is_le))
            link(dve.tensor_tensor(LG[:, 3, :], LG[:, 3, :], LG[:, 4, :], ALU.mult))
            dve.tensor_tensor(LG[:, 2, :], LG[:, 2, :], LG[:, 3, :], ALU.add).then_inc(S("selected"), 1)
            dve.wait_ge(S("selected"), 1)
            dve.wait_ge(S("lg_exp"), 1)
            link(dve.tensor_tensor(LG[:, 1, :], LG[:, 1, :], LG[:, 2, :], ALU.mult))
            link(dve.tensor_reduce(rt[:, 1, :], lgv(1), AX.X, ALU.add))
            link(dve.reciprocal(rt[:, 1, :], rt[:, 1, :]))
            link(dve.memset(pos_t[:, :, :], -1.0))
            link(dve.memset(vals_t[:, :, :, :], 0.0))
            link(dve.tensor_tensor(vals_t[:, :, 0:NE, 1:2].rearrange("p t e o -> p t (e o)"), lgv(1), spread(rt[:, 1, :], NE), ALU.mult))
            full(dve, "pos")
            link(dve.scalar_tensor_tensor(LG[:, 5, :], bank("pos")[:, 0:TT * NE], 1.0, LG[:, 2, :], ALU.add, ALU.mult))
            link(dve.tensor_copy(LG[:, 6, 0:NE], bank("pos")[:, TT * NE:TT * NE + NE]))
            link(dve.tensor_scalar(pos_t[:, :, 0:NE], lgv(5), -1.0, None, ALU.add))
            link(dve.tensor_scalar(lgv(7), pos_t[:, :, 0:NE], float(P), None, ALU.is_ge))
            link(dve.scalar_tensor_tensor(lgv(7), pos_t[:, :, 0:NE], float(2 * P), lgv(7), ALU.is_ge, ALU.add))
            link(dve.scalar_tensor_tensor(lgv(7), pos_t[:, :, 0:NE], float(3 * P), lgv(7), ALU.is_ge, ALU.add))
            link(dve.scalar_tensor_tensor(lgv(7), lgv(7), -float(P), pos_t[:, :, 0:NE], ALU.mult, ALU.add))
            link(dve.tensor_tensor(vals_t[:, :, 0:NE, 0:1].rearrange("p t e o -> p t (e o)"), spread(cst("tok"), NE), lgv(7), ALU.subtract))
            cnt = LG[:, 6, 0:NE]
            ext, base, last = LG[:, 6, NE:2 * NE], LG[:, 6, 2 * NE:3 * NE], LG[:, 6, 3 * NE:4 * NE]
            link(dve.tensor_scalar(ext, cnt, float(P), None, ALU.is_gt))
            link(dve.scalar_tensor_tensor(ext, cnt, float(2 * P), ext, ALU.is_gt, ALU.add))
            link(dve.scalar_tensor_tensor(ext, cnt, float(3 * P), ext, ALU.is_gt, ALU.add))
            link(dve.tensor_tensor_scan(last, ones[:, 0:NE], ext, 0.0, ALU.mult, ALU.add))
            link(dve.tensor_tensor(base, last, ext, ALU.subtract))
            it1, it2 = items[:, 0, :, :], items[:, 1, :, :]
            num = spread(cst("item"), NE)
            link(dve.tensor_tensor(it1, base.unsqueeze(1).broadcast_to([P, MAXX, NE]), num, ALU.is_le))
            link(dve.tensor_tensor(it2, last.unsqueeze(1).broadcast_to([P, MAXX, NE]), num, ALU.is_gt))
            link(dve.tensor_tensor(it1, it1, it2, ALU.mult))
            link(dve.tensor_tensor(it2, num, base.unsqueeze(1).broadcast_to([P, MAXX, NE]), ALU.subtract))
            link(dve.scalar_tensor_tensor(it2, it2, 1.0, it1, ALU.add, ALU.mult))
            link(dve.tensor_reduce(block_off[:, :], it2, AX.X, ALU.add))
            link(dve.tensor_scalar(block_off[:, :], block_off[:, :], -float(P), None, ALU.mult))
            link(dve.tensor_tensor(it2, it1, cst("iota")[:, 0:NE].unsqueeze(1).broadcast_to([P, MAXX, NE]), ALU.mult))
            link(dve.tensor_reduce(itf[:, :], it2, AX.X, ALU.add))
            link(dve.tensor_copy(CNT[:, MAXX:2 * MAXX], itf[:, :]))
            link(dve.tensor_copy(CNT[:, 0:1], last[:, NE - 1:NE]))
            dve.tensor_copy(CNT[:, 1:2], last[:, NE - 1:NE]).then_inc(S("items_ready"), 1)
            dve.wait_ge(S("items_ready"), 1)
            dve.wait_ge(S("rows_out"), 64)
            full(dve, "pos")
            dve.tensor_copy(CNT[:, 2:3], last[:, NE - 1:NE]).then_inc(S("front_done"), 1)

            def make_sel(col, offset=None):
                for i in range(TT):
                    p_col = pos_t[:, i, bass.ds(col, 1)]
                    if offset is None:
                        ins = dve.tensor_scalar(SEL[:, i, :], cst("iota"), p_col, None, ALU.is_equal)
                    else:
                        ins = dve.tensor_scalar(SEL[:, i, :], cst("iota"), p_col, offset, ALU.subtract, ALU.is_equal)
                    ins.then_inc(sel_ready, 1)

            def slot_rows(g, use, col, before=True):
                dve.wait_ge(t_full, use + 1)
                if before:
                    dve.wait_ge(gathered, g * 16)
                dve.tensor_tensor(IDXG[:, 0:1], Tflat[:, 0:1], cst("dump_row")[:, 0:1], ALU.add).then_inc(idxg_ready, 1)
                dve.tensor_tensor(slot_t[:, bass.ds(col, 1), :].rearrange("p a b -> p (a b)"), Tflat[:, 0:2], cst("dump_row"), ALU.add
                                  ).then_inc(t_free, 1)

            def split(q, m):
                dve.wait_ge(wh_ready, q.count(m, 1))
                dve.tensor_tensor(wl[:, q.slot(m, SPL), :], raw[:, q.slot(m, RAW), :],
                                  wh[:, q.slot(m, SPL), :].bitcast(F32), ALU.subtract).then_inc(wl_ready, 1)

            def x_low(g, use):
                dve.wait_ge(xh_ready, g + 1)
                dve.tensor_tensor(xl[:, :, :].rearrange("p k m -> p (k m)"), Tflat,
                                  xh[:, :, :].rearrange("p k m -> p (k m)").bitcast(F32), ALU.subtract).then_inc(t_free, 1)

            def a_low(q):
                dve.wait_ge(ah_ready, q + 1)
                dve.tensor_tensor(al[:, :, :].rearrange("p k m -> p (k m)"), Tflat,
                                  ah[:, :, :].rearrange("p k m -> p (k m)").bitcast(F32), ALU.subtract).then_inc(t_free, 1)

            def bias_row(buf, col, done):
                dve.tensor_scalar(buf[:, :], ones[0:64, :], cst("expert_row")[0:64, bass.ds(col, 1)], None, ALU.mult
                                  ).then_inc(done, 1)

            def scatter_rows(q, col):
                dve.wait_ge(blocks_added, q + 1)
                dve.tensor_copy(IDXS[:, 0:1], slot_t[:, bass.ds(col, 1), 0:1].rearrange("p a b -> p (a b)")).then_inc(idxs_ready, 1)

            def clamp(q, up_chunks_end):
                dve.wait_ge(chunk_used, up_chunks_end)
                dve.tensor_scalar(GL[:, :], Uflat[:, :, 0], LIMIT, None, ALU.min).then_inc(g_ready, 1)
                dve.tensor_scalar(LN[:, :], Uflat[:, :, 1], LIMIT, -LIMIT, ALU.min, ALU.max).then_inc(u_free, 1)

            def swiglu(q):
                dve.wait_ge(sig_ready, q + 1)
                dve.wait_ge(u_free, q + 1)
                dve.scalar_tensor_tensor(LN[:, :], LN[:, :], 1.0, GL[:, :], ALU.add, ALU.mult).then_inc(S("lin_glu"), 1)
                dve.wait_ge(S("lin_glu"), q + 1)
                dve.tensor_tensor(GL[:, :], LN[:, :], SG[:, :], ALU.mult).then_inc(a_ready, 1)

            def step(e, q, up, down, y):
                for n in range(NC):
                    if (n < UPC and up) or (n >= UPC and down):
                        split(q, n if up else n - UPC)
                    if n == 0 and y:
                        scatter_rows(e - 2, e - 2)
                    if n == 2 and up:
                        make_sel(e + 2)
                    if n == 3 and down:
                        a_low(e - 1)
                        bias_row(BSD, e - 1, bsd_ready)
                    if n == 6 and up:
                        slot_rows(e + 2, use_sel(e + 2) if down else SEL2, e + 2)
                    if n == 9 and up:
                        clamp(e, q.count(UPC - 1, 1))
                        bias_row(BSU, e + 1, bsu_ready)
                    if n == 10 and up:
                        x_low(e + 1, None)
                    if n == 11 and up:
                        swiglu(e)

            make_sel(0)
            slot_rows(0, SEL0, 0, before=False)
            bias_row(BSU, 0, bsu_ready)
            make_sel(1)
            x_low(0, X0)
            slot_rows(1, SEL1, 1)
            step(0, FIRST, True, False, False)
            step(1, Chunks(0, 0, UPC), True, True, False)
            with dve.Fori(2, NE) as e:
                step(e, main_chunks(e), True, True, True)
            scatter_rows(NE - 2, NE - 2)
            a_low(NE - 1)
            bias_row(BSD, NE - 1, bsd_ready)
            for n in range(UPC, NC):
                split(END, n - UPC)
            scatter_rows(NE - 1, NE - 1)
            nx = dve.value_load(CNT[0:1, 0:1], min_val=0, max_val=MAXX)
            with dve.Fori(0, MAXX) as j:
                with dve.If(nx > j):
                    ex = dve.value_load(CNT[0:1, bass.ds(j + MAXX, 1)], min_val=0, max_val=NE - 1)
                    q = over_chunks(j)
                    dve.wait_ge(blocks_added, j + NE + 1)
                    make_sel(ex, block_off[:, bass.ds(j, 1)])
                    slot_rows(j + NE + 2, j * 3 + OVER, 0)
                    bias_row(BSU, ex, bsu_ready)
                    bias_row(BSD, ex, bsd_ready)
                    x_low(j + NE + 1, None)
                    for n in range(UPC):
                        split(q, n)
                    clamp(j + NE, q.count(UPC - 1, 1))
                    swiglu(j + NE)
                    a_low(j + NE)
                    for n in range(UPC, NC):
                        split(q, n)
                    scatter_rows(j + NE, 0)
            dve.wait_ge(S("ssf"), TT)
            mean_eps(ss1, ss1, D)
            link(refined(r1, ss1, rtmp[:, 0:TT]))
            dve.wait_ge(S("gf_in"), 16)
            for i in range(TT):
                dve.scalar_tensor_tensor(YF[:, i, :], XF[:, i, :], r1[:, i:i + 1], GF[:, :], ALU.mult, ALU.mult
                                         ).then_inc(S("out_ready"), 1)

        @block.tensor
        def _(pe):
            def begin(*name):
                n = number[name]
                if n >= 8:
                    pe.wait_ge(bank_free[n % 8], n // 8)
                return bank(*name)

            def blocks(*name):
                return begin(*name).rearrange("p (t m) -> p t m", m=P)

            pe.wait_ge(S("c_in"), 16)
            pe.wait_ge(S("vec_in"), 64)
            pe.transpose(begin("vec")[:, 0:24], vec_rows[:, :], ident[0:24, 0:24]).then_inc(full_sem("vec"), 1)
            for k in range(DK):
                o = blocks("hT", k)
                for i in range(TT):
                    pe.wait_ge(S("xn"), i + 1)
                    ins = pe.transpose(o[:, i, :], XN[:, i, k * P:(k + 1) * P], ident)
                ins.then_inc(full_sem("hT", k), 1)
            for k in range(DK):
                freed(pe, "hT", k)
            for n, g in enumerate(GORDER):
                pe.wait_ge(S(f"w_in{n % 2}"), 16 * (n // 2 + 1))
                for j in range(4):
                    o = begin(g, j)
                    for k in range(DK):
                        if g in ("v", "av"):
                            l, r = HT[:, k, j * P:(j + 1) * P], Wb[:, n % 2, k, :]
                        else:
                            l, r = Wb[:, n % 2, k, j * P:(j + 1) * P], HT[:, k, :]
                        ins = pe.matmul(o, l, r, start=(k == 0), stop=(k == DK - 1))
                    ins.then_inc(full_sem(g, j), 1)

            def hgrn_inputs(h):
                b = h % 2
                pe.wait_ge(S("qk_scaled"), 4 * (h + 1))
                o = blocks("kdT", h)
                for i in range(TT):
                    ins = pe.transpose(o[:, i, :], KD[:, b, i * P:(i + 1) * P], ident)
                ins.then_inc(full_sem("kdT", h), 1)
                o = blocks("sc", h)
                for i in range(TT):
                    s = slice(i * P, (i + 1) * P)
                    ins = pe.matmul(o[:, i, :], KE[:, b, s], QE[:, b, s], start=True, stop=True)
                ins.then_inc(full_sem("sc", h), 1)
                freed(pe, "kdT", h)
                if h == 0:
                    for j in range(4):
                        freed(pe, "v", j)
                for j in range(4):
                    o = blocks("kv", h, j)
                    r = slice(j * CH, (j + 1) * CH)
                    for i in range(TT):
                        ins = pe.matmul(o[:, i, :], KDT[r, b, i, :], V[r, i, h * P:(h + 1) * P], start=True, stop=True)
                    ins.then_inc(full_sem("kv", h, j), 1)

            def hgrn_outputs(h):
                b = h % 2
                o = begin("o", h)
                freed(pe, "sc", h)
                freed(pe, "kv", h, 2)
                for i in range(TT):
                    s = slice(i * P, (i + 1) * P)
                    ins = pe.matmul(o[:, s], V[:, i, h * P:(h + 1) * P], A[:, b, i, :], start=(i == 0), stop=False,
                                    skip_group_check=True)
                for c in range(1, NCH):
                    s = slice(c * CH, (c + 1) * CH)
                    ins = pe.matmul(o[:, s], ST[:, c, :], QB[:, b, s], start=False, stop=(c == NCH - 1),
                                    skip_group_check=True)
                ins.then_inc(full_sem("o", h), 1)
                o = begin("ss", h)
                pe.wait_ge(S("o_sq"), h + 1)
                pe.matmul(o, ones, SQ[:, :], start=True, stop=True).then_inc(full_sem("ss", h), 1)

            hgrn_inputs(0)
            for h in range(HH):
                if h + 1 < HH:
                    hgrn_inputs(h + 1)
                hgrn_outputs(h)

            def attn_scores(h):
                if h == 0:
                    for j in range(4):
                        freed(pe, "aq", j)
                        freed(pe, "ak", j)
                        freed(pe, "av", j)
                r = slice(DH * (h % 2), DH * (h % 2) + DH)
                for i in range(TT):
                    ins = pe.matmul(begin("qk", h, i)[:, 0:(i + 1) * P], AQ[r, h // 2, i * P:(i + 1) * P],
                                    AK[r, h // 2, 0:(i + 1) * P], start=True, stop=True)
                    ins.then_inc(full_sem("qk", h, i), 1)

            attn_scores(0)
            for h in range(AH):
                if h + 1 < AH:
                    attn_scores(h + 1)
                pe.wait_ge(S("probs"), TT * (h + 1))
                for c, tiles in enumerate(((0,), (1, 3), (2,))):
                    o = begin("pt", h, c)
                    for kt in tiles:
                        for i in range(kt, TT):
                            a = KB[kt] - KB[tiles[0]] + (i - kt) * P
                            e0 = EOFF[i] + kt * P
                            ins = pe.transpose(o[:, a:a + P], E[:, h % 2, e0:e0 + P], ident)
                    ins.then_inc(full_sem("pt", h, c), 1)
                o = begin("pv", h)
                for c in range(3):
                    freed(pe, "pt", h, c)
                for i in range(TT):
                    for kt in range(i + 1):
                        a = KB[kt] + (i - kt) * P
                        ins = pe.matmul(o[:, i * DH:(i + 1) * DH], PTs[:, h % 2, a:a + P], AV[:, kt, h * DH:(h + 1) * DH],
                                        start=(kt == 0), stop=(kt == i))
                ins.then_inc(full_sem("pv", h), 1)
            pe.wait_ge(S("attn_read"), AH)
            for j in range(4):
                o = blocks("oT", j)
                for i in range(TT):
                    ins = pe.transpose(o[:, i, :], OA[:, i, j * P:(j + 1) * P], ident)
                ins.then_inc(full_sem("oT", j), 1)
            for j in range(4):
                freed(pe, "oT", j)
            for h in range(HH):
                freed(pe, "o", h)
            for n in range(7, 9):
                pe.wait_ge(S(f"w_in{n % 2}"), 16 * (n // 2 + 1))
            for i in range(TT):
                for n in range(2):
                    o = begin("x2", i, n)
                    for k in range(DK):
                        ins = pe.matmul(o, HT[:, k, i * P:(i + 1) * P], Wb[:, (7 + n) % 2, k, :], start=(k == 0), stop=(k == DK - 1))
                    ins.then_inc(full_sem("x2", i, n), 1)
            for k in range(DK):
                o = blocks("h2T", k)
                for i in range(TT):
                    pe.wait_ge(S("h2_rows"), i + 1)
                    ins = pe.transpose(o[:, i, :], H2[:, i, k * P:(k + 1) * P], ident)
                ins.then_inc(full_sem("h2T", k), 1)
            for k in range(DK):
                freed(pe, "h2T", k)
            pe.wait_ge(S("rw_in"), 16)
            pe.wait_ge(S("rb_in"), 16)
            pe.wait_ge(S("one_row"), 1)
            o = begin("lg")
            for i in range(TT):
                s = o[:, i * NE:(i + 1) * NE]
                for k in range(DK):
                    pe.matmul(s, HT[:, k, i * P:(i + 1) * P], rw_sb[:, k, :], start=(k == 0), stop=False)
                ins = pe.matmul(s, one_row[0:1, :], rb_row[0:1, :], start=False, stop=True)
            ins.then_inc(full_sem("lg"), 1)
            pe.wait_ge(S("selected"), 1)
            o = begin("pos")
            for i in range(TT + 1):
                s = o[:, i * NE:(i + 1) * NE]
                for t in range(min(i + 1, TT)):
                    ins = pe.matmul(s, cst("before") if t == i else ones, LG[:, 2, t * NE:(t + 1) * NE],
                                    start=(t == 0), stop=(t == min(i, TT - 1)))
            ins.then_inc(full_sem("pos"), 1)

            def select(g, use, col):
                pe.wait_ge(sel_ready, g * TT + TT)
                pe.wait_ge(t_free, use)
                for i in range(TT):
                    ins = pe.matmul(Tflat[:, 0:2], SEL[:, i, :], vals_t[:, i, bass.ds(col, 1), :].rearrange("p a b -> p (a b)"),
                                    start=(i == 0), stop=(i == TT - 1))
                ins.then_inc(t_full, 1)

            def x_transposed(g, use):
                pe.wait_ge(gathered, (g + 1) * 16)
                pe.wait_ge(t_free, use)
                for k in range(DK):
                    ins = pe.transpose(T[:, k, :], XG[:, k * P:(k + 1) * P], ident)
                ins.then_inc(t_full, 1)

            def a_transposed(q, use):
                pe.wait_ge(a_ready, q + 1)
                pe.wait_ge(t_free, use)
                for k in range(DK):
                    ins = pe.transpose(T[:, k, :], GL[:, k * P:(k + 1) * P], ident)
                ins.then_inc(t_full, 1)

            def products(o, high, low, w_high, w_low, width, last):
                for x_part, w_part in ((low, w_high), (high, w_high), (high, w_low)):
                    for j in range(width // 512):
                        ins = pe.matmul(o[:, j, :], x_part, w_part[:, j * 512:(j + 1) * 512], start=False,
                                        stop=(last and x_part is high and w_part is w_low))
                return ins

            def up(ordinal, q, bias_ordinal, x_use):
                pe.wait_ge(bsu_ready, bias_ordinal + 1)
                pe.wait_ge(t_free, x_use + 1)
                if not isinstance(ordinal, int) or ordinal:
                    pe.wait_ge(u_free, ordinal)
                for j in range(4):
                    pe.matmul(U[:, j, :], BSU[:, :], bias_hl[:, j * 512:(j + 1) * 512], start=True, stop=False)

            def up_chunk(q, m, c, last=False):
                pe.wait_ge(wl_ready, q.count(m, 1))
                s = q.slot(m, SPL)
                return products(U, xh[:, c, :], xl[:, c, :], wh[:, s, :], wl[:, s, :], NF, last)

            def down(ordinal, a_use):
                pe.wait_ge(bsd_ready, ordinal + 1)
                pe.wait_ge(t_free, a_use + 1)
                if not isinstance(ordinal, int) or ordinal:
                    pe.wait_ge(y_ready, ordinal)
                for j in range(2):
                    pe.matmul(Yp[:, j, :], BSD[:, :], bias_hl[:, NF + j * 512:NF + (j + 1) * 512], start=True, stop=False)

            def down_chunk(q, m, c, last=False):
                pe.wait_ge(wl_ready, q.count(m, 1))
                s = q.slot(m, SPL)
                for t in range(2):
                    k = 2 * c + t
                    ins = products(Yp, ah[:, k, :], al[:, k, :], wh[:, s, t * D:(t + 1) * D], wl[:, s, t * D:(t + 1) * D],
                                   D, last and t == 1)
                return ins

            def step(e, q, has_up, has_down):
                if has_up:
                    up(e, q, e, use_x(e) if not isinstance(e, int) or e > 1 else (X0, X1)[e])
                    for c in range(UPC):
                        ins = up_chunk(q, c, c, c == UPC - 1)
                        ins.then_inc(chunk_used, 1)
                        if c == 1 and has_down:
                            a_transposed(e - 1, use_a(e - 1))
                        if c == 4:
                            select(e + 2, use_sel(e + 2) if has_down else SEL2, e + 2)
                else:
                    a_transposed(e - 1, use_a(e - 1))
                if has_down:
                    down(e - 1, use_a(e - 1))
                for c in range(DNC):
                    if has_down:
                        ins = down_chunk(q, (UPC if has_up else 0) + c, c, c == DNC - 1)
                        ins.then_inc(chunk_used, 1)
                    if c == 0 and has_up:
                        x_transposed(e + 1, use_x(e + 1) if has_down else X1)

            select(0, SEL0, 0)
            x_transposed(0, X0)
            select(1, SEL1, 1)
            step(0, FIRST, True, False)
            step(1, Chunks(0, 0, UPC), True, True)
            with pe.Fori(2, NE) as e:
                step(e, main_chunks(e), True, True)
            step(NE, END, False, True)
            pe.wait_ge(S("items_ready"), 1)
            nx = pe.value_load(CNT[0:1, 0:1], min_val=0, max_val=MAXX)
            with pe.Fori(0, MAXX) as j:
                with pe.If(nx > j):
                    ex = pe.value_load(CNT[0:1, bass.ds(j + MAXX, 1)], min_val=0, max_val=NE - 1)
                    q = over_chunks(j)
                    select(j + NE + 2, j * 3 + OVER, ex)
                    x_transposed(j + NE + 2, j * 3 + (OVER + 1))
                    up(j + NE, q, j + NE + 1, j * 3 + (OVER + 1))
                    for c in range(UPC):
                        up_chunk(q, c, c, c == UPC - 1).then_inc(chunk_used, 1)
                    a_transposed(j + NE, j * 3 + (OVER + 2))
                    down(j + NE, j * 3 + (OVER + 2))
                    for c in range(DNC):
                        down_chunk(q, UPC + c, c, c == DNC - 1).then_inc(chunk_used, 1)


def kernel(**inputs):
    import concourse.bacc as bacc
    from concourse.bass_utils import run_bass_kernel_spmd

    nc = bacc.Bacc("TRN2", target_bir_lowering=False, num_devices=1)
    names = ["x", "norm1_g", "w_in", "hgrn_lb_logits", "hgrn_norm_g", "attn_norm_g", "w_out", "norm2_g", "router_w",
             "router_b", "w_up", "b_up", "w_down", "b_down", "final_norm_g"]
    consts, where = shape_constants()
    arrays = {name: np.ascontiguousarray(inputs[name]) for name in names}
    arrays["shape_constants"] = consts
    args = [nc.dram_tensor(name, a.shape, mybir.dt.from_np(a.dtype), kind="ExternalInput").ap() for name, a in arrays.items()]
    out = nc.dram_tensor("out", (1, SEQ, D), F32, kind="ExternalOutput").ap()
    hybrid_moe_block(nc, *args, out, where)
    r = run_bass_kernel_spmd(nc, [arrays], core_ids=[0])
    return r.results[0]["out"]
```

```python
import math
from contextlib import ExitStack

import numpy as np

import concourse.bass as bass
from concourse import mybir

F32 = mybir.dt.float32
F32R = mybir.dt.float32r
I32 = mybir.dt.int32
ALU = mybir.AluOpType
ACT = mybir.ActivationFunctionType
AX = mybir.AxisListType

P = 128
SEQ = 512
TT = SEQ // P
D = 1024
DK = D // P
HALF = D // 2
HH = 4
AH = 8
DH = HALF // AH
CH = 32
NCH = SEQ // CH
NE = 32
TOPK = 4
NF = 2 * D
EPS = 1e-6
ALPHA = 1.702
LIMIT = 7.0
SILU_LIMIT = ALPHA * LIMIT / (1.0 + math.exp(-ALPHA * LIMIT))
PATTERNS = ((128, 1), (512, 4), (2048, 16))
MAXX = 16
NEG = -1e30

RAW = 12
SPL = 3
UPC = DK
DNC = DK // 2
NC = UPC + DNC


def shape_constants():
    p = np.arange(P)[:, None]
    f = np.arange(P)[None, :]
    cols = {}
    cols["ident"] = (p == f) * 1.0
    cols["ones"] = np.ones((P, P))
    cols["before"] = (p < f) * 1.0
    cols["iota"] = np.broadcast_to(f, (P, P)) * 1.0
    blocks = []
    for delta in range(TT - 1, -1, -1):
        d = P * delta + p - f
        count = np.zeros((P, P))
        for window, dil in PATTERNS:
            count += (d >= 0) & (d % dil == 0) & (d // dil <= window // dil)
        blocks.append(np.where(count > 0, np.log(np.maximum(count, 1)) * DH ** 0.5, NEG))
    cols["pairs"] = np.concatenate(blocks, 1)
    cols["chunk_causal"] = ((p // CH == f // CH) & (p <= f)) * 1.0
    cols["chunk_go"] = np.broadcast_to((np.arange(SEQ) % CH != 0)[None, :], (P, SEQ)) * 1.0
    cols["tile_go"] = np.broadcast_to((np.arange(TT * NE) % NE != 0)[None, :], (P, TT * NE)) * 1.0
    cols["tok"] = P * np.arange(TT)[None, :] + p - SEQ
    cols["dump_row"] = np.concatenate([SEQ + p, 0 * p], 1)
    cols["expert_row"] = (p % NE == np.arange(NE + 2)[None, :]) * 1.0
    cols["item"] = np.broadcast_to(np.arange(MAXX)[None, :], (P, MAXX)) * 1.0
    at, where = 0, {}
    for name, a in cols.items():
        where[name] = (at, at + a.shape[1])
        at += a.shape[1]
    return np.concatenate(list(cols.values()), 1).astype(np.float32), where


def hybrid_moe_block(nc, x, norm1_g, w_in, lb_logits, hgrn_g, attn_g, w_out, norm2_g, router_w,
                     router_b, w_up, b_up, w_down, b_down, final_g, consts, out, where):
    x = x[0]
    w_in, w_out, router_w = w_in[0], w_out[0], router_w[0]
    w_up, b_up, w_down, b_down = w_up[0], b_up[0], w_down[0], b_down[0]
    out = out[0]
    normed_dram = nc.dram_tensor("normed_rows", (SEQ + P, D), F32, kind="Internal").ap()
    acc_dram = nc.dram_tensor("residual_rows", (SEQ + P, D), F32, kind="Internal").ap()

    ctx = ExitStack()
    with ctx:
        sems = {}

        def S(name):
            if name not in sems:
                sems[name] = ctx.enter_context(nc.semaphore(name))
            return sems[name]

        top = [16512]

        def at(name, shape, dt=F32):
            size = int(np.prod(shape[1:])) * 4
            t = nc.alloc_sbuf_tensor_at(name, shape, dt, offset=top[0])
            top[0] += -(-size // 32) * 32
            return t

        CW = max(b for _, b in where.values())
        C = at("shape_consts", [P, CW])

        def cst(name):
            a, b = where[name]
            return C[:, a:b]

        ident, ones = cst("ident"), cst("ones")
        bias_hl = at("bias_hl", [64, NF + D], F32R)
        pos_t = at("pos_t", [P, TT, NE + 2])
        vals_t = at("vals_t", [P, TT, NE + 2, 2])
        slot_t = at("slot_t", [P, NE + 2, 2])
        block_off = at("block_off", [P, MAXX])
        small = at("small", [P, 288])
        CNT = at("counts_i", [P, 2 * MAXX + 8], I32)
        rb_row = at("rb_row", [1, NE])
        shared = top[0]

        def over(name, shape, offset, dt=F32):
            return nc.alloc_sbuf_tensor_at(name, shape, dt, offset=offset)

        X = at("x_rows", [P, TT, D])
        HT = at("h_T", [P, DK, SEQ])
        wb0 = top[0]
        Wb = at("w_buf", [P, 2, DK, 512])
        fk0 = top[0]
        F = at("f_T", [P, HH, SEQ])
        K = at("k_T", [P, HH, SEQ])
        Q = at("q_T", [P, HH, SEQ])
        g0 = top[0]
        G = at("gate_T", [P, HH, SEQ])
        v0 = top[0]
        V = at("v_rows", [P, TT, HALF])
        AQ = at("aq_T", [P, 4, SEQ])
        AK = at("ak_T", [P, 4, SEQ])
        AV = at("av_rows", [P, TT, HALF])
        oa0 = top[0]
        OA = at("attn_rows", [P, TT, HALF])
        rw_sb = at("router_w_sb", [P, DK, NE])
        hg0 = top[0]
        QE = at("q_mid", [P, 2, SEQ])
        KE = at("k_mid", [P, 2, SEQ])
        QB = at("q_start", [P, 2, SEQ])
        KD = at("k_end", [P, 2, SEQ])
        B = at("log_decay", [P, SEQ])
        DD = at("decay_to_mid", [P, SEQ])
        DE = at("decay_to_end", [P, SEQ])
        KDT = at("k_end_rows", [P, 2, TT, P])
        A = at("intra_T", [P, 2, TT, P])
        ST = at("states", [P, NCH, P])
        R = at("o_norm", [P, SEQ])
        RM = at("o_mean", [P, SEQ])
        RN = at("o_newton", [P, SEQ])
        SQ = at("o_sq", [P, SEQ])
        vec_rows = at("vec_rows", [24, P])
        XN = over("x_scaled", [P, TT, D], fk0)
        junk = over("x_sq", [P, D], g0)
        ZR = over("zero_rows", [P, D], hg0)
        E = over("scores", [P, 2, 1280], fk0)
        PTs = over("probs_T", [P, 2, 1280], fk0 + 10240)
        osq = over("attn_sq", [P, TT, DH], fk0 + 20480)
        assert fk0 + 20480 + 1024 <= g0
        H2 = over("h2_rows", [P, TT, D], v0)
        G2 = over("g2_rows", [P, D], v0 + 16384)
        bias_raw = over("bias_raw", [64, NF + D], v0 + 20480)
        LG = over("router_work", [P, 8, TT * NE], oa0)
        items = over("item_work", [P, 2, MAXX, NE], oa0 + 4096)
        assert v0 + 20480 + 12288 <= oa0 and oa0 + 8192 <= hg0

        top[0] = hg0
        raw = [at(f"w_raw{n}", [P, NF]) for n in range(6)]
        end = max(top[0], hg0 + 46 * 1024 + 512)
        assert end <= nc.sbuf_usable_end, (end, nc.sbuf_usable_end)
        raw += [over(f"w_raw{n}", [P, NF], fk0 + (n - 6) * 8192) for n in range(6, 9)]
        raw += [over(f"w_raw{n}", [P, NF], fk0 + (n - RAW) * 8192) for n in range(9, RAW)]
        assert fk0 + 3 * 8192 <= g0
        wh = over("w_high", [P, SPL, NF], g0, F32R)
        wl = over("w_low", [P, SPL, NF], g0 + SPL * 8192, F32R)
        assert g0 + 2 * SPL * 8192 <= hg0
        top[0] = shared
        XG = at("gathered", [P, D])
        xh = at("x_high", [P, DK, P], F32R)
        xl = at("x_low", [P, DK, P], F32R)
        GL = at("glu", [P, D])
        LN = at("lin", [P, D])
        SG = at("sig", [P, D])
        ah = at("a_high", [P, DK, P], F32R)
        al = at("a_low", [P, DK, P], F32R)
        Y = at("y_rows", [P, D])
        SEL = at("slot_sel", [P, TT, P])
        BSU = at("bias_sel_up", [64, P], F32R)
        BSD = at("bias_sel_down", [64, P], F32R)
        IDXG = at("gather_rows", [P, 1], I32)
        IDXS = at("scatter_rows", [P, 1], I32)
        assert top[0] <= fk0 - 3 * 8192
        XF = over("final_rows", [P, TT, D], shared)
        GF = over("final_g_rows", [P, D], shared + 16384)
        YF = over("final_out", [P, TT, D], shared + 16384 + 4096)

        PS = ctx.enter_context(nc.psum_tensor("psum", [P, 8, 512], F32))

        vec_T = small[:, 0:24]
        g1c, lbc, hgc, agc = small[:, 0:8], small[:, 8:16], small[:, 16:20], small[:, 20:24]
        ss1, r1 = small[:, 24:28], small[:, 28:32]
        lbe = small[:, 32:40]
        lbm, lbz, lb, oml = small[:, 40:44], small[:, 44:48], small[:, 48:52], small[:, 52:56]
        mx, nmx = small[:, 56:64], small[:, 64:72]
        den, rden = small[:, 72:80], small[:, 80:88]
        ss2, r2 = small[:, 88:92], small[:, 92:96]
        ssa, ra = small[:, 96:128], small[:, 128:160]
        dec = small[:, 160:192]
        rtmp = small[:, 192:224]
        top8 = small[:, 224:256].rearrange("p (t n) -> p t n", n=8)
        rt = small[:, 256:264].rearrange("p (a t) -> p a t", t=TT)
        itf = small[:, 264:280]

        jobs = [("vec",)] + [("hT", k) for k in range(DK)]
        for g in ("f", "q", "v"):
            jobs += [(g, j) for j in range(4)]
        BETWEEN = ("g", "aq", "ak", "av")
        for h in range(HH):
            g = BETWEEN[h]
            jobs += [("kdT", h), ("sc", h), (g, 0)] + [("kv", h, j) for j in range(4)]
            jobs += [(g, 1), ("o", h), (g, 2), ("ss", h), (g, 3)]
        jobs += [("qk", 0, i) for i in range(TT)]
        for h in range(AH):
            if h + 1 < AH:
                jobs += [("qk", h + 1, i) for i in range(TT)]
            jobs += [("pt", h, c) for c in range(3)] + [("pv", h)]
        jobs += [("oT", j) for j in range(4)]
        jobs += [("x2", i, n) for i in range(TT) for n in range(2)]
        jobs += [("h2T", k) for k in range(DK)] + [("lg",), ("pos",)]
        number = {name: n for n, name in enumerate(jobs)}
        uses = [len([n for n in range(len(jobs)) if n % 8 == b]) for b in range(8)]
        bank_full = [S(f"bank_full{b}") for b in range(8)]
        bank_free = [S(f"bank_free{b}") for b in range(8)]

        def bank(*name):
            return PS[:, number[name] % 8, :]

        def full(eng, *name):
            n = number[name]
            eng.wait_ge(bank_full[n % 8], n // 8 + 1)

        def freed(eng, *name):
            n = number[name]
            eng.wait_ge(bank_free[n % 8], n // 8 + 1)

        def free_sem(*name):
            return bank_free[number[name] % 8]

        def full_sem(*name):
            return bank_full[number[name] % 8]

        GROUPS = {"f": 1, "g": 3, "q": 0, "v": 2, "aq": 4, "ak": 5, "av": 6}
        GORDER = ["f", "q", "v", "g", "aq", "ak", "av"]

        KB = {0: 0, 1: 512, 3: 896, 2: 1024}
        EOFF = [128 * i * (i + 1) // 2 for i in range(TT)]

        U = PS[:, 0:4, :]
        Yp = PS[:, 4:6, :]
        T = PS[:, 6:8, :].rearrange("p b (k m) -> p (b k) m", m=P)
        Tflat = PS[:, 6:8, :].rearrange("p b f -> p (b f)")
        Uflat = PS[:, 0:4, :].rearrange("p b (f two) -> p (b f) two", two=2)
        Yflat = PS[:, 4:6, :].rearrange("p b f -> p (b f)")
        raw_landed = [S(f"raw_landed{s}") for s in range(RAW)]
        wh_ready, wl_ready, chunk_used = S("wh_ready"), S("wl_ready"), S("chunk_used")
        t_full, t_free = S("t_full"), S("t_free")
        sel_ready, idxg_ready, idxs_ready = S("sel_ready"), S("idxg_ready"), S("idxs_ready")
        gathered, acc_added, blocks_added = S("gathered"), S("acc_added"), S("blocks_added")
        xh_ready, ah_ready, bsu_ready, bsd_ready = S("xh_ready"), S("ah_ready"), S("bsu_ready"), S("bsd_ready")
        u_free, lin_ready, lin_clipped, a_ready = S("u_free"), S("lin_ready"), S("lin_clipped"), S("a_ready")
        y_ready = S("y_ready")

        class Chunks:

            def __init__(self, reg, mul, off):
                self.reg, self.mul, self.off = reg, mul, off

            def count(self, n, extra=0):
                return self.reg * self.mul + (self.off + n + extra)

            def slot(self, n, ring):
                return (self.off + n) % ring

            def turn(self, n, ring):
                return self.reg * (self.mul // ring) + (self.off + n) // ring

            def starts(self, n):
                return self.off + n if self.mul == 0 else NC + n

        CHUNKS = [("up", c) for c in range(UPC)] + [("down", c) for c in range(DNC)]
        FIRST = Chunks(0, 0, 0)
        END = Chunks(0, 0, UPC + NC * (NE - 1))

        def main_chunks(e):
            return Chunks(e, NC, UPC - NC)

        def over_chunks(j):
            return Chunks(j, NC, NC * NE)

        SEL0, X0, SEL1, SEL2, X1 = range(5)

        def use_a(e):
            return e * 3 + 5

        def use_sel(e):
            return e * 3 - 3

        def use_x(e):
            return e * 3 + 1

        OVER = 5 + 3 * (NE - 1) + 1

        block = ctx.enter_context(nc.Block())

        @block.sync
        def _(sp):
            sp.dma_start(C[:, :], consts).then_inc(S("c_in"), 16)
            xv = x.rearrange("(t p) d -> p t d", p=P)
            for i in range(TT):
                sp.dma_start(X[:, i, :], xv[:, i, :]).then_inc(S(f"x_in{i}"), 16)
            sp.dma_start(vec_rows[0:8, :], norm1_g.rearrange("o (k p) -> (o k) p", p=P)).then_inc(S("vec_in"), 16)
            sp.dma_start(vec_rows[8:16, :], lb_logits.rearrange("r (k p) -> (r k) p", p=P)).then_inc(S("vec_in"), 16)
            sp.dma_start(vec_rows[16:20, :], hgrn_g.rearrange("o (k p) -> (o k) p", p=P)).then_inc(S("vec_in"), 16)
            sp.dma_start(vec_rows[20:24, :], attn_g.rearrange("o (k p) -> (o k) p", p=P)).then_inc(S("vec_in"), 16)
            sp.dma_start(rb_row[0:1, :], router_b).then_inc(S("rb_in"), 16)
            sp.wait_ge(S("zero_rows"), 1)
            sp.dma_start(acc_dram[SEQ:SEQ + P, :], ZR[:, :]).then_inc(S("zeros_out"), 16)
            sp.dma_start(normed_dram[SEQ:SEQ + P, :], ZR[:, :]).then_inc(S("zeros_out"), 16)
            for n, g in enumerate(GORDER):
                if n >= 2:
                    full(sp, GORDER[n - 2], 3)
                c = GROUPS[g] * 512
                sp.dma_start(Wb[:, n % 2, :, :], w_in[:, c:c + 512].rearrange("(k p) n -> p k n", p=P)
                             ).then_inc(S(f"w_in{n % 2}"), 16)
                if n == 1:
                    sp.dma_start(rw_sb[:, :, :], router_w.rearrange("(k p) n -> p k n", p=P)).then_inc(S("rw_in"), 16)
            for n in range(7, 9):
                full(sp, GORDER[n - 2], 3)
                c = (n - 7) * 512
                sp.dma_start(Wb[:, n % 2, :, :], w_out[:, c:c + 512].rearrange("(k p) n -> p k n", p=P)
                             ).then_inc(S(f"w_in{n % 2}"), 16)

            def load(q, n, m, e):
                kind, c = CHUNKS[n]
                if q.starts(m) >= RAW:
                    sp.wait_ge(wl_ready, q.count(m, 1 - RAW))
                if kind == "up":
                    src = w_up[bass.ds(e, 1), c * P:(c + 1) * P, :].rearrange("e p n -> p (e n)")
                    dst = raw[q.slot(m, RAW)][:, :]
                else:
                    src = w_down[bass.ds(e, 1), 2 * c * P:2 * (c + 1) * P, :].rearrange("e (t p) n -> p (e t) n", p=P)
                    dst = raw[q.slot(m, RAW)][:, :].rearrange("p (t n) -> p t n", t=2)
                sp.dma_start(dst, src).then_inc(raw_landed[q.slot(m, RAW)], 16)

            def step(q, e_up, e_down, first=0):
                for n in range(first, NC):
                    e = e_up if n < UPC else e_down
                    if e is not None:
                        load(q, n, n if e_up is not None else n - UPC, e)

            SECOND = Chunks(0, 0, UPC)
            freed(sp, "o", HH - 1)
            for n in range(6):
                load(FIRST, n, n, 0)
            sp.wait_ge(S("attn_read"), AH)
            sp.dma_start(G2[:, :], norm2_g.to_broadcast([P, D])).then_inc(S("g2_in"), 16)
            sp.dma_start(bias_raw[0:NE, 0:NF], b_up).then_inc(S("bias_in"), 16)
            sp.dma_start(bias_raw[0:NE, NF:NF + D], b_down).then_inc(S("bias_in"), 16)
            sp.dma_start(bias_raw[NE:2 * NE, 0:NF], b_up).then_inc(S("bias_in"), 16)
            sp.dma_start(bias_raw[NE:2 * NE, NF:NF + D], b_down).then_inc(S("bias_in"), 16)
            load(FIRST, 6, 6, 0)
            load(FIRST, 7, 7, 0)
            load(SECOND, 0, 0, 1)
            accv = acc_dram[0:SEQ, :].rearrange("(t p) d -> p t d", p=P)
            norv = normed_dram[0:SEQ, :].rearrange("(t p) d -> p t d", p=P)
            for i in range(TT):
                for n in range(2):
                    freed(sp, "x2", i, n)
            sp.dma_start(accv, X[:, :, :]).then_inc(S("rows_out"), 16)
            sp.wait_ge(S("h2_rows"), TT)
            sp.dma_start(norv, H2[:, :, :]).then_inc(S("rows_out"), 16)
            for n in range(1, 4):
                load(SECOND, n, n, 1)
            step(SECOND, 1, 0, first=4)
            with sp.Fori(2, NE) as e:
                step(main_chunks(e), e, e - 1)
            step(END, None, NE - 1)
            sp.wait_ge(S("items_ready"), 1)
            nx = sp.value_load(CNT[0:1, 0:1], min_val=0, max_val=MAXX)
            with sp.Fori(0, MAXX) as j:
                with sp.If(nx > j):
                    ex = sp.value_load(CNT[0:1, bass.ds(j + MAXX, 1)], min_val=0, max_val=NE - 1)
                    step(over_chunks(j), ex, ex)
            sp.wait_ge(blocks_added, nx + (NE + 1))
            sp.dma_start(GF[:, :], final_g.rearrange("(o d) -> o d", o=1).to_broadcast([P, D])).then_inc(S("gf_in"), 16)
            for i in range(TT):
                sp.dma_start(XF[:, i, :], accv[:, i, :]).then_inc(S(f"xf_in{i}"), 16)
            outv = out.rearrange("(t p) d -> p t d", p=P)
            for i in range(TT):
                sp.wait_ge(S("out_ready"), i + 1)
                sp.dma_start(outv[:, i, :], YF[:, i, :]).then_inc(S("stored"), 16)
            sp.wait_ge(S("stored"), 16 * TT)

        @block.gpsimd
        def _(pool):
            pool.memset(ZR[:, :], 0.0).then_inc(S("zero_rows"), 1)

            def gather(g, x_before):
                pool.wait_ge(idxg_ready, g + 1)
                if x_before is not None:
                    pool.wait_ge(t_full, x_before + 1)
                pool.sem_inc(S("gathers_begun"), 1)
                pool.indirect_dma_start(XG[:, :], None, normed_dram, bass.IndirectOffsetOnAxis(IDXG[:, 0:1], 0)
                                        ).then_inc(gathered, 16)

            def scatter(q):
                pool.wait_ge(y_ready, q + 1)
                pool.wait_ge(idxs_ready, q + 1)
                pool.sem_inc(S("scatters_begun"), 1)
                pool.indirect_dma_start(acc_dram, bass.IndirectOffsetOnAxis(IDXS[:, 0:1], 0), Y[:, :], None,
                                        compute_op=ALU.add).then_inc(acc_added, 16)
                pool.wait_ge(acc_added, (q + 1) * 16)
                pool.sem_inc(blocks_added, 1)

            pool.wait_ge(S("zeros_out"), 32)
            pool.wait_ge(S("rows_out"), 32)
            pool.sem_inc(blocks_added, 1)
            gather(0, None)
            gather(1, X0)
            gather(2, X1)
            gather(3, use_x(2))
            with pool.Fori(2, NE) as e:
                scatter(e - 2)
                gather(e + 2, use_x(e + 1))
            scatter(NE - 2)
            scatter(NE - 1)
            pool.wait_ge(S("items_ready"), 1)
            nx = pool.value_load(CNT[0:1, 0:1], min_val=0, max_val=MAXX)
            with pool.Fori(0, MAXX) as j:
                with pool.If(nx > j):
                    gather(j + NE + 2, None)
                    scatter(j + NE)

        def rsqrt_guess(act, r, mean):
            act.activation(r, mean, ACT.Ln).then_inc(S("rsqrt_ln"), 1)
            rsqrts[0] += 1
            act.wait_ge(S("rsqrt_ln"), rsqrts[0])
            act.activation(r, r, ACT.Exp, scale=-0.5).then_inc(S("rsqrt_guess"), 1)

        rsqrts = [0]

        def hgrn_exps(act, h):
            b = h % 2
            if h >= 2:
                full(act, "o", h - 2)
            if h == 0:
                act.wait_ge(S("zeros_out"), 32)
            act.wait_ge(S("decays"), 3 * h + 3)
            act.activation(QE[:, b, :], DD[:, :], ACT.Exp).then_inc(S("exps"), 1)
            act.activation(KE[:, b, :], DD[:, :], ACT.Exp, scale=-1.0).then_inc(S("exps"), 1)
            act.activation(KD[:, b, :], DE[:, :], ACT.Exp).then_inc(S("exps"), 1)
            act.activation(QB[:, b, :], B[:, :], ACT.Exp).then_inc(S("exps"), 1)
            act.activation(dec[:, NCH * b:NCH * (b + 1)], B[:, CH - 1::CH], ACT.Exp).then_inc(S("exps"), 1)

        @block.scalar
        def _(act):
            for i in range(TT):
                act.wait_ge(S(f"x_in{i}"), 16)
                if i:
                    act.wait_ge(S("ss1"), i)
                act.activation(junk[:, :], X[:, i, :], ACT.Square, accum_out=ss1[:, i:i + 1]).then_inc(S("ss1"), 1)
            act.wait_ge(S("mean_eps"), 1)
            rsqrt_guess(act, r1, ss1)
            for i in range(TT):
                act.wait_ge(S("r1"), 1)
                act.activation(XN[:, i, :], X[:, i, :], ACT.Copy, scale=r1[:, i:i + 1]).then_inc(S("xn"), 1)
            freed(act, "vec")
            for k in range(1, DK, 2):
                full(act, "hT", k)
                act.activation(HT[:, k, :], bank("hT", k), ACT.Copy, scale=g1c[:, k:k + 1]
                               ).then_inc(free_sem("hT", k), 1)
            act.wait_ge(S("lb_shifted"), 1)
            act.activation(lbe[:, :], lbe[:, :], ACT.Exp).then_inc(S("lb_exp"), 1)
            for h in range(HH):
                full(act, "f", h)
                act.activation(F[:, h, :], bank("f", h), ACT.Sigmoid).then_inc(free_sem("f", h), 1)
            for h in range(HH):
                full(act, "q", h)
                act.activation(Q[:, h, :], bank("q", h), ACT.Copy).then_inc(free_sem("q", h), 1)
            for h in range(HH):
                act.wait_ge(S("f_ready"), h + 1)
                act.activation(F[:, h, :], F[:, h, :], ACT.Ln).then_inc(S("log_f"), 1)
            hgrn_exps(act, 0)
            for j in range(4):
                full(act, "v", j)
                act.activation(V[:, j, :], bank("v", j), ACT.Copy).then_inc(free_sem("v", j), 1)

            def projected(h, j):
                g = BETWEEN[h]
                full(act, g, j)
                if g == "g":
                    act.activation(G[:, j, :], bank(g, j), ACT.Sigmoid).then_inc(S("g_sig"), 1)
                else:
                    buf = {"aq": AQ, "ak": AK, "av": AV}[g]
                    act.activation(buf[:, j, :], bank(g, j), ACT.Copy).then_inc(free_sem(g, j), 1)

            def end_rows(h):
                full(act, "kdT", h)
                act.activation(KDT[:, h % 2, :, :], bank("kdT", h).rearrange("p (t m) -> p t m", m=P), ACT.Copy
                               ).then_inc(free_sem("kdT", h), 1)

            for h in range(HH):
                end_rows(h)
                projected(h, 0)
                if h + 1 < HH:
                    hgrn_exps(act, h + 1)
                projected(h, 1)
                full(act, "o", h)
                if h:
                    full(act, "ss", h - 1)
                act.activation(SQ[:, :], bank("o", h), ACT.Square).then_inc(S("o_sq"), 1)
                projected(h, 2)
                freed(act, "ss", h)
                rsqrt_guess(act, R[:, :], RM[:, :])
                projected(h, 3)
            for h in range(AH):
                for i in range(TT):
                    act.wait_ge(S("neg_max"), TT * h + i + 1)
                    s = E[:, h % 2, EOFF[i]:EOFF[i] + P * (i + 1)]
                    act.activation(s, s, ACT.Exp, bias=nmx[:, TT * (h % 2) + i:TT * (h % 2) + i + 1], scale=DH ** -0.5,
                                   accum_out=den[:, TT * (h % 2) + i:TT * (h % 2) + i + 1]).then_inc(S("probs"), 1)
                for c in range(3):
                    if c == 1:
                        continue
                    full(act, "pt", h, c)
                    if h >= 2:
                        full(act, "pv", h - 2)
                    lo, hi = (0, 512) if c == 0 else (1024, 1280)
                    act.activation(PTs[:, h % 2, lo:hi], bank("pt", h, c)[:, 0:hi - lo], ACT.Copy
                                   ).then_inc(free_sem("pt", h, c), 1)
            act.wait_ge(S("mean_eps"), 2)
            rsqrt_guess(act, ra, ssa)
            for j in range(4):
                full(act, "oT", j)
                act.activation(HT[:, 4 + j, :], bank("oT", j), ACT.Copy, scale=agc[:, j:j + 1]
                               ).then_inc(free_sem("oT", j), 1)
            for i in range(TT):
                for n in range(2):
                    freed(act, "x2", i, n)
                if i:
                    act.wait_ge(S("ss2"), i)
                act.activation(H2[:, i, :], X[:, i, :], ACT.Square, accum_out=ss2[:, i:i + 1]).then_inc(S("ss2"), 1)
            act.wait_ge(S("mean_eps"), 3)
            rsqrt_guess(act, r2, ss2)
            for k in range(1, DK, 2):
                full(act, "h2T", k)
                act.activation(HT[:, k, :], bank("h2T", k), ACT.Copy).then_inc(free_sem("h2T", k), 1)
            act.wait_ge(S("lg_shifted"), 1)
            act.activation(LG[:, 1, :], LG[:, 1, :], ACT.Exp).then_inc(S("lg_exp"), 1)

            def cast(q, n, m):
                act.wait_ge(raw_landed[q.slot(m, RAW)], (q.turn(m, RAW) + 1) * 16)
                if q.starts(m) >= SPL:
                    act.wait_ge(chunk_used, q.count(m, 1 - SPL))
                act.activation(wh[:, q.slot(m, SPL), :], raw[q.slot(m, RAW)][:, :], ACT.Copy).then_inc(wh_ready, 1)

            def x_high(e, use):
                act.wait_ge(t_full, use + 1)
                act.activation(xh[:, :, :].rearrange("p k m -> p (k m)"), Tflat, ACT.Copy).then_inc(xh_ready, 1)

            def a_high(q, use):
                act.wait_ge(t_full, use + 1)
                act.activation(ah[:, :, :].rearrange("p k m -> p (k m)"), Tflat, ACT.Copy, scale=1.0 / ALPHA
                               ).then_inc(ah_ready, 1)

            def silu(q, up_chunks_end):
                act.wait_ge(chunk_used, up_chunks_end)
                if not isinstance(q, int) or q:
                    act.wait_ge(a_ready, q)
                act.activation(LN[:, :], Uflat[:, :, 1], ACT.Copy, bias=1.0).then_inc(lin_ready, 1)
                act.activation(SG[:, :], Uflat[:, :, 0], ACT.Silu, scale=ALPHA).then_inc(u_free, 1)

            def gated(q, column, down_chunks_end):
                act.wait_ge(chunk_used, down_chunks_end)
                act.wait_ge(blocks_added, q + 1)
                act.activation(Y[:, :], Yflat, ACT.Copy, scale=slot_t[:, bass.ds(column, 1), 1:2].rearrange("p a b -> p (a b)")
                               ).then_inc(y_ready, 1)

            def step(e, q, up, down, y):
                for n in range(NC):
                    if (n < UPC and up) or (n >= UPC and down):
                        cast(q, n, n if up else n - UPC)
                    if n == 1 and y:
                        gated(e - 2, e - 2, q.count(0, 0))
                    if n == 3 and down:
                        a_high(e - 1, use_a(e - 1))
                    if n == 10 and up:
                        silu(e, q.count(UPC - 1, 1))
                        x_high(e + 1, use_x(e + 1) if down else X1)

            act.wait_ge(S("front_done"), 1)
            x_high(0, X0)
            step(0, FIRST, True, False, False)
            step(1, Chunks(0, 0, UPC), True, True, False)
            with act.Fori(2, NE) as e:
                step(e, main_chunks(e), True, True, True)
            gated(NE - 2, NE - 2, END.count(0))
            a_high(NE - 1, use_a(NE - 1))
            for n in range(UPC, NC):
                cast(END, n, n - UPC)
            gated(NE - 1, NE - 1, END.count(DNC))
            act.wait_ge(S("items_ready"), 1)
            nx = act.value_load(CNT[0:1, 0:1], min_val=0, max_val=MAXX)
            with act.Fori(0, MAXX) as j:
                with act.If(nx > j):
                    q = over_chunks(j)
                    x_high(j, j * 3 + (OVER + 1))
                    for n in range(UPC):
                        cast(q, n, n)
                    silu(j + NE, q.count(UPC - 1, 1))
                    a_high(j + NE, j * 3 + (OVER + 2))
                    for n in range(UPC, NC):
                        cast(q, n, n)
                    gated(j + NE, 0, q.count(NC))
            for i in range(TT):
                act.wait_ge(S(f"xf_in{i}"), 16)
                act.activation(YF[:, i, :], XF[:, i, :], ACT.Square, accum_out=ss1[:, i:i + 1]).then_inc(S("ssf"), 1)
            act.wait_ge(S("mean_eps"), 4)
            rsqrt_guess(act, r1, ss1)

        @block.vector
        def _(dve):
            link_count = [0]

            def link(ins):
                link_count[0] += 1
                ins.then_inc(S("dve_link"), 1)
                dve.wait_ge(S("dve_link"), link_count[0])

            def mean_eps(dst, src, n):
                dve.tensor_scalar(dst, src, 1.0 / n, EPS, ALU.mult, ALU.add).then_inc(S("mean_eps"), 1)

            guesses = [0]

            def refined(r, mean, tmp):
                guesses[0] += 1
                dve.wait_ge(S("rsqrt_guess"), guesses[0])
                link(dve.tensor_tensor(tmp, r, r, ALU.mult))
                link(dve.scalar_tensor_tensor(tmp, tmp, -0.5, mean, ALU.mult, ALU.mult))
                return dve.scalar_tensor_tensor(r, tmp, 1.5, r, ALU.add, ALU.mult)

            def spread(col, n):
                return col.unsqueeze(2).broadcast_to([P, col.shape[1], n])

            dve.wait_ge(S("ss1"), TT)
            mean_eps(ss1, ss1, D)
            refined(r1, ss1, rtmp[:, 0:TT]).then_inc(S("r1"), 1)
            full(dve, "vec")
            dve.tensor_copy(vec_T, bank("vec")[:, 0:24]).then_inc(free_sem("vec"), 1)
            freed(dve, "vec")
            for k in range(0, DK, 2):
                full(dve, "hT", k)
                dve.tensor_scalar(HT[:, k, :], bank("hT", k), g1c[:, k:k + 1], None, ALU.mult
                                  ).then_inc(free_sem("hT", k), 1)
            link(dve.tensor_tensor(lbm, lbc[:, 0:4], lbc[:, 4:8], ALU.max))
            link(dve.tensor_tensor(lbe[:, 0:4], lbc[:, 0:4], lbm, ALU.subtract))
            dve.tensor_tensor(lbe[:, 4:8], lbc[:, 4:8], lbm, ALU.subtract).then_inc(S("lb_shifted"), 1)
            dve.wait_ge(S("lb_exp"), 1)
            link(dve.tensor_tensor(lbz, lbe[:, 0:4], lbe[:, 4:8], ALU.add))
            link(dve.reciprocal(lbz, lbz))
            link(dve.tensor_tensor(lb, lbe[:, 0:4], lbz, ALU.mult))
            link(dve.tensor_scalar(oml, lb, -1.0, 1.0, ALU.mult, ALU.add))
            for h in range(HH):
                freed(dve, "f", h)
                link(dve.tensor_scalar(F[:, h, :], F[:, h, :], oml[:, h:h + 1], lb[:, h:h + 1], ALU.mult, ALU.add))
                dve.tensor_scalar(K[:, h, :], F[:, h, :], -1.0, 1.0, ALU.mult, ALU.add).then_inc(S("f_ready"), 1)

            def gate(h):
                dve.wait_ge(S("g_sig"), h + 1)
                dve.scalar_tensor_tensor(G[:, h, :], G[:, h, :], hgc[:, h:h + 1], bank("g", h), ALU.mult, ALU.mult
                                         ).then_inc(free_sem("g", h), 1)

            def chunked(ap):
                return ap.rearrange("p (c s) -> p c s", s=CH)

            def decays(h):
                if h == 0:
                    dve.wait_ge(S("log_f"), HH)
                else:
                    dve.wait_ge(S("exps"), 5 * h)
                link(dve.tensor_tensor_scan(B[:, :], cst("chunk_go"), F[:, h, :], 0.0, ALU.mult, ALU.add))
                bc = chunked(B[:, :])
                mid = bc[:, :, CH // 2 - 1:CH // 2].broadcast_to([P, NCH, CH])
                end = bc[:, :, CH - 1:CH].broadcast_to([P, NCH, CH])
                dve.tensor_tensor(chunked(DE[:, :]), end, bc, ALU.subtract).then_inc(S("decays"), 1)
                dve.tensor_tensor(chunked(DD[:, :]), bc, mid, ALU.subtract).then_inc(S("decays"), 1)
                dve.wait_ge(S("decays"), 3 * h + 2)
                dve.tensor_scalar(DD[:, :], DD[:, :], 80.0, -80.0, ALU.min, ALU.max).then_inc(S("decays"), 1)

            def scaled(h):
                b = h % 2
                dve.wait_ge(S("exps"), 5 * h + 5)
                if h == 0:
                    freed(dve, "q", 3)
                for buf, by in ((QE, Q), (KE, K), (KD, K), (QB, Q)):
                    dve.tensor_tensor(buf[:, b, :], buf[:, b, :], by[:, h, :], ALU.mult).then_inc(S("qk_scaled"), 1)

            decays(0)
            scaled(0)
            for h in range(HH):
                b = h % 2
                full(dve, "sc", h)
                dve.scalar_tensor_tensor(A[:, b, :, :], bank("sc", h).rearrange("p (t m) -> p t m", m=P), 3e38,
                                         cst("chunk_causal").unsqueeze(1).broadcast_to([P, TT, P]), ALU.min, ALU.mult
                                         ).then_inc(free_sem("sc", h), 1)
                if h + 1 < HH:
                    decays(h + 1)
                if h == 0:
                    gate(0)
                for j in range(4):
                    full(dve, "kv", h, j)
                if h:
                    full(dve, "o", h - 1)
                for c in range(1, NCH):
                    kv = bank("kv", h, (c - 1) % 4)[:, (c - 1) // 4 * P:(c - 1) // 4 * P + P]
                    if c == 1:
                        ins = dve.tensor_copy(ST[:, 1, :], kv)
                    else:
                        ins = dve.scalar_tensor_tensor(ST[:, c, :], ST[:, c - 1, :],
                                                       dec[:, NCH * b + c - 1:NCH * b + c], kv, ALU.mult, ALU.add)
                    if c >= NCH - 4:
                        last = {NCH - 4: 3, NCH - 3: 0, NCH - 2: 1, NCH - 1: 2}[c]
                        ins.then_inc(free_sem("kv", h, last), 1)
                        if c < NCH - 1:
                            freed(dve, "kv", h, last)
                    else:
                        link(ins)
                if h + 1 < HH:
                    scaled(h + 1)
                if h == 0:
                    gate(1)
                    gate(2)
                full(dve, "ss", h)
                if h == 0:
                    freed(dve, "g", 0)
                dve.tensor_scalar(RM[:, :], bank("ss", h), 1.0 / P, EPS, ALU.mult, ALU.add).then_inc(free_sem("ss", h), 1)
                freed(dve, "ss", h)
                link(refined(R[:, :], RM[:, :], RN[:, :]))
                link(dve.tensor_tensor(R[:, :], R[:, :], G[:, h, :], ALU.mult))
                dve.tensor_tensor(G[:, h, :], bank("o", h), R[:, :], ALU.mult).then_inc(free_sem("o", h), 1)
                if h == 0:
                    gate(3)
                elif h < HH:
                    freed(dve, "g", h)

            def masked_max(h):
                for i in range(TT):
                    full(dve, "qk", h, i)
                    n = TT * (h % 2) + i
                    if h >= 2:
                        full(dve, "pt", h - 2, 2)
                    dve.tensor_tensor_reduce(E[:, h % 2, EOFF[i]:EOFF[i] + P * (i + 1)], bank("qk", h, i)[:, 0:P * (i + 1)],
                                             cst("pairs")[:, (TT - 1 - i) * P:], 1.0, -3e38, ALU.add, ALU.max,
                                             mx[:, n:n + 1]).then_inc(free_sem("qk", h, i), 1)
                    freed(dve, "qk", h, i)
                    dve.tensor_scalar(nmx[:, n:n + 1], mx[:, n:n + 1], -DH ** -0.5, None, ALU.mult
                                      ).then_inc(S("neg_max"), 1)

            masked_max(0)
            for h in range(AH):
                if h + 1 < AH:
                    masked_max(h + 1)
                full(dve, "pt", h, 1)
                if h >= 2:
                    full(dve, "pv", h - 2)
                dve.tensor_copy(PTs[:, h % 2, 512:1024], bank("pt", h, 1)).then_inc(free_sem("pt", h, 1), 1)
                dve.wait_ge(S("probs"), TT * (h + 1))
                b = TT * (h % 2)
                link(dve.reciprocal(rden[:, b:b + TT], den[:, b:b + TT]))
                full(dve, "pv", h)
                dve.tensor_tensor(OA[:, :, h * DH:(h + 1) * DH], bank("pv", h)[:, 0:TT * DH].rearrange("p (t d) -> p t d", d=DH),
                                  spread(rden[:, b:b + TT], DH), ALU.mult).then_inc(free_sem("pv", h), 1)
                freed(dve, "pv", h)
                oh = OA[:, :, h * DH:(h + 1) * DH]
                link(dve.tensor_tensor(osq[:, :, :], oh, oh, ALU.mult))
                link(dve.tensor_reduce(ssa[:, TT * h:TT * (h + 1)], osq[:, :, :], AX.X, ALU.add))
            mean_eps(ssa, ssa, DH)
            link(refined(ra, ssa, rtmp[:, 0:AH * TT]))
            for h in range(AH):
                oh = OA[:, :, h * DH:(h + 1) * DH]
                dve.tensor_tensor(oh, oh, spread(ra[:, TT * h:TT * (h + 1)], DH), ALU.mult).then_inc(S("attn_read"), 1)

            dve.wait_ge(S("bias_in"), 64)
            dve.tensor_copy(bias_hl[:, :], bias_raw[:, :]).then_inc(S("bias_high"), 1)
            dve.wait_ge(S("bias_high"), 1)
            link(dve.tensor_tensor(bias_hl[NE:2 * NE, :], bias_raw[NE:2 * NE, :], bias_hl[NE:2 * NE, :].bitcast(F32), ALU.subtract))

            for i in range(TT):
                for n in range(2):
                    full(dve, "x2", i, n)
                    dve.tensor_tensor(X[:, i, n * 512:(n + 1) * 512], X[:, i, n * 512:(n + 1) * 512], bank("x2", i, n), ALU.add
                                      ).then_inc(free_sem("x2", i, n), 1)
            dve.wait_ge(S("ss2"), TT)
            mean_eps(ss2, ss2, D)
            link(refined(r2, ss2, rtmp[:, 0:TT]))
            dve.wait_ge(S("g2_in"), 16)
            for i in range(TT):
                dve.scalar_tensor_tensor(H2[:, i, :], X[:, i, :], r2[:, i:i + 1], G2[:, :], ALU.mult, ALU.mult
                                         ).then_inc(S("h2_rows"), 1)
            for k in range(0, DK, 2):
                full(dve, "h2T", k)
                dve.tensor_copy(HT[:, k, :], bank("h2T", k)).then_inc(free_sem("h2T", k), 1)

            def lgv(n):
                return LG[:, n, :].rearrange("p (t e) -> p t e", e=NE)

            full(dve, "lg")
            link(dve.tensor_copy(LG[:, 0, :], bank("lg")[:, 0:TT * NE]))
            for i in range(TT):
                ins = dve.max(top8[:, i, :], LG[:, 0, i * NE:(i + 1) * NE])
                link(ins)
            largest = top8[:, :, 0:1].broadcast_to([P, TT, NE])
            fourth = top8[:, :, TOPK - 1:TOPK].broadcast_to([P, TT, NE])
            dve.tensor_tensor(lgv(1), lgv(0), largest, ALU.subtract).then_inc(S("lg_shifted"), 1)
            link(dve.tensor_tensor(lgv(2), lgv(0), fourth, ALU.is_gt))
            link(dve.tensor_tensor(lgv(3), lgv(0), fourth, ALU.is_equal))
            link(dve.tensor_tensor_scan(LG[:, 4, :], cst("tile_go"), LG[:, 3, :], 0.0, ALU.mult, ALU.add))
            link(dve.tensor_reduce(rt[:, 0, :], lgv(2), AX.X, ALU.add))
            link(dve.tensor_scalar(rt[:, 0, :], rt[:, 0, :], -1.0, float(TOPK), ALU.mult, ALU.add))
            link(dve.tensor_tensor(lgv(4), lgv(4), spread(rt[:, 0, :], NE), ALU.is_le))
            link(dve.tensor_tensor(LG[:, 3, :], LG[:, 3, :], LG[:, 4, :], ALU.mult))
            dve.tensor_tensor(LG[:, 2, :], LG[:, 2, :], LG[:, 3, :], ALU.add).then_inc(S("selected"), 1)
            dve.wait_ge(S("selected"), 1)
            dve.wait_ge(S("lg_exp"), 1)
            link(dve.tensor_tensor(LG[:, 1, :], LG[:, 1, :], LG[:, 2, :], ALU.mult))
            link(dve.tensor_reduce(rt[:, 1, :], lgv(1), AX.X, ALU.add))
            link(dve.reciprocal(rt[:, 1, :], rt[:, 1, :]))
            link(dve.memset(pos_t[:, :, :], -1.0))
            link(dve.memset(vals_t[:, :, :, :], 0.0))
            link(dve.tensor_tensor(vals_t[:, :, 0:NE, 1:2].rearrange("p t e o -> p t (e o)"), lgv(1), spread(rt[:, 1, :], NE), ALU.mult))
            full(dve, "pos")
            link(dve.scalar_tensor_tensor(LG[:, 5, :], bank("pos")[:, 0:TT * NE], 1.0, LG[:, 2, :], ALU.add, ALU.mult))
            link(dve.tensor_copy(LG[:, 6, 0:NE], bank("pos")[:, TT * NE:TT * NE + NE]))
            link(dve.tensor_scalar(pos_t[:, :, 0:NE], lgv(5), -1.0, None, ALU.add))
            link(dve.tensor_scalar(lgv(7), pos_t[:, :, 0:NE], float(P), None, ALU.is_ge))
            link(dve.scalar_tensor_tensor(lgv(7), pos_t[:, :, 0:NE], float(2 * P), lgv(7), ALU.is_ge, ALU.add))
            link(dve.scalar_tensor_tensor(lgv(7), pos_t[:, :, 0:NE], float(3 * P), lgv(7), ALU.is_ge, ALU.add))
            link(dve.scalar_tensor_tensor(lgv(7), lgv(7), -float(P), pos_t[:, :, 0:NE], ALU.mult, ALU.add))
            link(dve.tensor_tensor(vals_t[:, :, 0:NE, 0:1].rearrange("p t e o -> p t (e o)"), spread(cst("tok"), NE), lgv(7), ALU.subtract))
            cnt = LG[:, 6, 0:NE]
            ext, base, last = LG[:, 6, NE:2 * NE], LG[:, 6, 2 * NE:3 * NE], LG[:, 6, 3 * NE:4 * NE]
            link(dve.tensor_scalar(ext, cnt, float(P), None, ALU.is_gt))
            link(dve.scalar_tensor_tensor(ext, cnt, float(2 * P), ext, ALU.is_gt, ALU.add))
            link(dve.scalar_tensor_tensor(ext, cnt, float(3 * P), ext, ALU.is_gt, ALU.add))
            link(dve.tensor_tensor_scan(last, ones[:, 0:NE], ext, 0.0, ALU.mult, ALU.add))
            link(dve.tensor_tensor(base, last, ext, ALU.subtract))
            it1, it2 = items[:, 0, :, :], items[:, 1, :, :]
            num = spread(cst("item"), NE)
            link(dve.tensor_tensor(it1, base.unsqueeze(1).broadcast_to([P, MAXX, NE]), num, ALU.is_le))
            link(dve.tensor_tensor(it2, last.unsqueeze(1).broadcast_to([P, MAXX, NE]), num, ALU.is_gt))
            link(dve.tensor_tensor(it1, it1, it2, ALU.mult))
            link(dve.tensor_tensor(it2, num, base.unsqueeze(1).broadcast_to([P, MAXX, NE]), ALU.subtract))
            link(dve.scalar_tensor_tensor(it2, it2, 1.0, it1, ALU.add, ALU.mult))
            link(dve.tensor_reduce(block_off[:, :], it2, AX.X, ALU.add))
            link(dve.tensor_scalar(block_off[:, :], block_off[:, :], -float(P), None, ALU.mult))
            link(dve.tensor_tensor(it2, it1, cst("iota")[:, 0:NE].unsqueeze(1).broadcast_to([P, MAXX, NE]), ALU.mult))
            link(dve.tensor_reduce(itf[:, :], it2, AX.X, ALU.add))
            link(dve.tensor_copy(CNT[:, MAXX:2 * MAXX], itf[:, :]))
            link(dve.tensor_copy(CNT[:, 0:1], last[:, NE - 1:NE]))
            dve.tensor_copy(CNT[:, 1:2], last[:, NE - 1:NE]).then_inc(S("items_ready"), 1)
            dve.wait_ge(S("items_ready"), 1)
            dve.wait_ge(S("rows_out"), 32)
            full(dve, "pos")
            dve.tensor_copy(CNT[:, 2:3], last[:, NE - 1:NE]).then_inc(S("front_done"), 1)

            def make_sel(col, offset=None):
                for i in range(TT):
                    p_col = pos_t[:, i, bass.ds(col, 1)]
                    if offset is None:
                        ins = dve.tensor_scalar(SEL[:, i, :], cst("iota"), p_col, None, ALU.is_equal)
                    else:
                        ins = dve.tensor_scalar(SEL[:, i, :], cst("iota"), p_col, offset, ALU.subtract, ALU.is_equal)
                    ins.then_inc(sel_ready, 1)

            def slot_rows(g, use, col, before=True):
                dve.wait_ge(t_full, use + 1)
                if before:
                    dve.wait_ge(gathered, g * 16)
                dve.tensor_tensor(IDXG[:, 0:1], Tflat[:, 0:1], cst("dump_row")[:, 0:1], ALU.add).then_inc(idxg_ready, 1)
                dve.tensor_tensor(slot_t[:, bass.ds(col, 1), :].rearrange("p a b -> p (a b)"), Tflat[:, 0:2], cst("dump_row"), ALU.add
                                  ).then_inc(t_free, 1)

            def split(q, m):
                dve.wait_ge(wh_ready, q.count(m, 1))
                dve.tensor_tensor(wl[:, q.slot(m, SPL), :], raw[q.slot(m, RAW)][:, :],
                                  wh[:, q.slot(m, SPL), :].bitcast(F32), ALU.subtract).then_inc(wl_ready, 1)

            def x_low(g, use):
                dve.wait_ge(xh_ready, g + 1)
                dve.tensor_tensor(xl[:, :, :].rearrange("p k m -> p (k m)"), Tflat,
                                  xh[:, :, :].rearrange("p k m -> p (k m)").bitcast(F32), ALU.subtract).then_inc(t_free, 1)

            def a_low(q):
                dve.wait_ge(ah_ready, q + 1)
                dve.scalar_tensor_tensor(al[:, :, :].rearrange("p k m -> p (k m)"), Tflat, 1.0 / ALPHA,
                                         ah[:, :, :].rearrange("p k m -> p (k m)").bitcast(F32), ALU.mult, ALU.subtract
                                         ).then_inc(t_free, 1)

            def bias_row(buf, col, done):
                dve.tensor_scalar(buf[:, :], ones[0:64, :], cst("expert_row")[0:64, bass.ds(col, 1)], None, ALU.mult
                                  ).then_inc(done, 1)

            def scatter_rows(q, col):
                dve.wait_ge(blocks_added, q + 1)
                dve.tensor_copy(IDXS[:, 0:1], slot_t[:, bass.ds(col, 1), 0:1].rearrange("p a b -> p (a b)")).then_inc(idxs_ready, 1)

            def swiglu(q):
                dve.wait_ge(lin_ready, q + 1)
                dve.tensor_scalar(LN[:, :], LN[:, :], LIMIT + 1.0, 1.0 - LIMIT, ALU.min, ALU.max).then_inc(lin_clipped, 1)
                dve.wait_ge(u_free, q + 1)
                dve.wait_ge(lin_clipped, q + 1)
                dve.scalar_tensor_tensor(GL[:, :], SG[:, :], SILU_LIMIT, LN[:, :], ALU.min, ALU.mult).then_inc(a_ready, 1)

            def step(e, q, up, down, y):
                for n in range(NC):
                    if (n < UPC and up) or (n >= UPC and down):
                        split(q, n if up else n - UPC)
                    if n == 0 and y:
                        scatter_rows(e - 2, e - 2)
                    if n == 2 and up:
                        make_sel(e + 2)
                    if n == 3 and down:
                        a_low(e - 1)
                        bias_row(BSD, e - 1, bsd_ready)
                    if n == 6 and up:
                        slot_rows(e + 2, use_sel(e + 2) if down else SEL2, e + 2)
                    if n == 9 and up:
                        bias_row(BSU, e + 1, bsu_ready)
                    if n == 10 and up:
                        x_low(e + 1, None)
                    if n == 11 and up:
                        swiglu(e)

            make_sel(0)
            slot_rows(0, SEL0, 0, before=False)
            bias_row(BSU, 0, bsu_ready)
            make_sel(1)
            x_low(0, X0)
            slot_rows(1, SEL1, 1)
            step(0, FIRST, True, False, False)
            step(1, Chunks(0, 0, UPC), True, True, False)
            with dve.Fori(2, NE) as e:
                step(e, main_chunks(e), True, True, True)
            scatter_rows(NE - 2, NE - 2)
            a_low(NE - 1)
            bias_row(BSD, NE - 1, bsd_ready)
            for n in range(UPC, NC):
                split(END, n - UPC)
            scatter_rows(NE - 1, NE - 1)
            nx = dve.value_load(CNT[0:1, 0:1], min_val=0, max_val=MAXX)
            with dve.Fori(0, MAXX) as j:
                with dve.If(nx > j):
                    ex = dve.value_load(CNT[0:1, bass.ds(j + MAXX, 1)], min_val=0, max_val=NE - 1)
                    q = over_chunks(j)
                    dve.wait_ge(blocks_added, j + NE + 1)
                    make_sel(ex, block_off[:, bass.ds(j, 1)])
                    slot_rows(j + NE + 2, j * 3 + OVER, 0)
                    bias_row(BSU, ex, bsu_ready)
                    bias_row(BSD, ex, bsd_ready)
                    x_low(j + NE + 1, None)
                    for n in range(UPC):
                        split(q, n)
                    swiglu(j + NE)
                    a_low(j + NE)
                    for n in range(UPC, NC):
                        split(q, n)
                    scatter_rows(j + NE, 0)
            dve.wait_ge(S("ssf"), TT)
            mean_eps(ss1, ss1, D)
            link(refined(r1, ss1, rtmp[:, 0:TT]))
            dve.wait_ge(S("gf_in"), 16)
            for i in range(TT):
                dve.scalar_tensor_tensor(YF[:, i, :], XF[:, i, :], r1[:, i:i + 1], GF[:, :], ALU.mult, ALU.mult
                                         ).then_inc(S("out_ready"), 1)

        @block.tensor
        def _(pe):
            def begin(*name):
                n = number[name]
                if n >= 8:
                    pe.wait_ge(bank_free[n % 8], n // 8)
                return bank(*name)

            def blocks(*name):
                return begin(*name).rearrange("p (t m) -> p t m", m=P)

            pe.wait_ge(S("c_in"), 16)
            pe.wait_ge(S("vec_in"), 64)
            pe.transpose(begin("vec")[:, 0:24], vec_rows[:, :], ident[0:24, 0:24]).then_inc(full_sem("vec"), 1)
            for k in range(DK):
                o = blocks("hT", k)
                for i in range(TT):
                    pe.wait_ge(S("xn"), i + 1)
                    ins = pe.transpose(o[:, i, :], XN[:, i, k * P:(k + 1) * P], ident)
                ins.then_inc(full_sem("hT", k), 1)
            for k in range(DK):
                freed(pe, "hT", k)

            def project(g, j):
                n = GORDER.index(g)
                pe.wait_ge(S(f"w_in{n % 2}"), 16 * (n // 2 + 1))
                o = begin(g, j)
                for k in range(DK):
                    if g in ("v", "av"):
                        l, r = HT[:, k, j * P:(j + 1) * P], Wb[:, n % 2, k, :]
                    else:
                        l, r = Wb[:, n % 2, k, j * P:(j + 1) * P], HT[:, k, :]
                    ins = pe.matmul(o, l, r, start=(k == 0), stop=(k == DK - 1))
                ins.then_inc(full_sem(g, j), 1)

            for g in ("f", "q", "v"):
                for j in range(4):
                    project(g, j)

            def hgrn_inputs(h):
                b = h % 2
                pe.wait_ge(S("qk_scaled"), 4 * (h + 1))
                o = blocks("kdT", h)
                for i in range(TT):
                    ins = pe.transpose(o[:, i, :], KD[:, b, i * P:(i + 1) * P], ident)
                ins.then_inc(full_sem("kdT", h), 1)
                o = blocks("sc", h)
                for i in range(TT):
                    s = slice(i * P, (i + 1) * P)
                    ins = pe.matmul(o[:, i, :], KE[:, b, s], QE[:, b, s], start=True, stop=True)
                ins.then_inc(full_sem("sc", h), 1)
                project(BETWEEN[h], 0)
                freed(pe, "kdT", h)
                if h == 0:
                    for j in range(4):
                        freed(pe, "v", j)
                for j in range(4):
                    o = blocks("kv", h, j)
                    r = slice(j * CH, (j + 1) * CH)
                    for i in range(TT):
                        ins = pe.matmul(o[:, i, :], KDT[r, b, i, :], V[r, i, h * P:(h + 1) * P], start=True, stop=True)
                    ins.then_inc(full_sem("kv", h, j), 1)
                project(BETWEEN[h], 1)

            def hgrn_outputs(h):
                b = h % 2
                o = begin("o", h)
                freed(pe, "sc", h)
                freed(pe, "kv", h, 2)
                for i in range(TT):
                    s = slice(i * P, (i + 1) * P)
                    ins = pe.matmul(o[:, s], V[:, i, h * P:(h + 1) * P], A[:, b, i, :], start=(i == 0), stop=False,
                                    skip_group_check=True)
                for c in range(1, NCH):
                    s = slice(c * CH, (c + 1) * CH)
                    ins = pe.matmul(o[:, s], ST[:, c, :], QB[:, b, s], start=False, stop=(c == NCH - 1),
                                    skip_group_check=True)
                ins.then_inc(full_sem("o", h), 1)
                project(BETWEEN[h], 2)
                o = begin("ss", h)
                pe.wait_ge(S("o_sq"), h + 1)
                pe.matmul(o, ones, SQ[:, :], start=True, stop=True).then_inc(full_sem("ss", h), 1)
                project(BETWEEN[h], 3)

            for h in range(HH):
                hgrn_inputs(h)
                hgrn_outputs(h)

            def attn_scores(h):
                if h == 0:
                    for j in range(4):
                        freed(pe, "aq", j)
                        freed(pe, "ak", j)
                        freed(pe, "av", j)
                r = slice(DH * (h % 2), DH * (h % 2) + DH)
                for i in range(TT):
                    ins = pe.matmul(begin("qk", h, i)[:, 0:(i + 1) * P], AQ[r, h // 2, i * P:(i + 1) * P],
                                    AK[r, h // 2, 0:(i + 1) * P], start=True, stop=True)
                    ins.then_inc(full_sem("qk", h, i), 1)

            attn_scores(0)
            for h in range(AH):
                if h + 1 < AH:
                    attn_scores(h + 1)
                pe.wait_ge(S("probs"), TT * (h + 1))
                for c, tiles in enumerate(((0,), (1, 3), (2,))):
                    o = begin("pt", h, c)
                    for kt in tiles:
                        for i in range(kt, TT):
                            a = KB[kt] - KB[tiles[0]] + (i - kt) * P
                            e0 = EOFF[i] + kt * P
                            ins = pe.transpose(o[:, a:a + P], E[:, h % 2, e0:e0 + P], ident)
                    ins.then_inc(full_sem("pt", h, c), 1)
                o = begin("pv", h)
                for c in range(3):
                    freed(pe, "pt", h, c)
                for i in range(TT):
                    for kt in range(i + 1):
                        a = KB[kt] + (i - kt) * P
                        ins = pe.matmul(o[:, i * DH:(i + 1) * DH], PTs[:, h % 2, a:a + P], AV[:, kt, h * DH:(h + 1) * DH],
                                        start=(kt == 0), stop=(kt == i))
                ins.then_inc(full_sem("pv", h), 1)
            pe.wait_ge(S("attn_read"), AH)
            for j in range(4):
                o = blocks("oT", j)
                for i in range(TT):
                    ins = pe.transpose(o[:, i, :], OA[:, i, j * P:(j + 1) * P], ident)
                ins.then_inc(full_sem("oT", j), 1)
            for j in range(4):
                freed(pe, "oT", j)
            for h in range(HH):
                freed(pe, "o", h)
            for n in range(7, 9):
                pe.wait_ge(S(f"w_in{n % 2}"), 16 * (n // 2 + 1))
            for i in range(TT):
                for n in range(2):
                    o = begin("x2", i, n)
                    for k in range(DK):
                        mixed = G[:, k, i * P:(i + 1) * P] if k < HH else HT[:, k, i * P:(i + 1) * P]
                        ins = pe.matmul(o, mixed, Wb[:, (7 + n) % 2, k, :], start=(k == 0), stop=(k == DK - 1))
                    ins.then_inc(full_sem("x2", i, n), 1)
            for k in range(DK):
                o = blocks("h2T", k)
                for i in range(TT):
                    pe.wait_ge(S("h2_rows"), i + 1)
                    ins = pe.transpose(o[:, i, :], H2[:, i, k * P:(k + 1) * P], ident)
                ins.then_inc(full_sem("h2T", k), 1)
            for k in range(DK):
                freed(pe, "h2T", k)
            pe.wait_ge(S("rw_in"), 16)
            pe.wait_ge(S("rb_in"), 16)
            o = begin("lg")
            for i in range(TT):
                s = o[:, i * NE:(i + 1) * NE]
                for k in range(DK):
                    pe.matmul(s, HT[:, k, i * P:(i + 1) * P], rw_sb[:, k, :], start=(k == 0), stop=False)
                ins = pe.matmul(s, ones[0:1, :], rb_row[0:1, :], start=False, stop=True)
            ins.then_inc(full_sem("lg"), 1)
            pe.wait_ge(S("selected"), 1)
            o = begin("pos")
            for i in range(TT + 1):
                s = o[:, i * NE:(i + 1) * NE]
                for t in range(min(i + 1, TT)):
                    ins = pe.matmul(s, cst("before") if t == i else ones, LG[:, 2, t * NE:(t + 1) * NE],
                                    start=(t == 0), stop=(t == min(i, TT - 1)))
            ins.then_inc(full_sem("pos"), 1)

            def select(g, use, col):
                pe.wait_ge(sel_ready, g * TT + TT)
                pe.wait_ge(t_free, use)
                for i in range(TT):
                    ins = pe.matmul(Tflat[:, 0:2], SEL[:, i, :], vals_t[:, i, bass.ds(col, 1), :].rearrange("p a b -> p (a b)"),
                                    start=(i == 0), stop=(i == TT - 1))
                ins.then_inc(t_full, 1)

            def x_transposed(g, use):
                pe.wait_ge(gathered, (g + 1) * 16)
                pe.wait_ge(t_free, use)
                for k in range(DK):
                    ins = pe.transpose(T[:, k, :], XG[:, k * P:(k + 1) * P], ident)
                ins.then_inc(t_full, 1)

            def a_transposed(q, use):
                pe.wait_ge(a_ready, q + 1)
                pe.wait_ge(t_free, use)
                for k in range(DK):
                    ins = pe.transpose(T[:, k, :], GL[:, k * P:(k + 1) * P], ident)
                ins.then_inc(t_full, 1)

            def products(o, high, low, w_high, w_low, width, last):
                for x_part, w_part in ((low, w_high), (high, w_high), (high, w_low)):
                    for j in range(width // 512):
                        ins = pe.matmul(o[:, j, :], x_part, w_part[:, j * 512:(j + 1) * 512], start=False,
                                        stop=(last and x_part is high and w_part is w_low))
                return ins

            def up(ordinal, q, bias_ordinal, x_use):
                pe.wait_ge(bsu_ready, bias_ordinal + 1)
                pe.wait_ge(t_free, x_use + 1)
                if not isinstance(ordinal, int) or ordinal:
                    pe.wait_ge(u_free, ordinal)
                for j in range(4):
                    pe.matmul(U[:, j, :], BSU[:, :], bias_hl[:, j * 512:(j + 1) * 512], start=True, stop=False)

            def up_chunk(q, m, c, last=False):
                pe.wait_ge(wl_ready, q.count(m, 1))
                s = q.slot(m, SPL)
                return products(U, xh[:, c, :], xl[:, c, :], wh[:, s, :], wl[:, s, :], NF, last)

            def down(ordinal, a_use):
                pe.wait_ge(bsd_ready, ordinal + 1)
                pe.wait_ge(t_free, a_use + 1)
                if not isinstance(ordinal, int) or ordinal:
                    pe.wait_ge(y_ready, ordinal)
                for j in range(2):
                    pe.matmul(Yp[:, j, :], BSD[:, :], bias_hl[:, NF + j * 512:NF + (j + 1) * 512], start=True, stop=False)

            def down_chunk(q, m, c, last=False):
                pe.wait_ge(wl_ready, q.count(m, 1))
                s = q.slot(m, SPL)
                for t in range(2):
                    k = 2 * c + t
                    ins = products(Yp, ah[:, k, :], al[:, k, :], wh[:, s, t * D:(t + 1) * D], wl[:, s, t * D:(t + 1) * D],
                                   D, last and t == 1)
                return ins

            def step(e, q, has_up, has_down):
                if has_up:
                    up(e, q, e, use_x(e) if not isinstance(e, int) or e > 1 else (X0, X1)[e])
                    for c in range(UPC):
                        ins = up_chunk(q, c, c, c == UPC - 1)
                        ins.then_inc(chunk_used, 1)
                        if c == 1 and has_down:
                            a_transposed(e - 1, use_a(e - 1))
                        if c == 4:
                            select(e + 2, use_sel(e + 2) if has_down else SEL2, e + 2)
                else:
                    a_transposed(e - 1, use_a(e - 1))
                if has_down:
                    down(e - 1, use_a(e - 1))
                for c in range(DNC):
                    if has_down:
                        ins = down_chunk(q, (UPC if has_up else 0) + c, c, c == DNC - 1)
                        ins.then_inc(chunk_used, 1)
                    if c == 0 and has_up:
                        x_transposed(e + 1, use_x(e + 1) if has_down else X1)

            select(0, SEL0, 0)
            x_transposed(0, X0)
            select(1, SEL1, 1)
            step(0, FIRST, True, False)
            step(1, Chunks(0, 0, UPC), True, True)
            with pe.Fori(2, NE) as e:
                step(e, main_chunks(e), True, True)
            step(NE, END, False, True)
            pe.wait_ge(S("items_ready"), 1)
            nx = pe.value_load(CNT[0:1, 0:1], min_val=0, max_val=MAXX)
            with pe.Fori(0, MAXX) as j:
                with pe.If(nx > j):
                    ex = pe.value_load(CNT[0:1, bass.ds(j + MAXX, 1)], min_val=0, max_val=NE - 1)
                    q = over_chunks(j)
                    select(j + NE + 2, j * 3 + OVER, ex)
                    x_transposed(j + NE + 2, j * 3 + (OVER + 1))
                    up(j + NE, q, j + NE + 1, j * 3 + (OVER + 1))
                    for c in range(UPC):
                        up_chunk(q, c, c, c == UPC - 1).then_inc(chunk_used, 1)
                    a_transposed(j + NE, j * 3 + (OVER + 2))
                    down(j + NE, j * 3 + (OVER + 2))
                    for c in range(DNC):
                        down_chunk(q, UPC + c, c, c == DNC - 1).then_inc(chunk_used, 1)


def kernel(**inputs):
    import concourse.bacc as bacc
    from concourse.bass_utils import run_bass_kernel_spmd

    nc = bacc.Bacc("TRN2", target_bir_lowering=False, num_devices=1)
    names = ["x", "norm1_g", "w_in", "hgrn_lb_logits", "hgrn_norm_g", "attn_norm_g", "w_out", "norm2_g", "router_w",
             "router_b", "w_up", "b_up", "w_down", "b_down", "final_norm_g"]
    consts, where = shape_constants()
    arrays = {name: np.ascontiguousarray(inputs[name]) for name in names}
    arrays["shape_constants"] = consts
    args = [nc.dram_tensor(name, a.shape, mybir.dt.from_np(a.dtype), kind="ExternalInput").ap() for name, a in arrays.items()]
    out = nc.dram_tensor("out", (1, SEQ, D), F32, kind="ExternalOutput").ap()
    hybrid_moe_block(nc, *args, out, where)
    r = run_bass_kernel_spmd(nc, [arrays], core_ids=[0])
    return r.results[0]["out"]
```

```python
import math
from contextlib import ExitStack

import numpy as np

import concourse.bass as bass
from concourse import mybir

F32 = mybir.dt.float32
F32R = mybir.dt.float32r
I32 = mybir.dt.int32
ALU = mybir.AluOpType
ACT = mybir.ActivationFunctionType
AX = mybir.AxisListType

P = 128
SEQ = 512
TT = SEQ // P
D = 1024
DK = D // P
HALF = D // 2
HH = 4
AH = 8
DH = HALF // AH
CH = 32
NCH = SEQ // CH
NE = 32
TOPK = 4
NF = 2 * D
EPS = 1e-6
ALPHA = 1.702
LIMIT = 7.0
SILU_LIMIT = ALPHA * LIMIT / (1.0 + math.exp(-ALPHA * LIMIT))
PATTERNS = ((128, 1), (512, 4), (2048, 16))
MAXX = 16
NEG = -1e30

RAW = 12
SPL = 3
UPC = DK
DNC = DK // 2
NC = UPC + DNC


def shape_constants():
    p = np.arange(P)[:, None]
    f = np.arange(P)[None, :]
    cols = {}
    cols["ident"] = (p == f) * 1.0
    cols["ones"] = np.ones((P, P))
    cols["before"] = (p < f) * 1.0
    cols["iota"] = np.broadcast_to(f, (P, P)) * 1.0
    blocks = []
    for delta in range(TT - 1, -1, -1):
        d = P * delta + p - f
        count = np.zeros((P, P))
        for window, dil in PATTERNS:
            count += (d >= 0) & (d % dil == 0) & (d // dil <= window // dil)
        blocks.append(np.where(count > 0, np.log(np.maximum(count, 1)) * DH ** 0.5, NEG))
    cols["pairs"] = np.concatenate(blocks, 1)
    cols["chunk_causal"] = ((p // CH == f // CH) & (p <= f)) * 1.0
    cols["chunk_go"] = np.broadcast_to((np.arange(SEQ) % CH != 0)[None, :], (P, SEQ)) * 1.0
    cols["tile_go"] = np.broadcast_to((np.arange(TT * NE) % NE != 0)[None, :], (P, TT * NE)) * 1.0
    cols["tok"] = P * np.arange(TT)[None, :] + p - SEQ
    cols["dump_row"] = np.concatenate([SEQ + p, 0 * p], 1)
    cols["expert_row"] = (p % NE == np.arange(NE + 2)[None, :]) * 1.0
    cols["item"] = np.broadcast_to(np.arange(MAXX)[None, :], (P, MAXX)) * 1.0
    at, where = 0, {}
    for name, a in cols.items():
        where[name] = (at, at + a.shape[1])
        at += a.shape[1]
    return np.concatenate(list(cols.values()), 1).astype(np.float32), where


def hybrid_moe_block(nc, x, norm1_g, w_in, lb_logits, hgrn_g, attn_g, w_out, norm2_g, router_w,
                     router_b, w_up, b_up, w_down, b_down, final_g, consts, out, where):
    x = x[0]
    w_in, w_out, router_w = w_in[0], w_out[0], router_w[0]
    w_up, b_up, w_down, b_down = w_up[0], b_up[0], w_down[0], b_down[0]
    out = out[0]
    normed_dram = nc.dram_tensor("normed_rows", (SEQ + P, D), F32, kind="Internal").ap()
    acc_dram = nc.dram_tensor("residual_rows", (SEQ + P, D), F32, kind="Internal").ap()

    ctx = ExitStack()
    with ctx:
        sems = {}

        def S(name):
            if name not in sems:
                sems[name] = ctx.enter_context(nc.semaphore(name))
            return sems[name]

        top = [16512]

        def at(name, shape, dt=F32):
            size = int(np.prod(shape[1:])) * 4
            t = nc.alloc_sbuf_tensor_at(name, shape, dt, offset=top[0])
            top[0] += -(-size // 32) * 32
            return t

        CW = max(b for _, b in where.values())
        C = at("shape_consts", [P, CW])

        def cst(name):
            a, b = where[name]
            return C[:, a:b]

        ident, ones = cst("ident"), cst("ones")
        bias_hl = at("bias_hl", [64, NF + D], F32R)
        pos_t = at("pos_t", [P, TT, NE + 2])
        vals_t = at("vals_t", [P, TT, NE + 2, 2])
        slot_t = at("slot_t", [P, NE + 2, 2])
        block_off = at("block_off", [P, MAXX])
        small = at("small", [P, 320])
        CNT = at("counts_i", [P, 2 * MAXX + 8], I32)
        rb_row = at("rb_row", [1, NE])
        shared = top[0]

        def over(name, shape, offset, dt=F32):
            return nc.alloc_sbuf_tensor_at(name, shape, dt, offset=offset)

        X = at("x_rows", [P, TT, D])
        ht0 = top[0]
        HT = at("h_T", [P, DK, SEQ])
        wb0 = top[0]
        Wb = at("w_buf", [P, 2, DK, 512])
        fk0 = top[0]
        F = at("f_T", [P, HH, SEQ])
        K = at("k_T", [P, HH, SEQ])
        Q = at("q_T", [P, HH, SEQ])
        g0 = top[0]
        G = at("gate_T", [P, HH, SEQ])
        v0 = top[0]
        V = at("v_rows", [P, TT, HALF])
        AQ = at("aq_T", [P, 4, SEQ])
        AK = at("ak_T", [P, 4, SEQ])
        AV = at("av_rows", [P, TT, HALF])
        oa0 = top[0]
        OA = at("attn_rows", [P, TT, HALF])
        rw_sb = at("router_w_sb", [P, DK, NE])
        hg0 = top[0]
        QE = at("q_mid", [P, 2, SEQ])
        KE = at("k_mid", [P, 2, SEQ])
        QB = at("q_start", [P, 2, SEQ])
        KD = at("k_end", [P, 2, SEQ])
        B = at("log_decay", [P, SEQ])
        DD = at("decay_to_mid", [P, SEQ])
        DE = at("decay_to_end", [P, SEQ])
        KDT = at("k_end_rows", [P, 2, TT, P])
        A = at("intra_T", [P, 2, TT, P])
        ST = at("states", [P, NCH, P])
        R = at("o_norm", [P, SEQ])
        RM = at("o_mean", [P, SEQ])
        RN = at("o_newton", [P, SEQ])
        SQ = at("o_sq", [P, SEQ])
        vec_rows = at("vec_rows", [24, P])
        HX = over("h_high", [P, DK, SEQ], ht0, F32R)
        HL = over("h_low", [P, DK, SEQ], shared, F32R)
        WPH = over("w_in_high", [P, 4, DK, P], wb0, F32R)
        WPL = over("w_in_low", [P, 4, DK, P], wb0 + 16384, F32R)
        WPR = over("w_in_raw", [P, 2, DK, P], oa0)
        XN = over("x_scaled", [P, TT, D], fk0)
        junk = over("x_sq", [P, D], g0)
        ZR = over("zero_rows", [P, D], hg0)
        E = over("scores", [P, 2, 1280], fk0)
        PTs = over("probs_T", [P, 2, 1280], fk0 + 10240)
        osq = over("attn_sq", [P, TT, DH], fk0 + 20480)
        assert fk0 + 20480 + 1024 <= g0
        H2T = HT[:, 0:HH, :].rearrange("p k s -> p (k s)").rearrange("p (b k m) -> p b k m", b=2, m=P)
        H2 = over("h2_rows", [P, TT, D], v0)
        G2 = over("g2_rows", [P, D], v0 + 16384)
        bias_raw = over("bias_raw", [64, NF + D], v0 + 20480)
        LG = over("router_work", [P, 8, TT * NE], oa0)
        assert v0 + 20480 + 12288 <= oa0 and oa0 + 8192 <= hg0

        top[0] = hg0
        raw = [at(f"w_raw{n}", [P, NF]) for n in range(6)]
        end = max(top[0], hg0 + 46 * 1024 + 512)
        assert end <= nc.sbuf_usable_end, (end, nc.sbuf_usable_end)
        raw += [over(f"w_raw{n}", [P, NF], fk0 + (n - 6) * 8192) for n in range(6, 9)]
        raw += [over(f"w_raw{n}", [P, NF], fk0 + (n - RAW) * 8192) for n in range(9, RAW)]
        assert fk0 + 3 * 8192 <= g0
        wh = over("w_high", [P, SPL, NF], g0, F32R)
        wl = over("w_low", [P, SPL, NF], g0 + SPL * 8192, F32R)
        assert g0 + 2 * SPL * 8192 <= hg0
        top[0] = shared
        XG = at("gathered", [P, D])
        xh = at("x_high", [P, DK, P], F32R)
        xl = at("x_low", [P, DK, P], F32R)
        GL = at("glu", [P, D])
        LN = at("lin", [P, D])
        SG = at("sig", [P, D])
        ah = at("a_high", [P, DK, P], F32R)
        al0 = top[0]
        al = at("a_low", [P, DK, P], F32R)
        Y = at("y_rows", [P, D])
        SEL = at("slot_sel", [P, TT, P])
        BSU = at("bias_sel_up", [64, P], F32R)
        BSD = at("bias_sel_down", [64, P], F32R)
        IDXG = at("gather_rows", [P, 1], I32)
        IDXS = at("scatter_rows", [P, 1], I32)
        assert top[0] <= fk0 - 3 * 8192
        items = over("item_work", [P, 2, MAXX, NE], al0)
        XF = over("final_rows", [P, TT, D], shared)
        GF = over("final_g_rows", [P, D], shared + 16384)
        YF = over("final_out", [P, TT, D], shared + 16384 + 4096)

        PS = ctx.enter_context(nc.psum_tensor("psum", [P, 8, 512], F32))

        vec_T = small[:, 0:24]
        g1c, lbc, hgc, agc = small[:, 0:8], small[:, 8:16], small[:, 16:20], small[:, 20:24]
        ss1, r1 = small[:, 24:28], small[:, 28:32]
        lbe = small[:, 32:40]
        lbm, lbz, lb, oml = small[:, 40:44], small[:, 44:48], small[:, 48:52], small[:, 52:56]
        mx, nmx = small[:, 56:64], small[:, 64:72]
        den, rden = small[:, 72:80], small[:, 80:88]
        ss2, r2 = small[:, 88:92], small[:, 92:96]
        ssa, ra = small[:, 96:128], small[:, 128:160]
        dec = small[:, 160:192]
        rtmp = small[:, 192:224]
        top8 = small[:, 224:256].rearrange("p (t n) -> p t n", n=8)
        rt = small[:, 256:264].rearrange("p (a t) -> p a t", t=TT)
        itf = small[:, 264:280]
        warm = small[:, 280:283]
        counts = small[:, 288:320]

        jobs = [("vec",)] + [("hT", k) for k in range(DK)]
        for g in ("f", "q", "v"):
            jobs += [(g, j) for j in range(4)]
        BETWEEN = ("g", "aq", "ak", "av")
        for h in range(HH):
            g = BETWEEN[h]
            kv = [("kv", h, j) for j in range(4)]
            jobs += [("kdT", h), ("sc", h)] + ([(g, 0)] + kv if g != "av" else kv + [(g, 0)])
            jobs += [(g, 1), ("o", h), (g, 2), ("ss", h), (g, 3)]
        jobs += [("qk", 0, i) for i in range(TT)]
        for h in range(AH):
            if h + 1 < AH:
                jobs += [("qk", h + 1, i) for i in range(TT)]
            jobs += [("xa", n) for n in ([h - 1] if 1 <= h < AH - 1 else [])]
            jobs += [("pt", h, c) for c in range(3)] + [("pv", h)]
        LATE_SHARES = (2 * TT - 2, 2 * TT - 1)
        jobs += [("xa", n) for n in LATE_SHARES]
        jobs += [("oT", j) for j in range(4)]
        for i in range(TT + 2):
            jobs += [("x2", i, n) for n in range(2) if i < TT]
            jobs += [("h2T", i - 1, n) for n in range(2) if 1 <= i <= TT]
            jobs += [("lg", i - 2)] if i >= 2 else []
        jobs += [("pos",)]
        number = {name: n for n, name in enumerate(jobs)}
        bank_full = [S(f"bank_full{b}") for b in range(8)]
        bank_free = [S(f"bank_free{b}") for b in range(8)]

        def bank(*name):
            return PS[:, number[name] % 8, :]

        def full(eng, *name):
            n = number[name]
            eng.wait_ge(bank_full[n % 8], n // 8 + 1)

        def freed(eng, *name):
            n = number[name]
            eng.wait_ge(bank_free[n % 8], n // 8 + 1)

        def free_sem(*name):
            return bank_free[number[name] % 8]

        def full_sem(*name):
            return bank_full[number[name] % 8]

        GROUPS = {"f": 1, "g": 3, "q": 0, "v": 2, "aq": 4, "ak": 5, "av": 6}
        GORDER = ["f", "q", "v", "g", "aq", "ak", "av"]

        def used(eng, c):
            g = GORDER[c // 4]
            full(eng, g, 3 if g in ("v", "av") else c % 4)

        KB = {0: 0, 1: 512, 3: 896, 2: 1024}
        EOFF = [128 * i * (i + 1) // 2 for i in range(TT)]

        U = PS[:, 0:4, :]
        Yp = PS[:, 4:6, :]
        T = PS[:, 6:8, :].rearrange("p b (k m) -> p (b k) m", m=P)
        Tflat = PS[:, 6:8, :].rearrange("p b f -> p (b f)")
        Uflat = PS[:, 0:4, :].rearrange("p b (f two) -> p (b f) two", two=2)
        Yflat = PS[:, 4:6, :].rearrange("p b f -> p (b f)")
        raw_landed = [S(f"raw_landed{s}") for s in range(RAW)]
        wh_ready, wl_ready, chunk_used = S("wh_ready"), S("wl_ready"), S("chunk_used")
        t_full, t_free = S("t_full"), S("t_free")
        sel_ready, idxg_ready, idxs_ready = S("sel_ready"), S("idxg_ready"), S("idxs_ready")
        gathered, acc_added, blocks_added = S("gathered"), S("acc_added"), S("blocks_added")
        xh_ready, ah_ready, bsu_ready, bsd_ready = S("xh_ready"), S("ah_ready"), S("bsu_ready"), S("bsd_ready")
        u_free, lin_ready, lin_clipped, a_ready = S("u_free"), S("lin_ready"), S("lin_clipped"), S("a_ready")
        y_ready = S("y_ready")

        class Chunks:

            def __init__(self, reg, mul, off):
                self.reg, self.mul, self.off = reg, mul, off

            def count(self, n, extra=0):
                return self.reg * self.mul + (self.off + n + extra)

            def slot(self, n, ring):
                return (self.off + n) % ring

            def turn(self, n, ring):
                return self.reg * (self.mul // ring) + (self.off + n) // ring

            def starts(self, n):
                return self.off + n if self.mul == 0 else NC + n

        CHUNKS = [("up", c) for c in range(UPC)] + [("down", c) for c in range(DNC)]
        FIRST = Chunks(0, 0, 0)
        SECOND = Chunks(0, 0, UPC)
        END = Chunks(0, 0, UPC + NC * (NE - 1))

        def main_chunks(e):
            return Chunks(e, NC, UPC - NC)

        def over_chunks(j):
            return Chunks(j, NC, NC * NE)

        SEL0, SEL1, X0, SEL2, X1 = range(5)

        def use_a(e):
            return e * 3 + 5

        def use_sel(e):
            return e * 3 - 3

        def use_x(e):
            return e * 3 + 1

        OVER = 5 + 3 * (NE - 1) + 1

        block = ctx.enter_context(nc.Block())

        @block.sync
        def _(sp):
            xv = x.rearrange("(t p) d -> p t d", p=P)
            for i in range(TT):
                sp.dma_start(X[:, i, :], xv[:, i, :]).then_inc(S(f"x_in{i}"), 16)
            sp.dma_start(C[:, :], consts).then_inc(S("c_in"), 16)
            sp.dma_start(vec_rows[0:8, :], norm1_g.rearrange("o (k p) -> (o k) p", p=P)).then_inc(S("vec_in"), 16)
            sp.dma_start(vec_rows[8:16, :], lb_logits.rearrange("r (k p) -> (r k) p", p=P)).then_inc(S("vec_in"), 16)
            sp.dma_start(vec_rows[16:20, :], hgrn_g.rearrange("o (k p) -> (o k) p", p=P)).then_inc(S("vec_in"), 16)
            sp.dma_start(vec_rows[20:24, :], attn_g.rearrange("o (k p) -> (o k) p", p=P)).then_inc(S("vec_in"), 16)
            sp.dma_start(rb_row[0:1, :], router_b).then_inc(S("rb_in"), 16)
            for c in range(4 * len(GORDER)):
                if c == 2:
                    sp.wait_ge(S("zero_rows"), 1)
                    sp.dma_start(acc_dram[SEQ:SEQ + P, :], ZR[:, :]).then_inc(S("zeros_out"), 16)
                    sp.dma_start(normed_dram[SEQ:SEQ + P, :], ZR[:, :]).then_inc(S("zeros_out"), 16)
                if c == 4:
                    sp.dma_start(rw_sb[:, :, :], router_w.rearrange("(k p) n -> p k n", p=P)).then_inc(S("rw_in"), 16)
                if c >= 2:
                    sp.wait_ge(S("w_in_low"), c - 1)
                col = GROUPS[GORDER[c // 4]] * 512 + c % 4 * P
                sp.dma_start(WPR[:, c % 2, :, :], w_in[:, col:col + P].rearrange("(k p) n -> p k n", p=P)
                             ).then_inc(S(f"w_in{c % 2}"), 16)
            full(sp, "av", 3)
            for n in range(2):
                sp.dma_start(Wb[:, n, :, :], w_out[:, n * 512:(n + 1) * 512].rearrange("(k p) n -> p k n", p=P)
                             ).then_inc(S(f"w_out{n}"), 16)
            sp.dma_start(X[:, :, :], xv).then_inc(S("x_again"), 16)

            def load(q, n, m, e):
                kind, c = CHUNKS[n]
                if q.starts(m) >= RAW:
                    sp.wait_ge(wl_ready, q.count(m, 1 - RAW))
                if kind == "up":
                    src = w_up[bass.ds(e, 1), c * P:(c + 1) * P, :].rearrange("e p n -> p (e n)")
                    dst = raw[q.slot(m, RAW)][:, :]
                else:
                    src = w_down[bass.ds(e, 1), 2 * c * P:2 * (c + 1) * P, :].rearrange("e (t p) n -> p (e t) n", p=P)
                    dst = raw[q.slot(m, RAW)][:, :].rearrange("p (t n) -> p t n", t=2)
                sp.dma_start(dst, src).then_inc(raw_landed[q.slot(m, RAW)], 16)

            def step(q, e_up, e_down, first=0):
                for n in range(first, NC):
                    e = e_up if n < UPC else e_down
                    if e is not None:
                        load(q, n, n if e_up is not None else n - UPC, e)

            freed(sp, "o", HH - 1)
            for n in range(6):
                load(FIRST, n, n, 0)
            sp.wait_ge(S("attn_read"), AH)
            sp.dma_start(G2[:, :], norm2_g.to_broadcast([P, D])).then_inc(S("g2_in"), 16)
            sp.dma_start(bias_raw[0:NE, 0:NF], b_up).then_inc(S("bias_in"), 16)
            sp.dma_start(bias_raw[0:NE, NF:NF + D], b_down).then_inc(S("bias_in"), 16)
            sp.dma_start(bias_raw[NE:2 * NE, 0:NF], b_up).then_inc(S("bias_in"), 16)
            sp.dma_start(bias_raw[NE:2 * NE, NF:NF + D], b_down).then_inc(S("bias_in"), 16)
            load(FIRST, 6, 6, 0)
            load(FIRST, 7, 7, 0)
            load(SECOND, 0, 0, 1)
            accv = acc_dram[0:SEQ, :].rearrange("(t p) d -> p t d", p=P)
            norv = normed_dram[0:SEQ, :].rearrange("(t p) d -> p t d", p=P)
            for i in range(TT):
                for n in range(2):
                    freed(sp, "x2", i, n)
                sp.dma_start(accv[:, i, :], X[:, i, :]).then_inc(S("rows_out"), 16)
                sp.wait_ge(S("h2_rows"), i + 1)
                sp.dma_start(norv[:, i, :], H2[:, i, :]).then_inc(S("rows_out"), 16)
            for n in range(1, 4):
                load(SECOND, n, n, 1)
            step(SECOND, 1, 0, first=4)
            with sp.Fori(2, NE) as e:
                step(main_chunks(e), e, e - 1)
            step(END, None, NE - 1)
            sp.wait_ge(S("items_ready"), 1)
            nx = sp.value_load(CNT[0:1, 0:1], min_val=0, max_val=MAXX)
            with sp.Fori(0, MAXX) as j:
                with sp.If(nx > j):
                    ex = sp.value_load(CNT[0:1, bass.ds(j + MAXX, 1)], min_val=0, max_val=NE - 1)
                    step(over_chunks(j), ex, ex)
            sp.wait_ge(blocks_added, nx + (NE + 1))
            sp.dma_start(GF[:, :], final_g.rearrange("(o d) -> o d", o=1).to_broadcast([P, D])).then_inc(S("gf_in"), 16)
            for i in range(TT):
                sp.dma_start(XF[:, i, :], accv[:, i, :]).then_inc(S(f"xf_in{i}"), 16)
            outv = out.rearrange("(t p) d -> p t d", p=P)
            for i in range(TT):
                sp.wait_ge(S("out_ready"), i + 1)
                sp.dma_start(outv[:, i, :], YF[:, i, :]).then_inc(S("stored"), 16)
            sp.wait_ge(S("stored"), 16 * TT)

        @block.gpsimd
        def _(pool):
            pool.memset(warm[:, 0:1], 1.0).then_inc(S("warm"), 1)
            pool.memset(ZR[:, :], 0.0).then_inc(S("zero_rows"), 1)

            def gather(g, x_before):
                pool.wait_ge(idxg_ready, g + 1)
                if x_before is not None:
                    pool.wait_ge(t_full, x_before + 1)
                pool.sem_inc(S("gathers_begun"), 1)
                pool.indirect_dma_start(XG[:, :], None, normed_dram, bass.IndirectOffsetOnAxis(IDXG[:, 0:1], 0)
                                        ).then_inc(gathered, 16)

            def scatter(q):
                pool.wait_ge(y_ready, q + 1)
                pool.wait_ge(idxs_ready, q + 1)
                pool.sem_inc(S("scatters_begun"), 1)
                pool.indirect_dma_start(acc_dram, bass.IndirectOffsetOnAxis(IDXS[:, 0:1], 0), Y[:, :], None,
                                        compute_op=ALU.add).then_inc(acc_added, 16)
                pool.wait_ge(acc_added, (q + 1) * 16)
                pool.sem_inc(blocks_added, 1)

            pool.wait_ge(S("zeros_out"), 32)
            pool.wait_ge(S("rows_out"), 32 * TT)
            pool.sem_inc(blocks_added, 1)
            gather(0, None)
            gather(1, X0)
            gather(2, X1)
            gather(3, use_x(2))
            with pool.Fori(2, NE) as e:
                scatter(e - 2)
                gather(e + 2, use_x(e + 1))
            scatter(NE - 2)
            scatter(NE - 1)
            pool.wait_ge(S("items_ready"), 1)
            nx = pool.value_load(CNT[0:1, 0:1], min_val=0, max_val=MAXX)
            with pool.Fori(0, MAXX) as j:
                with pool.If(nx > j):
                    gather(j + NE + 2, None)
                    scatter(j + NE)

        def root(act, r, mean):
            act.activation(r, mean, ACT.Sqrt).then_inc(S("root"), 1)

        def hgrn_exps(act, h):
            b = h % 2
            if h >= 2:
                full(act, "o", h - 2)
            if h == 0:
                act.wait_ge(S("zeros_out"), 32)
            act.wait_ge(S("decays"), 3 * h + 3)
            act.activation(QE[:, b, :], DD[:, :], ACT.Exp).then_inc(S("exps"), 1)
            act.activation(KE[:, b, :], DD[:, :], ACT.Exp, scale=-1.0).then_inc(S("exps"), 1)
            act.activation(KD[:, b, :], DE[:, :], ACT.Exp).then_inc(S("exps"), 1)
            act.activation(QB[:, b, :], B[:, :], ACT.Exp).then_inc(S("exps"), 1)
            act.activation(dec[:, NCH * b:NCH * (b + 1)], B[:, CH - 1::CH], ACT.Exp).then_inc(S("exps"), 1)

        @block.scalar
        def _(act):
            act.wait_ge(S("warm"), 1)
            act.activation(warm[:, 1:2], warm[:, 0:1], ACT.Sqrt).then_inc(S("tables"), 1)
            for i in range(TT):
                act.wait_ge(S(f"x_in{i}"), 16)
                if i:
                    act.wait_ge(S("ss1"), i)
                act.activation(junk[:, :], X[:, i, :], ACT.Square, accum_out=ss1[:, i:i + 1]).then_inc(S("ss1"), 1)
            act.wait_ge(S("mean_eps"), 1)
            root(act, r1, ss1)
            for i in range(TT // 2):
                act.wait_ge(S("r1"), 1)
                act.activation(XN[:, i, :], X[:, i, :], ACT.Copy, scale=r1[:, i:i + 1]).then_inc(S("xn"), 1)

            def w_high(c):
                act.wait_ge(S(f"w_in{c % 2}"), 16 * (c // 2 + 1))
                if c >= 4:
                    used(act, c - 4)
                act.activation(WPH[:, c % 4, :, :], WPR[:, c % 2, :, :], ACT.Copy).then_inc(S("w_in_high"), 1)

            w_high(0)
            w_high(1)
            freed(act, "vec")
            for k in range(DK):
                full(act, "hT", k)
                act.activation(HX[:, k, :], bank("hT", k), ACT.Copy, scale=g1c[:, k:k + 1]).then_inc(S("h_high"), 1)
            w_high(2)
            w_high(3)
            act.wait_ge(S("lb_shifted"), 1)
            act.activation(lbe[:, :], lbe[:, :], ACT.Exp).then_inc(S("lb_exp"), 1)
            for h in range(HH):
                full(act, "f", h)
                act.activation(F[:, h, :], bank("f", h), ACT.Sigmoid).then_inc(free_sem("f", h), 1)
                w_high(4 + h)
            for h in range(HH):
                full(act, "q", h)
                act.activation(Q[:, h, :], bank("q", h), ACT.Copy).then_inc(free_sem("q", h), 1)
                w_high(8 + h)
            for h in range(HH):
                act.wait_ge(S("f_ready"), h + 1)
                act.activation(F[:, h, :], F[:, h, :], ACT.Ln).then_inc(S("log_f"), 1)
            hgrn_exps(act, 0)
            for j in range(4):
                full(act, "v", j)
                act.activation(V[:, j, :], bank("v", j), ACT.Copy).then_inc(free_sem("v", j), 1)
            for c in range(12, 16):
                w_high(c)

            def projected(h, j):
                g = BETWEEN[h]
                full(act, g, j)
                if g == "g":
                    act.activation(G[:, j, :], bank(g, j), ACT.Sigmoid).then_inc(S("g_sig"), 1)
                else:
                    buf = {"aq": AQ, "ak": AK, "av": AV}[g]
                    act.activation(buf[:, j, :], bank(g, j), ACT.Copy).then_inc(free_sem(g, j), 1)
                if h + 1 < HH:
                    w_high(16 + 4 * h + j)

            def end_rows(h):
                full(act, "kdT", h)
                act.activation(KDT[:, h % 2, :, :], bank("kdT", h).rearrange("p (t m) -> p t m", m=P), ACT.Copy
                               ).then_inc(free_sem("kdT", h), 1)

            for h in range(HH):
                end_rows(h)
                projected(h, 0)
                if h + 1 < HH:
                    hgrn_exps(act, h + 1)
                projected(h, 1)
                full(act, "o", h)
                if h:
                    full(act, "ss", h - 1)
                act.activation(SQ[:, :], bank("o", h), ACT.Square).then_inc(S("o_sq"), 1)
                projected(h, 2)
                freed(act, "ss", h)
                root(act, R[:, :], RM[:, :])
                projected(h, 3)
            for h in range(AH):
                for i in range(TT):
                    act.wait_ge(S("neg_max"), TT * h + i + 1)
                    s = E[:, h % 2, EOFF[i]:EOFF[i] + P * (i + 1)]
                    act.activation(s, s, ACT.Exp, bias=nmx[:, TT * (h % 2) + i:TT * (h % 2) + i + 1], scale=DH ** -0.5,
                                   accum_out=den[:, TT * (h % 2) + i:TT * (h % 2) + i + 1]).then_inc(S("probs"), 1)
                for c in range(3):
                    if c == 1:
                        continue
                    full(act, "pt", h, c)
                    if h >= 2:
                        full(act, "pv", h - 2)
                    lo, hi = (0, 512) if c == 0 else (1024, 1280)
                    act.activation(PTs[:, h % 2, lo:hi], bank("pt", h, c)[:, 0:hi - lo], ACT.Copy
                                   ).then_inc(free_sem("pt", h, c), 1)
            act.wait_ge(S("mean_eps"), 2)
            root(act, ra, ssa)
            for j in range(4):
                full(act, "oT", j)
                act.activation(HT[:, 4 + j, :], bank("oT", j), ACT.Copy, scale=agc[:, j:j + 1]
                               ).then_inc(free_sem("oT", j), 1)
            for i in range(TT + 1):
                if i < TT:
                    for n in range(2):
                        freed(act, "x2", i, n)
                    act.activation(H2[:, i, :], X[:, i, :], ACT.Square, accum_out=ss2[:, i:i + 1]).then_inc(S("ss2"), 1)
                    act.wait_ge(S("mean_eps"), 3 + i)
                    root(act, r2[:, i:i + 1], ss2[:, i:i + 1])
                if i:
                    full(act, "h2T", i - 1, 1)
                    if i >= 3:
                        full(act, "lg", i - 3)
                    act.activation(H2T[:, (i - 1) % 2, 4:8, :], bank("h2T", i - 1, 1).rearrange("p (k m) -> p k m", m=P),
                                   ACT.Copy).then_inc(free_sem("h2T", i - 1, 1), 1)
            act.wait_ge(S("lg_shifted"), 1)
            act.activation(LG[:, 1, :], LG[:, 1, :], ACT.Exp).then_inc(S("lg_exp"), 1)
            act.activation(warm[:, 2:3], warm[:, 0:1], ACT.Silu).then_inc(S("tables"), 1)

            def cast(q, n, m):
                act.wait_ge(raw_landed[q.slot(m, RAW)], (q.turn(m, RAW) + 1) * 16)
                if q.starts(m) >= SPL:
                    act.wait_ge(chunk_used, q.count(m, 1 - SPL))
                act.activation(wh[:, q.slot(m, SPL), :], raw[q.slot(m, RAW)][:, :], ACT.Copy).then_inc(wh_ready, 1)

            def x_high(e, use):
                act.wait_ge(t_full, use + 1)
                act.activation(xh[:, :, :].rearrange("p k m -> p (k m)"), Tflat, ACT.Copy).then_inc(xh_ready, 1)

            def a_high(q, use):
                act.wait_ge(t_full, use + 1)
                act.activation(ah[:, :, :].rearrange("p k m -> p (k m)"), Tflat, ACT.Copy, scale=1.0 / ALPHA
                               ).then_inc(ah_ready, 1)

            def silu(q, up_chunks_end):
                act.wait_ge(chunk_used, up_chunks_end)
                if not isinstance(q, int) or q:
                    act.wait_ge(a_ready, q)
                act.activation(LN[:, :], Uflat[:, :, 1], ACT.Copy, bias=1.0).then_inc(lin_ready, 1)
                act.activation(SG[:, :], Uflat[:, :, 0], ACT.Silu, scale=ALPHA).then_inc(u_free, 1)

            def gated(q, column, down_chunks_end):
                act.wait_ge(chunk_used, down_chunks_end)
                act.wait_ge(blocks_added, q + 1)
                act.activation(Y[:, :], Yflat, ACT.Copy, scale=slot_t[:, bass.ds(column, 1), 1:2].rearrange("p a b -> p (a b)")
                               ).then_inc(y_ready, 1)

            def step(e, q, up, down, y, first=0):
                for n in range(first, NC):
                    if (n < UPC and up) or (n >= UPC and down):
                        cast(q, n, n if up else n - UPC)
                    if n == 1 and y:
                        gated(e - 2, e - 2, q.count(0, 0))
                    if n == 3 and down:
                        a_high(e - 1, use_a(e - 1))
                    if n == 10 and up:
                        silu(e, q.count(UPC - 1, 1))
                        x_high(e + 1, use_x(e + 1) if down else X1)

            act.wait_ge(S("front_done"), 1)
            for n in range(SPL):
                cast(FIRST, n, n)
            x_high(0, X0)
            for n in range(SPL, UPC):
                cast(FIRST, n, n)
            cast(SECOND, 0, 0)
            cast(SECOND, 1, 1)
            act.wait_ge(chunk_used, FIRST.count(UPC - 1, 1))
            x_high(1, X1)
            silu(0, FIRST.count(UPC - 1, 1))
            step(1, SECOND, True, True, False, first=2)
            with act.Fori(2, NE) as e:
                step(e, main_chunks(e), True, True, True)
            gated(NE - 2, NE - 2, END.count(0))
            a_high(NE - 1, use_a(NE - 1))
            for n in range(UPC, NC):
                cast(END, n, n - UPC)
            gated(NE - 1, NE - 1, END.count(DNC))
            act.wait_ge(S("items_ready"), 1)
            nx = act.value_load(CNT[0:1, 0:1], min_val=0, max_val=MAXX)
            with act.Fori(0, MAXX) as j:
                with act.If(nx > j):
                    q = over_chunks(j)
                    x_high(j, j * 3 + (OVER + 1))
                    for n in range(UPC):
                        cast(q, n, n)
                    silu(j + NE, q.count(UPC - 1, 1))
                    a_high(j + NE, j * 3 + (OVER + 2))
                    for n in range(UPC, NC):
                        cast(q, n, n)
                    gated(j + NE, 0, q.count(NC))
            for i in range(TT):
                act.wait_ge(S(f"xf_in{i}"), 16)
                act.activation(YF[:, i, :], XF[:, i, :], ACT.Square, accum_out=ss1[:, i:i + 1]).then_inc(S("ssf"), 1)
                act.wait_ge(S("mean_eps"), 3 + TT + i)
                root(act, r1[:, i:i + 1], ss1[:, i:i + 1])

        @block.vector
        def _(dve):
            link_count = [0]

            def link(ins):
                link_count[0] += 1
                ins.then_inc(S("dve_link"), 1)
                dve.wait_ge(S("dve_link"), link_count[0])

            def mean_eps(dst, src, n):
                dve.tensor_scalar(dst, src, 1.0 / n, EPS, ALU.mult, ALU.add).then_inc(S("mean_eps"), 1)

            roots = [0]

            def refined(r, mean, tmp):
                roots[0] += 1
                dve.wait_ge(S("root"), roots[0])
                link(dve.reciprocal(r, r))
                link(dve.tensor_tensor(tmp, r, r, ALU.mult))
                link(dve.scalar_tensor_tensor(tmp, tmp, -0.5, mean, ALU.mult, ALU.mult))
                return dve.scalar_tensor_tensor(r, tmp, 1.5, r, ALU.add, ALU.mult)

            def spread(col, n):
                return col.unsqueeze(2).broadcast_to([P, col.shape[1], n])

            dve.wait_ge(S("ss1"), TT)
            mean_eps(ss1, ss1, D)
            refined(r1, ss1, rtmp[:, 0:TT]).then_inc(S("r1"), 1)
            dve.wait_ge(S("r1"), 1)
            for i in range(TT // 2, TT):
                dve.tensor_scalar(XN[:, i, :], X[:, i, :], r1[:, i:i + 1], None, ALU.mult).then_inc(S("xn_rest"), 1)
            full(dve, "vec")
            dve.tensor_copy(vec_T, bank("vec")[:, 0:24]).then_inc(free_sem("vec"), 1)
            freed(dve, "vec")

            def w_low(c):
                dve.wait_ge(S("w_in_high"), c + 1)
                dve.tensor_tensor(WPL[:, c % 4, :, :], WPR[:, c % 2, :, :], WPH[:, c % 4, :, :].bitcast(F32), ALU.subtract
                                  ).then_inc(S("w_in_low"), 1)

            w_low(0)
            w_low(1)
            for k in range(DK):
                dve.wait_ge(S("h_high"), k + 1)
                dve.scalar_tensor_tensor(HL[:, k, :], bank("hT", k), g1c[:, k:k + 1], HX[:, k, :].bitcast(F32),
                                         ALU.mult, ALU.subtract).then_inc(free_sem("hT", k), 1)
            w_low(2)
            w_low(3)
            link(dve.tensor_tensor(lbm, lbc[:, 0:4], lbc[:, 4:8], ALU.max))
            link(dve.tensor_tensor(lbe[:, 0:4], lbc[:, 0:4], lbm, ALU.subtract))
            dve.tensor_tensor(lbe[:, 4:8], lbc[:, 4:8], lbm, ALU.subtract).then_inc(S("lb_shifted"), 1)
            dve.wait_ge(S("lb_exp"), 1)
            link(dve.tensor_tensor(lbz, lbe[:, 0:4], lbe[:, 4:8], ALU.add))
            link(dve.reciprocal(lbz, lbz))
            link(dve.tensor_tensor(lb, lbe[:, 0:4], lbz, ALU.mult))
            link(dve.tensor_scalar(oml, lb, -1.0, 1.0, ALU.mult, ALU.add))
            for h in range(HH):
                freed(dve, "f", h)
                link(dve.tensor_scalar(F[:, h, :], F[:, h, :], oml[:, h:h + 1], lb[:, h:h + 1], ALU.mult, ALU.add))
                dve.tensor_scalar(K[:, h, :], F[:, h, :], -1.0, 1.0, ALU.mult, ALU.add).then_inc(S("f_ready"), 1)
                w_low(4 + h)
            for c in range(8, 12):
                w_low(c)

            def gate(h):
                dve.wait_ge(S("g_sig"), h + 1)
                dve.scalar_tensor_tensor(G[:, h, :], G[:, h, :], hgc[:, h:h + 1], bank("g", h), ALU.mult, ALU.mult
                                         ).then_inc(free_sem("g", h), 1)

            def chunked(ap):
                return ap.rearrange("p (c s) -> p c s", s=CH)

            def decays(h):
                if h == 0:
                    dve.wait_ge(S("log_f"), HH)
                else:
                    dve.wait_ge(S("exps"), 5 * h)
                link(dve.tensor_tensor_scan(B[:, :], cst("chunk_go"), F[:, h, :], 0.0, ALU.mult, ALU.add))
                bc = chunked(B[:, :])
                mid = bc[:, :, CH // 2 - 1:CH // 2].broadcast_to([P, NCH, CH])
                end = bc[:, :, CH - 1:CH].broadcast_to([P, NCH, CH])
                dve.tensor_tensor(chunked(DE[:, :]), end, bc, ALU.subtract).then_inc(S("decays"), 1)
                dve.tensor_tensor(chunked(DD[:, :]), bc, mid, ALU.subtract).then_inc(S("decays"), 1)
                dve.wait_ge(S("decays"), 3 * h + 2)
                dve.tensor_scalar(DD[:, :], DD[:, :], 80.0, -80.0, ALU.min, ALU.max).then_inc(S("decays"), 1)

            def scaled(h):
                b = h % 2
                dve.wait_ge(S("exps"), 5 * h + 5)
                if h == 0:
                    freed(dve, "q", 3)
                for buf, by in ((QE, Q), (KE, K), (KD, K), (QB, Q)):
                    dve.tensor_tensor(buf[:, b, :], buf[:, b, :], by[:, h, :], ALU.mult).then_inc(S("qk_scaled"), 1)

            decays(0)
            scaled(0)
            for c in range(12, 16):
                w_low(c)
            for h in range(HH):
                b = h % 2
                full(dve, "sc", h)
                dve.scalar_tensor_tensor(A[:, b, :, :], bank("sc", h).rearrange("p (t m) -> p t m", m=P), 3e38,
                                         cst("chunk_causal").unsqueeze(1).broadcast_to([P, TT, P]), ALU.min, ALU.mult
                                         ).then_inc(free_sem("sc", h), 1)
                if h + 1 < HH:
                    decays(h + 1)
                if h == 0:
                    gate(0)
                for j in range(4):
                    full(dve, "kv", h, j)
                if h:
                    full(dve, "o", h - 1)
                for c in range(1, NCH):
                    kv = bank("kv", h, (c - 1) % 4)[:, (c - 1) // 4 * P:(c - 1) // 4 * P + P]
                    if c == 1:
                        ins = dve.tensor_copy(ST[:, 1, :], kv)
                    else:
                        ins = dve.scalar_tensor_tensor(ST[:, c, :], ST[:, c - 1, :],
                                                       dec[:, NCH * b + c - 1:NCH * b + c], kv, ALU.mult, ALU.add)
                    if c >= NCH - 4:
                        last = {NCH - 4: 3, NCH - 3: 0, NCH - 2: 1, NCH - 1: 2}[c]
                        ins.then_inc(free_sem("kv", h, last), 1)
                        if c < NCH - 1:
                            freed(dve, "kv", h, last)
                    else:
                        link(ins)
                if h + 1 < HH:
                    w_low(16 + 4 * h)
                    scaled(h + 1)
                    w_low(17 + 4 * h)
                if h == 0:
                    gate(1)
                    gate(2)
                if h + 1 < HH:
                    w_low(18 + 4 * h)
                full(dve, "ss", h)
                if h == 0:
                    freed(dve, "g", 0)
                dve.tensor_scalar(RM[:, :], bank("ss", h), 1.0 / P, EPS, ALU.mult, ALU.add).then_inc(free_sem("ss", h), 1)
                freed(dve, "ss", h)
                link(refined(R[:, :], RM[:, :], RN[:, :]))
                link(dve.tensor_tensor(R[:, :], R[:, :], G[:, h, :], ALU.mult))
                dve.tensor_tensor(G[:, h, :], bank("o", h), R[:, :], ALU.mult).then_inc(free_sem("o", h), 1)
                if h == 0:
                    gate(3)
                else:
                    freed(dve, "g", h)
                if h + 1 < HH:
                    w_low(19 + 4 * h)

            def masked_max(h):
                for i in range(TT):
                    full(dve, "qk", h, i)
                    n = TT * (h % 2) + i
                    if h >= 2:
                        full(dve, "pt", h - 2, 2)
                    dve.tensor_tensor_reduce(E[:, h % 2, EOFF[i]:EOFF[i] + P * (i + 1)], bank("qk", h, i)[:, 0:P * (i + 1)],
                                             cst("pairs")[:, (TT - 1 - i) * P:], 1.0, -3e38, ALU.add, ALU.max,
                                             mx[:, n:n + 1]).then_inc(free_sem("qk", h, i), 1)
                    freed(dve, "qk", h, i)
                    dve.tensor_scalar(nmx[:, n:n + 1], mx[:, n:n + 1], -DH ** -0.5, None, ALU.mult
                                      ).then_inc(S("neg_max"), 1)

            def add_share(*name):
                i, n = (name[1] // 2, name[1] % 2) if name[0] == "xa" else name[1:]
                full(dve, *name)
                dve.tensor_tensor(X[:, i, n * 512:(n + 1) * 512], X[:, i, n * 512:(n + 1) * 512], bank(*name), ALU.add
                                  ).then_inc(free_sem(*name), 1)

            masked_max(0)
            for h in range(AH):
                if h + 1 < AH:
                    masked_max(h + 1)
                if 1 <= h < AH - 1:
                    if h == 1:
                        dve.wait_ge(S("x_again"), 16)
                    add_share("xa", h - 1)
                full(dve, "pt", h, 1)
                if h >= 2:
                    full(dve, "pv", h - 2)
                dve.tensor_copy(PTs[:, h % 2, 512:1024], bank("pt", h, 1)).then_inc(free_sem("pt", h, 1), 1)
                dve.wait_ge(S("probs"), TT * (h + 1))
                b = TT * (h % 2)
                link(dve.reciprocal(rden[:, b:b + TT], den[:, b:b + TT]))
                full(dve, "pv", h)
                dve.tensor_tensor(OA[:, :, h * DH:(h + 1) * DH], bank("pv", h)[:, 0:TT * DH].rearrange("p (t d) -> p t d", d=DH),
                                  spread(rden[:, b:b + TT], DH), ALU.mult).then_inc(free_sem("pv", h), 1)
                freed(dve, "pv", h)
                oh = OA[:, :, h * DH:(h + 1) * DH]
                link(dve.tensor_tensor(osq[:, :, :], oh, oh, ALU.mult))
                link(dve.tensor_reduce(ssa[:, TT * h:TT * (h + 1)], osq[:, :, :], AX.X, ALU.add))
            mean_eps(ssa, ssa, DH)
            link(refined(ra, ssa, rtmp[:, 0:AH * TT]))
            for h in range(AH):
                oh = OA[:, :, h * DH:(h + 1) * DH]
                dve.tensor_tensor(oh, oh, spread(ra[:, TT * h:TT * (h + 1)], DH), ALU.mult).then_inc(S("attn_read"), 1)

            dve.wait_ge(S("bias_in"), 64)
            dve.tensor_copy(bias_hl[:, :], bias_raw[:, :]).then_inc(S("bias_high"), 1)
            dve.wait_ge(S("bias_high"), 1)
            link(dve.tensor_tensor(bias_hl[NE:2 * NE, :], bias_raw[NE:2 * NE, :], bias_hl[NE:2 * NE, :].bitcast(F32), ALU.subtract))

            for n in LATE_SHARES:
                add_share("xa", n)
            dve.wait_ge(S("g2_in"), 16)
            for i in range(TT + 2):
                if i < TT:
                    for n in range(2):
                        freed(dve, "xa", 2 * i + n)
                        add_share("x2", i, n)
                    dve.wait_ge(S("ss2"), i + 1)
                    r, mean = r2[:, i:i + 1], ss2[:, i:i + 1]
                    mean_eps(mean, mean, D)
                    link(refined(r, mean, rtmp[:, 0:1]))
                    dve.scalar_tensor_tensor(H2[:, i, :], X[:, i, :], r, G2[:, :], ALU.mult, ALU.mult
                                             ).then_inc(S("h2_rows"), 1)
                if 1 <= i <= TT:
                    full(dve, "h2T", i - 1, 0)
                    if i >= 3:
                        full(dve, "lg", i - 3)
                    dve.tensor_copy(H2T[:, (i - 1) % 2, 0:4, :], bank("h2T", i - 1, 0).rearrange("p (k m) -> p k m", m=P)
                                    ).then_inc(free_sem("h2T", i - 1, 0), 1)
                if i >= 2:
                    full(dve, "lg", i - 2)
                    tile = slice((i - 2) * NE, (i - 1) * NE)
                    dve.tensor_copy(LG[:, 0, tile], bank("lg", i - 2)[:, 0:NE]).then_inc(free_sem("lg", i - 2), 1)
                    freed(dve, "lg", i - 2)
                    link(dve.max(top8[:, i - 2, :], LG[:, 0, tile]))

            def lgv(n):
                return LG[:, n, :].rearrange("p (t e) -> p t e", e=NE)

            largest = top8[:, :, 0:1].broadcast_to([P, TT, NE])
            fourth = top8[:, :, TOPK - 1:TOPK].broadcast_to([P, TT, NE])
            dve.tensor_tensor(lgv(1), lgv(0), largest, ALU.subtract).then_inc(S("lg_shifted"), 1)
            link(dve.tensor_tensor(lgv(2), lgv(0), fourth, ALU.is_gt))
            link(dve.tensor_tensor(lgv(3), lgv(0), fourth, ALU.is_equal))
            link(dve.tensor_tensor_scan(LG[:, 4, :], cst("tile_go"), LG[:, 3, :], 0.0, ALU.mult, ALU.add))
            link(dve.tensor_reduce(rt[:, 0, :], lgv(2), AX.X, ALU.add))
            link(dve.tensor_scalar(rt[:, 0, :], rt[:, 0, :], -1.0, float(TOPK), ALU.mult, ALU.add))
            link(dve.tensor_tensor(lgv(4), lgv(4), spread(rt[:, 0, :], NE), ALU.is_le))
            link(dve.tensor_tensor(LG[:, 3, :], LG[:, 3, :], LG[:, 4, :], ALU.mult))
            link(dve.tensor_tensor(LG[:, 2, :], LG[:, 2, :], LG[:, 3, :], ALU.add))
            dve.memset(LG[:, 3, 0:NE], 0.0).then_inc(S("selected"), 1)
            dve.wait_ge(S("selected"), 1)
            dve.wait_ge(S("lg_exp"), 1)
            link(dve.tensor_tensor(LG[:, 1, :], LG[:, 1, :], LG[:, 2, :], ALU.mult))
            link(dve.tensor_reduce(rt[:, 1, :], lgv(1), AX.X, ALU.add))
            link(dve.reciprocal(rt[:, 1, :], rt[:, 1, :]))
            link(dve.memset(pos_t[:, :, :], -1.0))
            link(dve.memset(vals_t[:, :, :, :], 0.0))
            link(dve.tensor_tensor(vals_t[:, :, 0:NE, 1:2].rearrange("p t e o -> p t (e o)"), lgv(1), spread(rt[:, 1, :], NE), ALU.mult))
            full(dve, "pos")
            link(dve.scalar_tensor_tensor(LG[:, 5, :], bank("pos")[:, 0:TT * NE], 1.0, LG[:, 2, :], ALU.add, ALU.mult))
            link(dve.tensor_copy(counts, bank("pos")[:, TT * NE:TT * NE + NE]))
            link(dve.tensor_scalar(pos_t[:, :, 0:NE], lgv(5), -1.0, None, ALU.add))
            link(dve.tensor_scalar(lgv(7), pos_t[:, :, 0:NE], float(P), None, ALU.is_ge))
            link(dve.scalar_tensor_tensor(lgv(7), pos_t[:, :, 0:NE], float(2 * P), lgv(7), ALU.is_ge, ALU.add))
            link(dve.scalar_tensor_tensor(lgv(7), pos_t[:, :, 0:NE], float(3 * P), lgv(7), ALU.is_ge, ALU.add))
            link(dve.scalar_tensor_tensor(lgv(7), lgv(7), -float(P), pos_t[:, :, 0:NE], ALU.mult, ALU.add))
            link(dve.tensor_tensor(vals_t[:, :, 0:NE, 0:1].rearrange("p t e o -> p t (e o)"), spread(cst("tok"), NE), lgv(7), ALU.subtract))
            dve.wait_ge(S("rows_out"), 32 * TT)
            full(dve, "pos")
            dve.tensor_copy(CNT[:, 2:3], bank("pos")[:, 0:1]).then_inc(S("front_done"), 1)

            def overflow_items():
                cnt = counts
                ext, last = small[:, 96:128], small[:, 128:160]
                link(dve.tensor_scalar(ext, cnt, float(P), None, ALU.is_gt))
                link(dve.scalar_tensor_tensor(ext, cnt, float(2 * P), ext, ALU.is_gt, ALU.add))
                link(dve.scalar_tensor_tensor(ext, cnt, float(3 * P), ext, ALU.is_gt, ALU.add))
                link(dve.tensor_tensor_scan(last, ones[:, 0:NE], ext, 0.0, ALU.mult, ALU.add))
                before, ends = items[:, 0, :, :], items[:, 1, :, :]
                lasts = last.unsqueeze(1).broadcast_to([P, MAXX, NE])
                link(dve.tensor_tensor(before, lasts, spread(cst("item"), NE), ALU.is_le))
                link(dve.tensor_reduce(itf[:, :], before, AX.X, ALU.add))
                link(dve.tensor_tensor(ends, before, lasts, ALU.mult))
                link(dve.tensor_reduce(block_off[:, :], ends, AX.X, ALU.max))
                link(dve.scalar_tensor_tensor(block_off[:, :], block_off[:, :], -1.0, cst("item"), ALU.add, ALU.subtract))
                link(dve.tensor_scalar(block_off[:, :], block_off[:, :], float(P), None, ALU.mult))
                link(dve.tensor_copy(CNT[:, MAXX:2 * MAXX], itf[:, :]))
                link(dve.tensor_copy(CNT[:, 0:1], last[:, NE - 1:NE]))
                dve.tensor_copy(CNT[:, 1:2], last[:, NE - 1:NE]).then_inc(S("items_ready"), 1)

            def make_sel(col, offset=None):
                for i in range(TT):
                    p_col = pos_t[:, i, bass.ds(col, 1)]
                    if offset is None:
                        ins = dve.tensor_scalar(SEL[:, i, :], cst("iota"), p_col, None, ALU.is_equal)
                    else:
                        ins = dve.tensor_scalar(SEL[:, i, :], cst("iota"), p_col, offset, ALU.subtract, ALU.is_equal)
                    ins.then_inc(sel_ready, 1)

            def slot_rows(g, use, col, before=True):
                dve.wait_ge(t_full, use + 1)
                if before:
                    dve.wait_ge(gathered, g * 16)
                dve.tensor_tensor(IDXG[:, 0:1], Tflat[:, 0:1], cst("dump_row")[:, 0:1], ALU.add).then_inc(idxg_ready, 1)
                dve.tensor_tensor(slot_t[:, bass.ds(col, 1), :].rearrange("p a b -> p (a b)"), Tflat[:, 0:2], cst("dump_row"), ALU.add
                                  ).then_inc(t_free, 1)

            def split(q, m):
                dve.wait_ge(wh_ready, q.count(m, 1))
                dve.tensor_tensor(wl[:, q.slot(m, SPL), :], raw[q.slot(m, RAW)][:, :],
                                  wh[:, q.slot(m, SPL), :].bitcast(F32), ALU.subtract).then_inc(wl_ready, 1)

            def x_low(g, use):
                dve.wait_ge(xh_ready, g + 1)
                dve.tensor_tensor(xl[:, :, :].rearrange("p k m -> p (k m)"), Tflat,
                                  xh[:, :, :].rearrange("p k m -> p (k m)").bitcast(F32), ALU.subtract).then_inc(t_free, 1)

            def a_low(q):
                dve.wait_ge(ah_ready, q + 1)
                dve.scalar_tensor_tensor(al[:, :, :].rearrange("p k m -> p (k m)"), Tflat, 1.0 / ALPHA,
                                         ah[:, :, :].rearrange("p k m -> p (k m)").bitcast(F32), ALU.mult, ALU.subtract
                                         ).then_inc(t_free, 1)

            def bias_row(buf, col, done):
                dve.tensor_scalar(buf[:, :], ones[0:64, :], cst("expert_row")[0:64, bass.ds(col, 1)], None, ALU.mult
                                  ).then_inc(done, 1)

            def scatter_rows(q, col):
                dve.wait_ge(blocks_added, q + 1)
                dve.tensor_copy(IDXS[:, 0:1], slot_t[:, bass.ds(col, 1), 0:1].rearrange("p a b -> p (a b)")).then_inc(idxs_ready, 1)

            def swiglu(q):
                dve.wait_ge(lin_ready, q + 1)
                dve.tensor_scalar(LN[:, :], LN[:, :], LIMIT + 1.0, 1.0 - LIMIT, ALU.min, ALU.max).then_inc(lin_clipped, 1)
                dve.wait_ge(u_free, q + 1)
                dve.wait_ge(lin_clipped, q + 1)
                dve.scalar_tensor_tensor(GL[:, :], SG[:, :], SILU_LIMIT, LN[:, :], ALU.min, ALU.mult).then_inc(a_ready, 1)

            def step(e, q, up, down, y, first=0):
                for n in range(first, NC):
                    if (n < UPC and up) or (n >= UPC and down):
                        split(q, n if up else n - UPC)
                    if n == 0 and y:
                        scatter_rows(e - 2, e - 2)
                    if n == 2 and up:
                        make_sel(e + 2)
                        if not y:
                            overflow_items()
                    if n == 3 and down:
                        a_low(e - 1)
                        bias_row(BSD, e - 1, bsd_ready)
                    if n == 6 and up:
                        slot_rows(e + 2, use_sel(e + 2) if down else SEL2, e + 2)
                    if n == 9 and up:
                        bias_row(BSU, e + 1, bsu_ready)
                    if n == 10 and up:
                        x_low(e + 1, None)
                    if n == 11 and up:
                        swiglu(e)

            make_sel(0)
            slot_rows(0, SEL0, 0, before=False)
            bias_row(BSU, 0, bsu_ready)
            make_sel(1)
            split(FIRST, 0)
            slot_rows(1, SEL1, 1)
            split(FIRST, 1)
            x_low(0, X0)
            for n in range(2, UPC):
                split(FIRST, n)
                if n == 2:
                    make_sel(2)
                if n == 6:
                    slot_rows(2, SEL2, 2)
            split(SECOND, 0)
            split(SECOND, 1)
            bias_row(BSU, 1, bsu_ready)
            x_low(1, X1)
            swiglu(0)
            step(1, SECOND, True, True, False, first=2)
            with dve.Fori(2, NE) as e:
                step(e, main_chunks(e), True, True, True)
            scatter_rows(NE - 2, NE - 2)
            a_low(NE - 1)
            bias_row(BSD, NE - 1, bsd_ready)
            for n in range(UPC, NC):
                split(END, n - UPC)
            scatter_rows(NE - 1, NE - 1)
            nx = dve.value_load(CNT[0:1, 0:1], min_val=0, max_val=MAXX)
            with dve.Fori(0, MAXX) as j:
                with dve.If(nx > j):
                    ex = dve.value_load(CNT[0:1, bass.ds(j + MAXX, 1)], min_val=0, max_val=NE - 1)
                    q = over_chunks(j)
                    dve.wait_ge(blocks_added, j + NE + 1)
                    make_sel(ex, block_off[:, bass.ds(j, 1)])
                    slot_rows(j + NE + 2, j * 3 + OVER, 0)
                    bias_row(BSU, ex, bsu_ready)
                    bias_row(BSD, ex, bsd_ready)
                    x_low(j + NE + 1, None)
                    for n in range(UPC):
                        split(q, n)
                    swiglu(j + NE)
                    a_low(j + NE)
                    for n in range(UPC, NC):
                        split(q, n)
                    scatter_rows(j + NE, 0)
            dve.wait_ge(S("gf_in"), 16)
            for i in range(TT):
                dve.wait_ge(S("ssf"), i + 1)
                mean_eps(ss1[:, i:i + 1], ss1[:, i:i + 1], D)
                link(refined(r1[:, i:i + 1], ss1[:, i:i + 1], rtmp[:, 0:1]))
                dve.scalar_tensor_tensor(YF[:, i, :], XF[:, i, :], r1[:, i:i + 1], GF[:, :], ALU.mult, ALU.mult
                                         ).then_inc(S("out_ready"), 1)

        @block.tensor
        def _(pe):
            def begin(*name):
                n = number[name]
                if n >= 8:
                    pe.wait_ge(bank_free[n % 8], n // 8)
                return bank(*name)

            def blocks_of(o):
                return o.rearrange("p (t m) -> p t m", m=P)

            def blocks(*name):
                return blocks_of(begin(*name))

            pe.wait_ge(S("c_in"), 16)
            pe.wait_ge(S("vec_in"), 64)
            pe.transpose(begin("vec")[:, 0:24], vec_rows[:, :], ident[0:24, 0:24]).then_inc(full_sem("vec"), 1)
            for k in range(DK):
                o = blocks("hT", k)
                for i in range(TT):
                    if i < TT // 2:
                        pe.wait_ge(S("xn"), i + 1)
                    else:
                        pe.wait_ge(S("xn_rest"), i + 1 - TT // 2)
                    ins = pe.transpose(o[:, i, :], XN[:, i, k * P:(k + 1) * P], ident)
                ins.then_inc(full_sem("hT", k), 1)

            def project(g, j):
                c = 4 * GORDER.index(g) + j
                rows = g in ("v", "av")
                pe.wait_ge(S("w_in_low"), c - j + 4 if rows else c + 1)
                o = begin(g, j)
                for k in range(DK):
                    if c == 0:
                        freed(pe, "hT", k)
                    for h_part, w_part in ((HL, WPH), (HX, WPH), (HX, WPL)):
                        if rows:
                            ins = pe.matmul(blocks_of(o), h_part[:, k, j * P:(j + 1) * P], w_part[:, :, k, :],
                                            start=(k == 0 and h_part is HL), stop=(k == DK - 1 and w_part is WPL))
                        else:
                            ins = pe.matmul(o, w_part[:, j, k, :], h_part[:, k, :],
                                            start=(k == 0 and h_part is HL), stop=(k == DK - 1 and w_part is WPL))
                ins.then_inc(full_sem(g, j), 1)

            for g in ("f", "q", "v"):
                for j in range(4):
                    project(g, j)

            def hgrn_inputs(h):
                b = h % 2
                pe.wait_ge(S("qk_scaled"), 4 * (h + 1))
                o = blocks("kdT", h)
                for i in range(TT):
                    ins = pe.transpose(o[:, i, :], KD[:, b, i * P:(i + 1) * P], ident)
                ins.then_inc(full_sem("kdT", h), 1)
                o = blocks("sc", h)
                for i in range(TT):
                    s = slice(i * P, (i + 1) * P)
                    ins = pe.matmul(o[:, i, :], KE[:, b, s], QE[:, b, s], start=True, stop=True)
                ins.then_inc(full_sem("sc", h), 1)
                if BETWEEN[h] != "av":
                    project(BETWEEN[h], 0)
                freed(pe, "kdT", h)
                if h == 0:
                    for j in range(4):
                        freed(pe, "v", j)
                for j in range(4):
                    o = blocks("kv", h, j)
                    r = slice(j * CH, (j + 1) * CH)
                    for i in range(TT):
                        ins = pe.matmul(o[:, i, :], KDT[r, b, i, :], V[r, i, h * P:(h + 1) * P], start=True, stop=True)
                    ins.then_inc(full_sem("kv", h, j), 1)
                if BETWEEN[h] == "av":
                    project(BETWEEN[h], 0)
                project(BETWEEN[h], 1)

            def hgrn_outputs(h):
                b = h % 2
                o = begin("o", h)
                freed(pe, "sc", h)
                freed(pe, "kv", h, 2)
                for i in range(TT):
                    s = slice(i * P, (i + 1) * P)
                    ins = pe.matmul(o[:, s], V[:, i, h * P:(h + 1) * P], A[:, b, i, :], start=(i == 0), stop=False,
                                    skip_group_check=True)
                for c in range(1, NCH):
                    s = slice(c * CH, (c + 1) * CH)
                    ins = pe.matmul(o[:, s], ST[:, c, :], QB[:, b, s], start=False, stop=(c == NCH - 1),
                                    skip_group_check=True)
                ins.then_inc(full_sem("o", h), 1)
                project(BETWEEN[h], 2)
                o = begin("ss", h)
                pe.wait_ge(S("o_sq"), h + 1)
                pe.matmul(o, ones, SQ[:, :], start=True, stop=True).then_inc(full_sem("ss", h), 1)
                project(BETWEEN[h], 3)

            for h in range(HH):
                hgrn_inputs(h)
                hgrn_outputs(h)

            def attn_scores(h):
                if h == 0:
                    for j in range(4):
                        freed(pe, "aq", j)
                        freed(pe, "ak", j)
                        freed(pe, "av", j)
                r = slice(DH * (h % 2), DH * (h % 2) + DH)
                for i in range(TT):
                    ins = pe.matmul(begin("qk", h, i)[:, 0:(i + 1) * P], AQ[r, h // 2, i * P:(i + 1) * P],
                                    AK[r, h // 2, 0:(i + 1) * P], start=True, stop=True)
                    ins.then_inc(full_sem("qk", h, i), 1)

            def hgrn_share(n):
                if n == 0:
                    for h in range(HH):
                        freed(pe, "o", h)
                    pe.wait_ge(S("w_out0"), 16)
                    pe.wait_ge(S("w_out1"), 16)
                i = n // 2
                o = begin("xa", n)
                for k in range(HH):
                    ins = pe.matmul(o, G[:, k, i * P:(i + 1) * P], Wb[:, n % 2, k, :], start=(k == 0), stop=(k == HH - 1))
                ins.then_inc(full_sem("xa", n), 1)

            attn_scores(0)
            for h in range(AH):
                if h + 1 < AH:
                    attn_scores(h + 1)
                if 1 <= h < AH - 1:
                    hgrn_share(h - 1)
                pe.wait_ge(S("probs"), TT * (h + 1))
                for c, tiles in enumerate(((0,), (1, 3), (2,))):
                    o = begin("pt", h, c)
                    for kt in tiles:
                        for i in range(kt, TT):
                            a = KB[kt] - KB[tiles[0]] + (i - kt) * P
                            e0 = EOFF[i] + kt * P
                            ins = pe.transpose(o[:, a:a + P], E[:, h % 2, e0:e0 + P], ident)
                    ins.then_inc(full_sem("pt", h, c), 1)
                o = begin("pv", h)
                for c in range(3):
                    freed(pe, "pt", h, c)
                for i in range(TT):
                    for kt in range(i + 1):
                        a = KB[kt] + (i - kt) * P
                        ins = pe.matmul(o[:, i * DH:(i + 1) * DH], PTs[:, h % 2, a:a + P], AV[:, kt, h * DH:(h + 1) * DH],
                                        start=(kt == 0), stop=(kt == i))
                ins.then_inc(full_sem("pv", h), 1)
            for n in LATE_SHARES:
                hgrn_share(n)
            pe.wait_ge(S("attn_read"), AH)
            for j in range(4):
                o = blocks("oT", j)
                for i in range(TT):
                    ins = pe.transpose(o[:, i, :], OA[:, i, j * P:(j + 1) * P], ident)
                ins.then_inc(full_sem("oT", j), 1)
            for j in range(4):
                freed(pe, "oT", j)
            pe.wait_ge(S("rw_in"), 16)
            pe.wait_ge(S("rb_in"), 16)
            for i in range(TT + 2):
                for n in range(2):
                    if i < TT:
                        o = begin("x2", i, n)
                        for k in range(HH, DK):
                            ins = pe.matmul(o, HT[:, k, i * P:(i + 1) * P], Wb[:, n, k, :], start=(k == HH), stop=(k == DK - 1))
                        ins.then_inc(full_sem("x2", i, n), 1)
                for n in range(2):
                    if 1 <= i <= TT:
                        pe.wait_ge(S("h2_rows"), i)
                        o = blocks("h2T", i - 1, n)
                        for k in range(4):
                            c = (4 * n + k) * P
                            ins = pe.transpose(o[:, k, :], H2[:, i - 1, c:c + P], ident)
                        ins.then_inc(full_sem("h2T", i - 1, n), 1)
                if i >= 2:
                    o = begin("lg", i - 2)[:, 0:NE]
                    for n in range(2):
                        freed(pe, "h2T", i - 2, n)
                    for k in range(DK):
                        pe.matmul(o, H2T[:, (i - 2) % 2, k, :], rw_sb[:, k, :], start=(k == 0), stop=False)
                    ins = pe.matmul(o, ones[0:1, :], rb_row[0:1, :], start=False, stop=True)
                    ins.then_inc(full_sem("lg", i - 2), 1)
            pe.wait_ge(S("selected"), 1)
            o = begin("pos")
            sel = LG[:, 2, :].rearrange("p (t e) -> p t e", e=NE)
            counts_of = o[:, 0:(TT + 1) * NE].rearrange("p (t e) -> p t e", e=NE)
            pe.matmul(o[:, 0:(TT + 1) * NE], cst("before"), LG[:, 2:4, :].rearrange("p n e -> p (n e)")[:, 0:(TT + 1) * NE],
                      start=True, stop=False, skip_group_check=True)
            for t in range(TT):
                ins = pe.matmul(counts_of[:, t + 1:, :], ones, sel[:, t:t + 1, :].broadcast_to([P, TT - t, NE]), start=False,
                                stop=(t == TT - 1), skip_group_check=True)
            ins.then_inc(full_sem("pos"), 1)

            def select(g, use, col):
                pe.wait_ge(sel_ready, g * TT + TT)
                pe.wait_ge(t_free, use)
                for i in range(TT):
                    ins = pe.matmul(Tflat[:, 0:2], SEL[:, i, :], vals_t[:, i, bass.ds(col, 1), :].rearrange("p a b -> p (a b)"),
                                    start=(i == 0), stop=(i == TT - 1))
                ins.then_inc(t_full, 1)

            def x_transposed(g, use):
                pe.wait_ge(gathered, (g + 1) * 16)
                pe.wait_ge(t_free, use)
                for k in range(DK):
                    ins = pe.transpose(T[:, k, :], XG[:, k * P:(k + 1) * P], ident)
                ins.then_inc(t_full, 1)

            def a_transposed(q, use):
                pe.wait_ge(a_ready, q + 1)
                pe.wait_ge(t_free, use)
                for k in range(DK):
                    ins = pe.transpose(T[:, k, :], GL[:, k * P:(k + 1) * P], ident)
                ins.then_inc(t_full, 1)

            def products(o, high, low, w_high, w_low, width, last):
                for x_part, w_part in ((low, w_high), (high, w_high), (high, w_low)):
                    for j in range(width // 512):
                        ins = pe.matmul(o[:, j, :], x_part, w_part[:, j * 512:(j + 1) * 512], start=False,
                                        stop=(last and x_part is high and w_part is w_low))
                return ins

            def up(ordinal, q, bias_ordinal, x_use):
                pe.wait_ge(bsu_ready, bias_ordinal + 1)
                pe.wait_ge(t_free, x_use + 1)
                if not isinstance(ordinal, int) or ordinal:
                    pe.wait_ge(u_free, ordinal)
                for j in range(4):
                    pe.matmul(U[:, j, :], BSU[:, :], bias_hl[:, j * 512:(j + 1) * 512], start=True, stop=False)

            def up_chunk(q, m, c, last=False):
                pe.wait_ge(wl_ready, q.count(m, 1))
                s = q.slot(m, SPL)
                return products(U, xh[:, c, :], xl[:, c, :], wh[:, s, :], wl[:, s, :], NF, last)

            def down(ordinal, a_use):
                pe.wait_ge(bsd_ready, ordinal + 1)
                pe.wait_ge(t_free, a_use + 1)
                if not isinstance(ordinal, int) or ordinal:
                    pe.wait_ge(y_ready, ordinal)
                for j in range(2):
                    pe.matmul(Yp[:, j, :], BSD[:, :], bias_hl[:, NF + j * 512:NF + (j + 1) * 512], start=True, stop=False)

            def down_chunk(q, m, c, last=False):
                pe.wait_ge(wl_ready, q.count(m, 1))
                s = q.slot(m, SPL)
                for t in range(2):
                    k = 2 * c + t
                    ins = products(Yp, ah[:, k, :], al[:, k, :], wh[:, s, t * D:(t + 1) * D], wl[:, s, t * D:(t + 1) * D],
                                   D, last and t == 1)
                return ins

            def step(e, q, has_up, has_down):
                if has_up:
                    up(e, q, e, use_x(e) if not isinstance(e, int) or e > 1 else (X0, X1)[e])
                    for c in range(UPC):
                        ins = up_chunk(q, c, c, c == UPC - 1)
                        ins.then_inc(chunk_used, 1)
                        if c == 1 and has_down:
                            a_transposed(e - 1, use_a(e - 1))
                        if c == 4:
                            select(e + 2, use_sel(e + 2) if has_down else SEL2, e + 2)
                        if c == 6 and not has_down:
                            x_transposed(e + 1, X1)
                else:
                    a_transposed(e - 1, use_a(e - 1))
                if has_down:
                    down(e - 1, use_a(e - 1))
                for c in range(DNC):
                    if has_down:
                        ins = down_chunk(q, (UPC if has_up else 0) + c, c, c == DNC - 1)
                        ins.then_inc(chunk_used, 1)
                    if c == 0 and has_up and has_down:
                        x_transposed(e + 1, use_x(e + 1))

            select(0, SEL0, 0)
            select(1, SEL1, 1)
            x_transposed(0, X0)
            step(0, FIRST, True, False)
            step(1, SECOND, True, True)
            with pe.Fori(2, NE) as e:
                step(e, main_chunks(e), True, True)
            step(NE, END, False, True)
            pe.wait_ge(S("items_ready"), 1)
            nx = pe.value_load(CNT[0:1, 0:1], min_val=0, max_val=MAXX)
            with pe.Fori(0, MAXX) as j:
                with pe.If(nx > j):
                    ex = pe.value_load(CNT[0:1, bass.ds(j + MAXX, 1)], min_val=0, max_val=NE - 1)
                    q = over_chunks(j)
                    select(j + NE + 2, j * 3 + OVER, ex)
                    x_transposed(j + NE + 2, j * 3 + (OVER + 1))
                    up(j + NE, q, j + NE + 1, j * 3 + (OVER + 1))
                    for c in range(UPC):
                        up_chunk(q, c, c, c == UPC - 1).then_inc(chunk_used, 1)
                    a_transposed(j + NE, j * 3 + (OVER + 2))
                    down(j + NE, j * 3 + (OVER + 2))
                    for c in range(DNC):
                        down_chunk(q, UPC + c, c, c == DNC - 1).then_inc(chunk_used, 1)


def kernel(**inputs):
    import concourse.bacc as bacc
    from concourse.bass_utils import run_bass_kernel_spmd

    nc = bacc.Bacc("TRN2", target_bir_lowering=False, num_devices=1)
    names = ["x", "norm1_g", "w_in", "hgrn_lb_logits", "hgrn_norm_g", "attn_norm_g", "w_out", "norm2_g", "router_w",
             "router_b", "w_up", "b_up", "w_down", "b_down", "final_norm_g"]
    consts, where = shape_constants()
    arrays = {name: np.ascontiguousarray(inputs[name]) for name in names}
    arrays["shape_constants"] = consts
    args = [nc.dram_tensor(name, a.shape, mybir.dt.from_np(a.dtype), kind="ExternalInput").ap() for name, a in arrays.items()]
    out = nc.dram_tensor("out", (1, SEQ, D), F32, kind="ExternalOutput").ap()
    hybrid_moe_block(nc, *args, out, where)
    r = run_bass_kernel_spmd(nc, [arrays], core_ids=[0])
    return r.results[0]["out"]
```
